# Optimizing a Trainium2 kernel written in Bass

```python
import jax, jax.numpy as jnp
from jax import lax
import numpy as np
import math

D_MODEL = 1024
BATCH = 1
SEQ = 512
DEPTH = 1

MIX_WIDTH = D_MODEL
HEAD_DIM = 64
ATTN_WIDTH = MIX_WIDTH // 2
ATTN_HEADS = ATTN_WIDTH // HEAD_DIM
SGU_WIDTH = MIX_WIDTH - ATTN_WIDTH
SGU_GROUP_DIM = 64
SGU_GROUPS = SGU_WIDTH // SGU_GROUP_DIM
SGU_CHUNK = 128
DILATED_PATTERNS = ((128, 1), (512, 4), (2048, 16))
BLOCK_Q = 128
ROPE_THETA = 500000.0
ROT_DIM = HEAD_DIM // 4
ROT_HALF = ROT_DIM // 2
D_FF = ((8 * D_MODEL // 3 + 255) // 256) * 256
IN_PROJ_WIDTH = 3 * ATTN_WIDTH + 2 * SGU_WIDTH
RMS_EPS = 1e-6
LN_EPS = 1e-5


def rms_norm(x, gain):
    xf = x.astype(jnp.float32)
    y = xf * lax.rsqrt(jnp.mean(xf * xf, axis=-1, keepdims=True) + RMS_EPS)
    return (y * gain.astype(jnp.float32)).astype(x.dtype)

def layer_norm(x, gain, bias):
    xf = x.astype(jnp.float32)
    mu = jnp.mean(xf, axis=-1, keepdims=True)
    xc = xf - mu
    y = xc * lax.rsqrt(jnp.mean(xc * xc, axis=-1, keepdims=True) + LN_EPS)
    return (y * gain.astype(jnp.float32) + bias.astype(jnp.float32)).astype(x.dtype)

def partial_rotary(x, positions):
    inv_freq = ROPE_THETA ** (-jnp.arange(0, ROT_DIM, 2, dtype=jnp.float32) / ROT_DIM)
    ang = positions.astype(jnp.float32)[:, :, None, None] * inv_freq
    cos, sin = jnp.cos(ang), jnp.sin(ang)
    xf = x.astype(jnp.float32)
    x1 = xf[..., :ROT_HALF]
    x2 = xf[..., ROT_HALF:ROT_DIM]
    out = jnp.concatenate([x1 * cos - x2 * sin, x2 * cos + x1 * sin, xf[..., ROT_DIM:]], axis=-1)
    return out.astype(x.dtype)

def dilated_window_attention(q, k, v, window, dilation):
    B, H, S, Dh = q.shape
    L = S // dilation
    W = window // dilation
    nblk = -(-L // BLOCK_Q)
    Lp = nblk * BLOCK_Q

    def strided(t):
        return t.reshape(B, H, L, dilation, Dh).transpose(0, 1, 3, 2, 4)

    qs, ks, vs = strided(q), strided(k), strided(v)
    qs = jnp.pad(qs, ((0, 0), (0, 0), (0, 0), (0, Lp - L), (0, 0)))
    kv_pad = ((0, 0), (0, 0), (0, 0), (W, Lp - L), (0, 0))
    kp = jnp.pad(ks, kv_pad)
    vp = jnp.pad(vs, kv_pad)
    blk = jnp.arange(nblk)[:, None]
    col = jnp.arange(BLOCK_Q + W)[None, :]
    idx = blk * BLOCK_Q + col
    kb = kp[:, :, :, idx]
    vb = vp[:, :, :, idx]
    qb = qs.reshape(B, H, dilation, nblk, BLOCK_Q, Dh)

    scale = 1.0 / np.sqrt(HEAD_DIM)
    s = jnp.einsum('bhrnqd,bhrnkd->bhrnqk', qb, kb,
                   preferred_element_type=jnp.float32) * scale
    row = jnp.arange(BLOCK_Q)[:, None]
    dist = row + W - jnp.arange(BLOCK_Q + W)[None, :]
    key_pos = jnp.arange(nblk)[:, None, None] * BLOCK_Q + jnp.arange(BLOCK_Q + W)[None, None, :] - W
    mask = (dist >= 0)[None] & (dist <= W)[None] & (key_pos >= 0)
    s = jnp.where(mask, s, jnp.finfo(jnp.float32).min)
    m = jnp.max(s, axis=-1, keepdims=True)
    p = jnp.exp(s - m)
    denom = jnp.sum(p, axis=-1, keepdims=True)
    o = jnp.einsum('bhrnqk,bhrnkd->bhrnqd', p, vb.astype(jnp.float32)) / denom
    lse = (m + jnp.log(denom))[..., 0]
    o = o.reshape(B, H, dilation, Lp, Dh)[:, :, :, :L]
    lse = lse.reshape(B, H, dilation, Lp)[:, :, :, :L]
    o = o.transpose(0, 1, 3, 2, 4).reshape(B, H, S, Dh)
    lse = lse.transpose(0, 1, 3, 2).reshape(B, H, S)
    return o, lse

def dilated_mixture_attention(q, k, v):
    outs, lses = [], []
    for window, dilation in DILATED_PATTERNS:
        o, lse = dilated_window_attention(q, k, v, window, dilation)
        outs.append(o)
        lses.append(lse)
    wts = jax.nn.softmax(jnp.stack(lses, axis=0), axis=0)
    o = jnp.sum(wts[..., None] * jnp.stack(outs, axis=0), axis=0)
    return o.astype(q.dtype)

def spatial_gating(u, v, ln_gain, ln_bias, w_spatial, b_spatial):
    B, S, _ = u.shape
    u = jax.nn.gelu(u, approximate=False)
    v = layer_norm(jax.nn.gelu(v, approximate=False), ln_gain, ln_bias)
    vc = v.reshape(B, S // SGU_CHUNK, SGU_CHUNK, SGU_GROUPS, SGU_GROUP_DIM)
    causal = jnp.tril(jnp.ones((SGU_CHUNK, SGU_CHUNK), dtype=bool))
    w = jnp.where(causal[None], w_spatial, 0.0).astype(v.dtype)
    mixed = jnp.einsum('gij,bnjgc->bnigc', w, vc) + b_spatial.T[:, :, None].astype(v.dtype)
    return u * mixed.reshape(B, S, SGU_WIDTH)

def first_inputs(seed: int = 0) -> dict:
    key = jax.random.key(seed)
    ks = jax.random.split(key, 20)
    f32 = jnp.float32

    def nrm(k, shape, scale):
        return jax.random.normal(k, shape, f32) * scale

    def gain(k, width):
        return 1.0 + 0.05 * jax.random.normal(k, (DEPTH, width), f32)

    x = jax.random.normal(ks[0], (BATCH, SEQ, D_MODEL), f32)
    offsets = jax.random.randint(ks[1], (BATCH, 1), 0, 4096, dtype=jnp.int32)
    positions = (jnp.arange(SEQ, dtype=jnp.int32)[None, :] + offsets).astype(jnp.int32)
    return {
        "x": x,
        "positions": positions,
        "pre_mix_norm": gain(ks[2], D_MODEL),
        "w_in": nrm(ks[3], (DEPTH, D_MODEL, IN_PROJ_WIDTH), D_MODEL ** -0.5),
        "sgu_ln_gain": gain(ks[4], SGU_WIDTH),
        "sgu_ln_bias": nrm(ks[5], (DEPTH, SGU_WIDTH), 0.02),
        "sgu_w_spatial": nrm(ks[6], (DEPTH, SGU_GROUPS, SGU_CHUNK, SGU_CHUNK), 0.5 * SGU_CHUNK ** -0.5),
        "sgu_b_spatial": 1.0 + nrm(ks[7], (DEPTH, SGU_GROUPS, SGU_CHUNK), 0.1),
        "attn_out_norm": gain(ks[8], ATTN_WIDTH),
        "sgu_out_norm": gain(ks[9], SGU_WIDTH),
        "w_out": nrm(ks[10], (DEPTH, MIX_WIDTH, D_MODEL), MIX_WIDTH ** -0.5),
        "post_mix_norm": gain(ks[11], D_MODEL),
        "pre_ffn_norm": gain(ks[12], D_MODEL),
        "w_gate": nrm(ks[13], (DEPTH, D_MODEL, D_FF), D_MODEL ** -0.5),
        "w_up": nrm(ks[14], (DEPTH, D_MODEL, D_FF), D_MODEL ** -0.5),
        "w_down": nrm(ks[15], (DEPTH, D_FF, D_MODEL), D_FF ** -0.5),
        "post_ffn_norm": gain(ks[16], D_MODEL),
    }

def first_block(x, positions, pre_mix_norm, w_in, sgu_ln_gain, sgu_ln_bias, sgu_w_spatial,
              sgu_b_spatial, attn_out_norm, sgu_out_norm, w_out, post_mix_norm,
              pre_ffn_norm, w_gate, w_up, w_down, post_ffn_norm):
    B, S, _ = x.shape
    for l in range(DEPTH):
        h = rms_norm(x, pre_mix_norm[l])
        proj = h @ w_in[l]
        q, k, v_a, u, v_s = jnp.split(
            proj, [ATTN_WIDTH, 2 * ATTN_WIDTH, 3 * ATTN_WIDTH, 3 * ATTN_WIDTH + SGU_WIDTH], axis=-1)
        q = partial_rotary(q.reshape(B, S, ATTN_HEADS, HEAD_DIM), positions).transpose(0, 2, 1, 3)
        k = partial_rotary(k.reshape(B, S, ATTN_HEADS, HEAD_DIM), positions).transpose(0, 2, 1, 3)
        v_a = v_a.reshape(B, S, ATTN_HEADS, HEAD_DIM).transpose(0, 2, 1, 3)
        attn = dilated_mixture_attention(q, k, v_a)
        attn = attn.transpose(0, 2, 1, 3).reshape(B, S, ATTN_WIDTH)
        sgu = spatial_gating(u, v_s, sgu_ln_gain[l], sgu_ln_bias[l],
                             sgu_w_spatial[l], sgu_b_spatial[l])
        mixed = jnp.concatenate([rms_norm(attn, attn_out_norm[l]),
                                 rms_norm(sgu, sgu_out_norm[l])], axis=-1)
        y = mixed @ w_out[l]
        x = x + rms_norm(y, post_mix_norm[l])
        h = rms_norm(x, pre_ffn_norm[l])
        f = (jax.nn.silu(h @ w_gate[l]) * (h @ w_up[l])) @ w_down[l]
        x = x + rms_norm(f, post_ffn_norm[l])
    return x


MEM_LEN = 256
ATTN_HEADS_2 = 16
ATTN_KV_HEADS = 4
WINDOW = 128
BLOCK = 128
SSD_EXPAND = 2
D_INNER = SSD_EXPAND * D_MODEL
SSD_HEAD_DIM = 64
SSD_HEADS = D_INNER // SSD_HEAD_DIM
SSD_GROUPS = 8
D_STATE = 128
CONV_K = 5
CHUNK = 128
X_HEADS = 4
X_HEAD_DIM = 128
D_FF_2 = 4 * D_MODEL
EPS = 1e-6

Q_W = ATTN_HEADS_2 * HEAD_DIM
KV_W = ATTN_KV_HEADS * HEAD_DIM
BC_W = SSD_GROUPS * D_STATE
XBC_W = D_INNER + 2 * BC_W
DT_W = 2 * SSD_HEADS
GATE_W = 2 * D_MODEL
OFF_K = Q_W
OFF_V = OFF_K + KV_W
OFF_Z = OFF_V + KV_W
OFF_XBC = OFF_Z + D_INNER
OFF_DT = OFF_XBC + XBC_W
OFF_GATE = OFF_DT + DT_W
D_IN_PROJ = OFF_GATE + GATE_W


def rmsnorm(x, g):
    xf = x.astype(jnp.float32)
    y = xf * lax.rsqrt(jnp.mean(xf * xf, axis=-1, keepdims=True) + EPS)
    return (y * g.astype(jnp.float32)).astype(x.dtype)

def alibi_slopes(n_heads):
    return jnp.asarray(np.array([2.0 ** (-8.0 * (h + 1) / n_heads) for h in range(n_heads)], dtype=np.float32))

def windowed_gqa_sink(q, k, v, sink):
    b, l, H, d = q.shape
    kvh = k.shape[2]
    r = H // kvh
    nb = l // BLOCK
    qb = q.reshape(b, nb, BLOCK, kvh, r, d)
    pad = ((0, 0), (BLOCK, BLOCK), (0, 0), (0, 0))
    kp = jnp.pad(k, pad).reshape(b, nb + 2, BLOCK, kvh, d)
    vp = jnp.pad(v, pad).reshape(b, nb + 2, BLOCK, kvh, d)
    kw = jnp.concatenate([kp[:, :-2], kp[:, 1:-1], kp[:, 2:]], axis=2)
    vw = jnp.concatenate([vp[:, :-2], vp[:, 1:-1], vp[:, 2:]], axis=2)
    a_idx = np.arange(BLOCK)[:, None]
    w_idx = np.arange(3 * BLOCK)[None, :]
    rel = BLOCK + a_idx - w_idx
    in_band = np.abs(rel) <= WINDOW
    spos = (np.arange(nb)[:, None] - 1) * BLOCK + np.arange(3 * BLOCK)[None, :]
    valid = (spos >= 0) & (spos < l)
    mask = in_band[None] & valid[:, None, :]
    slopes = alibi_slopes(H).reshape(kvh, r, 1, 1)
    alibi = -slopes * jnp.asarray(np.abs(rel), jnp.float32)
    bias = jnp.where(jnp.asarray(mask)[:, None, None], alibi[None], -jnp.inf)
    s = jnp.einsum('bnqgrd,bnkgd->bngrqk', qb, kw).astype(jnp.float32) * (d ** -0.5) + bias[None]
    sink_f = sink.astype(jnp.float32).reshape(1, 1, kvh, r, 1, 1)
    m = jnp.maximum(jnp.max(s, axis=-1, keepdims=True), sink_f)
    p = jnp.exp(s - m)
    denom = jnp.sum(p, axis=-1, keepdims=True) + jnp.exp(sink_f - m)
    o = jnp.einsum('bngrqk,bnkgd->bnqgrd', (p / denom).astype(v.dtype), vw)
    return o.reshape(b, l, H * d)

def segsum_exp(a):
    T = a.shape[-1]
    cs = jnp.cumsum(a, axis=-1)
    diff = cs[..., :, None] - cs[..., None, :]
    tri = jnp.asarray(np.tril(np.ones((T, T), dtype=bool)))
    return jnp.where(tri, jnp.exp(jnp.where(tri, diff, 0.0)), 0.0)

def ssd_chunked(x, dt, A, Bm, Cm):
    b, l, H, P = x.shape
    G, N = Bm.shape[2], Bm.shape[3]
    r = H // G
    c = l // CHUNK
    xdt = (x * dt[..., None]).reshape(b, c, CHUNK, G, r, P)
    adt = jnp.moveaxis((dt * A).reshape(b, c, CHUNK, G, r), 2, -1)
    Bc = Bm.reshape(b, c, CHUNK, G, N)
    Cc = Cm.reshape(b, c, CHUNK, G, N)
    a_cs = jnp.cumsum(adt, axis=-1)
    CB = jnp.einsum('bclgn,bcsgn->bcgls', Cc, Bc)
    Wd = CB[:, :, :, None] * segsum_exp(adt)
    y_diag = jnp.einsum('bcgrls,bcsgrp->bclgrp', Wd, xdt)
    decay_states = jnp.exp(a_cs[..., -1:] - a_cs)
    states = jnp.einsum('bcsgn,bcgrs,bcsgrp->bcgrpn', Bc, decay_states, xdt)
    chunk_decay = jnp.exp(a_cs[..., -1])

    def step(carry, inp):
        st, dec = inp
        return carry * dec[..., None, None] + st, carry

    init = jnp.zeros((b, G, r, P, N), jnp.float32)
    _, prev = lax.scan(step, init, (jnp.moveaxis(states, 1, 0), jnp.moveaxis(chunk_decay, 1, 0)))
    prev = jnp.moveaxis(prev, 0, 1)
    y_off = jnp.einsum('bclgn,bcgrpn,bcgrl->bclgrp', Cc, prev, jnp.exp(a_cs))
    return (y_diag + y_off).reshape(b, l, H, P)

def depthwise_conv_centred(u, w, bias):
    out = lax.conv_general_dilated(u, w[:, None, :].astype(u.dtype), window_strides=(1,),
                                   padding=[(CONV_K // 2, CONV_K // 2)],
                                   dimension_numbers=('NWC', 'WIO', 'NWC'),
                                   feature_group_count=u.shape[-1])
    return out + bias.astype(u.dtype)

def ssd_branch(z, xbc, dt_raw, conv_w, conv_b, dt_bias, a_log, d_skip, norm_g):
    b, l, _ = z.shape
    f32 = jnp.float32
    xbc = jax.nn.silu(depthwise_conv_centred(xbc, conv_w, conv_b)).astype(f32)
    xs = xbc[..., :D_INNER].reshape(b, l, SSD_HEADS, SSD_HEAD_DIM)
    Bm = xbc[..., D_INNER:D_INNER + BC_W].reshape(b, l, SSD_GROUPS, D_STATE)
    Cm = xbc[..., D_INNER + BC_W:].reshape(b, l, SSD_GROUPS, D_STATE)
    A = -jnp.exp(a_log.astype(f32))
    dt = jax.nn.softplus(dt_raw.astype(f32).reshape(b, l, 2, SSD_HEADS) + dt_bias.astype(f32))
    y_fwd = ssd_chunked(xs, dt[:, :, 0], A[0], Bm, Cm)
    fl = lambda t: jnp.flip(t, axis=1)
    y_bwd = fl(ssd_chunked(fl(xs), fl(dt[:, :, 1]), A[1], fl(Bm), fl(Cm)))
    y = y_fwd + y_bwd + d_skip.astype(f32)[:, None] * xs
    y = y.reshape(b, l, D_INNER) * jax.nn.silu(z.astype(f32))
    yg = y.reshape(b, l, SSD_GROUPS, D_INNER // SSD_GROUPS)
    yg = yg * lax.rsqrt(jnp.mean(yg * yg, axis=-1, keepdims=True) + EPS)
    y = yg.reshape(b, l, D_INNER) * norm_g.astype(f32)
    return y.astype(z.dtype)

def cross_attention(h, mem_n, w_q, w_kv, w_o):
    b, l, _ = h.shape
    m = mem_n.shape[1]
    q = (h @ w_q).reshape(b, l, X_HEADS, X_HEAD_DIM)
    kv = mem_n @ w_kv
    k = kv[..., :X_HEADS * X_HEAD_DIM].reshape(b, m, X_HEADS, X_HEAD_DIM)
    v = kv[..., X_HEADS * X_HEAD_DIM:].reshape(b, m, X_HEADS, X_HEAD_DIM)
    s = jnp.einsum('blhd,bmhd->bhlm', q, k).astype(jnp.float32) * (X_HEAD_DIM ** -0.5)
    p = jax.nn.softmax(s, axis=-1)
    o = jnp.einsum('bhlm,bmhd->blhd', p.astype(v.dtype), v).reshape(b, l, X_HEADS * X_HEAD_DIM)
    return o @ w_o

def second_inputs(seed: int = 0) -> dict:
    key = jax.random.key(seed)
    ks = iter(jax.random.split(key, 32))
    f32 = jnp.float32

    def dense(shape, fan_in):
        return jax.random.normal(next(ks), shape, f32) * (fan_in ** -0.5)

    def gain(shape):
        return 1.0 + 0.02 * jax.random.normal(next(ks), shape, f32)

    x = jax.random.normal(next(ks), (BATCH, SEQ, D_MODEL), f32)
    mem = jax.random.normal(next(ks), (BATCH, MEM_LEN, D_MODEL), f32)
    norm_mix = gain((DEPTH, D_MODEL))
    w_in = dense((DEPTH, D_MODEL, D_IN_PROJ), D_MODEL)
    attn_sink = 0.1 * jax.random.normal(next(ks), (DEPTH, ATTN_HEADS_2), f32)
    conv_w = dense((DEPTH, CONV_K, XBC_W), CONV_K)
    conv_b = 0.01 * jax.random.normal(next(ks), (DEPTH, XBC_W), f32)
    dt0 = jnp.exp(jax.random.uniform(next(ks), (DEPTH, 2, SSD_HEADS), f32,
                                     minval=math.log(1e-3), maxval=math.log(1e-1)))
    dt_bias = dt0 + jnp.log(-jnp.expm1(-dt0))
    a_log = jnp.log(jax.random.uniform(next(ks), (DEPTH, 2, SSD_HEADS), f32, minval=1.0, maxval=16.0))
    d_skip = gain((DEPTH, SSD_HEADS))
    ssd_norm = gain((DEPTH, D_INNER))
    w_attn_branch = dense((DEPTH, Q_W, D_MODEL), Q_W)
    w_ssd_branch = dense((DEPTH, D_INNER, D_MODEL), D_INNER)
    w_out = dense((DEPTH, D_MODEL, D_MODEL), D_MODEL)
    norm_cross = gain((DEPTH, D_MODEL))
    norm_mem = gain((DEPTH, D_MODEL))
    w_xq = dense((DEPTH, D_MODEL, X_HEADS * X_HEAD_DIM), D_MODEL)
    w_xkv = dense((DEPTH, D_MODEL, 2 * X_HEADS * X_HEAD_DIM), D_MODEL)
    w_xo = dense((DEPTH, X_HEADS * X_HEAD_DIM, D_MODEL), X_HEADS * X_HEAD_DIM)
    norm_ffn = gain((DEPTH, D_MODEL))
    w_up = dense((DEPTH, D_MODEL, D_FF_2), D_MODEL)
    w_down = dense((DEPTH, D_FF_2, D_MODEL), D_FF_2)
    norm_final = gain((D_MODEL,))
    return {"x": x, "mem": mem, "norm_mix": norm_mix, "w_in": w_in, "attn_sink": attn_sink,
            "conv_w": conv_w, "conv_b": conv_b, "dt_bias": dt_bias, "a_log": a_log,
            "d_skip": d_skip, "ssd_norm": ssd_norm, "w_attn_branch": w_attn_branch,
            "w_ssd_branch": w_ssd_branch, "w_out": w_out, "norm_cross": norm_cross,
            "norm_mem": norm_mem, "w_xq": w_xq, "w_xkv": w_xkv, "w_xo": w_xo,
            "norm_ffn": norm_ffn, "w_up": w_up, "w_down": w_down, "norm_final": norm_final}

def second_block(x, mem, norm_mix, w_in, attn_sink, conv_w, conv_b, dt_bias, a_log, d_skip,
              ssd_norm, w_attn_branch, w_ssd_branch, w_out, norm_cross, norm_mem, w_xq,
              w_xkv, w_xo, norm_ffn, w_up, w_down, norm_final):
    b, l, _ = x.shape
    for i in range(DEPTH):
        h = rmsnorm(x, norm_mix[i])
        proj = h @ w_in[i]
        q = proj[..., :OFF_K].reshape(b, l, ATTN_HEADS_2, HEAD_DIM)
        k = proj[..., OFF_K:OFF_V].reshape(b, l, ATTN_KV_HEADS, HEAD_DIM)
        v = proj[..., OFF_V:OFF_Z].reshape(b, l, ATTN_KV_HEADS, HEAD_DIM)
        z = proj[..., OFF_Z:OFF_XBC]
        xbc = proj[..., OFF_XBC:OFF_DT]
        dt_raw = proj[..., OFF_DT:OFF_GATE]
        gate_a = proj[..., OFF_GATE:OFF_GATE + D_MODEL]
        gate_b = proj[..., OFF_GATE + D_MODEL:]
        attn = windowed_gqa_sink(q, k, v, attn_sink[i])
        ssd = ssd_branch(z, xbc, dt_raw, conv_w[i], conv_b[i], dt_bias[i], a_log[i],
                         d_skip[i], ssd_norm[i])
        merged = (jax.nn.sigmoid(gate_a) * (attn @ w_attn_branch[i])
                  + jax.nn.sigmoid(gate_b) * (ssd @ w_ssd_branch[i]))
        x = x + merged @ w_out[i]
        h = rmsnorm(x, norm_cross[i])
        x = x + cross_attention(h, rmsnorm(mem, norm_mem[i]), w_xq[i], w_xkv[i], w_xo[i])
        h = rmsnorm(x, norm_ffn[i])
        x = x + jnp.square(jax.nn.relu(h @ w_up[i])) @ w_down[i]
    return rmsnorm(x, norm_final)


def setup_inputs(seed=0):
    out = dict(first_inputs(seed))
    for name, value in second_inputs(seed + 1).items():
        if name != "x":
            out[name + "_2"] = value
    return out


def reference(
    x, positions, pre_mix_norm, w_in, sgu_ln_gain, sgu_ln_bias, sgu_w_spatial, sgu_b_spatial,
    attn_out_norm, sgu_out_norm, w_out, post_mix_norm, pre_ffn_norm, w_gate, w_up, w_down,
    post_ffn_norm, mem_2, norm_mix_2, w_in_2, attn_sink_2, conv_w_2, conv_b_2, dt_bias_2,
    a_log_2, d_skip_2, ssd_norm_2, w_attn_branch_2, w_ssd_branch_2, w_out_2, norm_cross_2,
    norm_mem_2, w_xq_2, w_xkv_2, w_xo_2, norm_ffn_2, w_up_2, w_down_2, norm_final_2,
):
    x = first_block(
        x, positions, pre_mix_norm, w_in, sgu_ln_gain, sgu_ln_bias, sgu_w_spatial,
        sgu_b_spatial, attn_out_norm, sgu_out_norm, w_out, post_mix_norm, pre_ffn_norm, w_gate,
        w_up, w_down, post_ffn_norm,
    )
    return second_block(
        x, mem_2, norm_mix_2, w_in_2, attn_sink_2, conv_w_2, conv_b_2, dt_bias_2, a_log_2,
        d_skip_2, ssd_norm_2, w_attn_branch_2, w_ssd_branch_2, w_out_2, norm_cross_2,
        norm_mem_2, w_xq_2, w_xkv_2, w_xo_2, norm_ffn_2, w_up_2, w_down_2, norm_final_2,
    )


_drawn_inputs = setup_inputs


def setup_inputs(seed=0):
    import zlib

    import numpy as np

    out = dict(_drawn_inputs(seed))
    spreads = {}
    factors = {'sgu_ln_gain': 5.494,
     'sgu_ln_bias': 8.0,
     'norm_mix_2': 5.751,
     'attn_sink_2': 8.0,
     'conv_b_2': 8.0,
     'd_skip_2': 8.0,
     'ssd_norm_2': 8.0,
     'norm_cross_2': 8.0,
     'norm_mem_2': 8.0,
     'norm_ffn_2': 4.023,
     'norm_final_2': 2.943}
    for name, (base, spread) in spreads.items():
        noise = np.random.default_rng([zlib.crc32(name.encode()), seed]).standard_normal(out[name].shape)
        drawn = base * np.exp(spread * noise) if base else spread * noise
        out[name] = __import__('jax').numpy.asarray(drawn.astype(out[name].dtype))
    for name, factor in factors.items():
        out[name] = (out[name] * factor).astype(out[name].dtype)
    return out
```

```python
from collections import deque
from contextlib import ExitStack

import numpy as np

import concourse.bass as bass
from concourse import mybir

ALU = mybir.AluOpType
ACT = mybir.ActivationFunctionType
AX = mybir.AxisListType
F32 = mybir.dt.float32
F32R = mybir.dt.float32r
I32 = mybir.dt.int32

S = 512
D = 1024
RMS_EPS = 1e-6
LN_EPS = 1e-5
NEG = -1e30
TWO_PI = 2.0 * np.pi
PI_C1 = 6.28125
PI_C2 = float(np.float32(np.round((TWO_PI - PI_C1) * 2.0 ** 20) / 2.0 ** 20))
PI_C3 = float(np.float32(TWO_PI - PI_C1 - PI_C2))
MAGIC = 12582912.0
PI_IN = 3.1415925

NRAW, NHL, AHEAD = 4, 6, 4
NTB = 7
RA = (2, 2, 4, 5, 3)
SCRATCH = {"ys": (2048, 512), "cs": (32, 1024), "km": (128, 1024), "vm": (128, 1024), "x": (128, 4096)}
FF1 = [(0, 4), (4, 4), (8, 3)]
NFF2 = 4

C_ID, C_PERM, C_BT, C_NB, C_TF, C_TB, C_LL, C_FF, C_SF, C_AF = 0, 128, 256, 768, 1152, 1280, 1408, 1536, 1664, 1665
C_W = 1672


def constants():
    c = np.zeros((128, C_W), np.float32)
    i = np.arange(128)
    c[:, C_ID:C_ID + 128] = np.eye(128)
    perm = np.zeros((128, 128), np.float32)
    for p in range(128):
        m = p % 64
        if m < 16:
            perm[p - m + (m + 8) % 16, p] = 1.0
    c[:, C_PERM:C_PERM + 128] = perm
    for n, delta in enumerate((3, 2, 1, 0)):
        dist = 128 * delta + i[:, None] - i[None, :]
        count = ((dist >= 0) & (dist <= 128)).astype(int) + ((dist >= 0) & (dist % 4 == 0)) + ((dist >= 0) & (dist % 16 == 0))
        c[:, C_BT + 128 * n:C_BT + 128 * (n + 1)] = np.where(count > 0, np.log(np.maximum(count, 1)), NEG)
    rel = 128 + i[:, None] - np.arange(384)[None, :]
    c[:, C_NB:C_NB + 384] = np.where(np.abs(rel) <= 128, -np.abs(rel), NEG)
    c[:, C_TF:C_TF + 128] = i[:, None] <= i[None, :]
    c[:, C_TB:C_TB + 128] = i[:, None] >= i[None, :]
    c[127, C_LL:C_LL + 128] = 1.0
    c[0, C_FF:C_FF + 128] = 1.0
    inv = np.float32(500000.0) ** (-np.arange(0, 16, 2, dtype=np.float32) / np.float32(16))
    for p in range(128):
        m = p % 64
        if m < 16:
            c[p, C_AF] = inv[m % 8]
            c[p, C_SF] = -1.0 if m < 8 else 1.0
    return c


class Engine:

    def __init__(self, sem):
        self.sem, self.n, self.steps, self.seen = sem, 0, [], {}

    def wait(self, *tokens):
        for t in tokens:
            if t is None:
                continue
            if isinstance(t, list):
                self.wait(*t)
                continue
            sem, value = t
            key = id(sem)
            if self.seen.get(key, 0) < value:
                self.seen[key] = value
                self.steps.append(lambda e, s=sem, v=value: e.wait_ge(s, v))

    def do(self, fn, *tokens, sig=True):
        self.wait(*tokens)
        if not sig:
            self.steps.append(fn)
            return None
        self.n += 1
        self.steps.append(lambda e: fn(e).then_inc(self.sem, 1))
        return (self.sem, self.n)

    def emit(self, e):
        for s in self.steps:
            s(e)


class Line:

    def __init__(self, sem):
        self.sem, self.n = sem, 0

    def go(self, eng, fn, *tokens):
        eng.wait(*tokens)
        self.n += 16
        eng.steps.append(lambda e: fn(e).then_inc(self.sem, 16))
        return (self.sem, self.n)


class Ring:

    def __init__(self, bufs):
        self.free = deque((b, None) for b in bufs)

    def take(self):
        return self.free.popleft()

    def give(self, buf, tok):
        self.free.append((buf, tok))


def bc(ap, n):
    a, b = ap.shape[0], ap.shape[1]
    return ap.unsqueeze(2).to_broadcast([a, b, n])


def mid(ap, n):
    a, b = ap.shape[0], ap.shape[1]
    return ap.unsqueeze(1).to_broadcast([a, n, b])


def build(nc, A, out, scr, dbg=None):
    ctx = ExitStack()
    with ctx:
        def sem(name):
            return ctx.enter_context(nc.semaphore(name))

        def sb(name, shape, dt=F32, c=ctx):
            return c.enter_context(nc.sbuf_tensor(name, shape, dt))

        pe, act, dve, pool, sp = (Engine(sem(f"s_{n}")) for n in ("pe", "act", "dve", "pool", "sp"))
        psum = [ctx.enter_context(nc.psum_tensor(f"ps{i}", [128, 512], F32)) for i in range(8)]
        main = Ring(psum[:4])
        side = Ring(psum[4:])

        RAW = [sb(f"raw{i}", [128, 2, 512]) for i in range(NRAW)]
        HI = [sb(f"hi{i}", [128, 2, 512], F32R) for i in range(NHL)]
        LO = [sb(f"lo{i}", [128, 2, 512], F32R) for i in range(NHL)]
        hH = sb("hH", [128, 8, S], F32R)
        hL = sb("hL", [128, 8, S], F32R)
        X = sb("X", [128, 4, D])
        CST = sb("CST", [128, C_W])
        ST = sb("ST", [128, 256])
        half = sb("half", [128, 16])

        ident = CST[:, C_ID:C_ID + 128]

        def line(name):
            return Line(sem(name))

        l_cst = line("l_cst")
        CSQ = pool
        t_cst = l_cst.go(sp, lambda e: e.dma_start(CST[:, :], A["consts"]))
        t_half = pool.do(lambda e: e.memset(half[:, :], -0.5))

        stat = [0]

        def small(n):
            if stat[0] + n > 256:
                stat[0] = 0
            a = stat[0]
            stat[0] += n
            return ST[:, a:a + n]

        small_tok = []

        def mm(outp, lhsT, rhs, start, stop, *tok, sig=False):
            return pe.do(lambda e: e.matmul(outp, lhsT, rhs, start=start, stop=stop), *tok, sig=sig)

        def tr(outp, inp, n, *tok, sig=False):
            return pe.do(lambda e: e.transpose(outp, inp, ident[0:n, 0:n]), *tok, sig=sig)

        def copy_act(o, i, *tok, func=ACT.Copy, **kw):
            return act.do(lambda e: e.activation(o, i, func, **kw), *tok)

        def tt(eng, o, a, b, op, *tok):
            return eng.do(lambda e: e.tensor_tensor(o, a, b, op), *tok)

        def ts(eng, o, a, s1, s2, op0, op1, *tok):
            if s2 is None:
                return eng.do(lambda e: e.tensor_scalar(o, a, s1, None, op0), *tok)
            return eng.do(lambda e: e.tensor_scalar(o, a, s1, s2, op0, op1), *tok)

        def stt(o, a, s, b, op0, op1, *tok):
            return dve.do(lambda e: e.scalar_tensor_tensor(out=o, in0=a, scalar=s, in1=b, op0=op0, op1=op1), *tok)

        def fn_act(o, i, func, *tok, **kw):
            return act.do(lambda e: e.activation(o, i, func, **kw), *tok)

        def ttr(o, a, b, init, op0, op1, acc, *tok):
            return dve.do(lambda e: e.tensor_tensor_reduce(o, a, b, 1.0, init, op0, op1, acc), *tok)

        def copy_dve(o, i, *tok):
            return dve.do(lambda e: e.tensor_copy(o, i), *tok)

        def recip(o, i, *tok):
            return dve.do(lambda e: e.reciprocal(o, i), *tok)

        def rstd(o, ss, n, eps, *tok):
            k = ss.shape[1]
            t = ts(pool, o, ss, 1.0 / n, eps, ALU.mult, ALU.add, *tok)
            return tt(pool, o, o, half[:, 0:k], ALU.pow, t, t_half)

        def split_from(src, hi, lo, *tok):
            th = copy_act(hi, src, *tok)
            tl = tt(dve, lo, src, hi.bitcast(F32), ALU.subtract, th, *tok)
            return th, tl

        dumps = line("l_dbg") if dbg is not None else None

        def dump(name, ap, *tok):
            if dbg is not None and name in dbg:
                pool_wait = dumps.go(pool, lambda e: e.dma_start(dbg[name], ap), *tok)
                for q in (pool, act, dve, pe, sp):
                    q.wait(pool_wait)

        units = []

        def plan(tag, parts_of, n, cols=512):
            for u in range(n):
                units.append((tag, parts_of(u), cols))

        def rows(w, u, c0, c1):
            return w[256 * u:256 * u + 256, c0:c1].rearrange("(k p) n -> p k n", p=128)

        def cols_of(name, c0, c1):
            w = A[name][0]
            return lambda u: [(0, rows(w, u, c0, c1))]

        def cols2(n1, a0, a1, n2, b0, b1):
            w1, w2 = A[n1][0], A[n2][0]
            return lambda u: [(0, rows(w1, u, a0, a1)), (a1 - a0, rows(w2, u, b0, b1))]

        XBC = 1536 + 2048
        B0, C0 = XBC + 2048, XBC + 3072
        DT0 = XBC + 4096
        G0 = DT0 + 64
        plan("xk", cols_of("w_xkv_2", 0, 512), 4)
        plan("xv", cols_of("w_xkv_2", 512, 1024), 4)
        for n, c in (("q", 0), ("k", 512), ("v", 1024), ("vs", 2048), ("u", 1536)):
            plan("in_" + n, cols_of("w_in", c, c + 512), 4)
        for h in range(2):
            plan("wout", cols_of("w_out", 512 * h, 512 * h + 512), 4)
        for b0, nb in FF1:
            for b in range(b0, b0 + nb):
                plan("gu", cols2("w_gate", 256 * b, 256 * b + 256, "w_up", 256 * b, 256 * b + 256), 4)
            for h in range(2):
                w = A["w_down"][0][256 * b0:256 * (b0 + nb), 512 * h:512 * h + 512]
                plan("down", lambda u, w=w: [(0, w[256 * u:256 * u + 256, :].rearrange("(k p) n -> p k n", p=128))], nb)
        plan("dt", cols_of("w_in_2", DT0, DT0 + 64), 4, 64)
        for j in range(4):
            plan("bc", cols2("w_in_2", B0 + 256 * j, B0 + 256 * j + 256, "w_in_2", C0 + 256 * j, C0 + 256 * j + 256), 4)
            plan("xs", cols_of("w_in_2", XBC + 512 * j, XBC + 512 * j + 512), 4)
            plan("z", cols_of("w_in_2", 1536 + 512 * j, 1536 + 512 * j + 512), 4)
        plan("kv2", cols_of("w_in_2", 1024, 1536), 4)
        for j in range(2):
            wq = A["w_in_2"][0]
            for u in range(4):
                units.append(("q2", [((k, b), wq[256 * u + 128 * k:256 * u + 128 * k + 128, 512 * j + 256 * b:512 * j + 256 * b + 256].rearrange(
                    "p (f c) -> p f c", c=64)) for k in range(2) for b in range(2)], 512))
        for j in range(4):
            plan("gate", cols_of("w_in_2", G0 + 512 * j, G0 + 512 * j + 512), 4)
        for j in range(2):
            w = A["w_ssd_branch_2"][0]
            for u in range(8):
                units.append(("wssd", [(0, rows(w, u, 512 * j, 512 * j + 512))], 512))
                units.append(("ys", [(0, rows(scr["ys"], u, 0, 512))], 512))
        for j in range(2):
            plan("wattn", cols_of("w_attn_branch_2", 512 * j, 512 * j + 512), 4)
        for h in range(2):
            plan("wout2", cols_of("w_out_2", 512 * h, 512 * h + 512), 4)
        plan("xq", cols_of("w_xq_2", 0, 512), 4)
        for h in range(2):
            plan("xo", cols_of("w_xo_2", 512 * h, 512 * h + 512), 2)
        for f in range(NFF2):
            for b in range(2):
                c = 1024 * f + 512 * b
                plan("up2", cols_of("w_up_2", c, c + 512), 4)
            for h in range(2):
                w = A["w_down_2"][0][1024 * f:1024 * f + 1024, 512 * h:512 * h + 512]
                plan("down2", lambda u, w=w: [(0, w[256 * u:256 * u + 256, :].rearrange("(k p) n -> p k n", p=128))], 4)

        l_raw = [line(f"l_raw{i}") for i in range(NRAW)]
        raw_free = [None] * NRAW
        hl_free = [None] * NHL
        unit_tok = {}
        ys_done = []
        st_ = {"load": 0, "conv": 0, "use": 0}

        def load_next():
            i = st_["load"]
            if i >= len(units):
                return
            st_["load"] += 1
            tag, parts, _ = units[i]
            r = i % NRAW
            dep = ys_done if tag == "ys" else None
            for c0, src in parts:
                if tag == "q2":
                    dst = RAW[r][:, c0[0], :].rearrange("p (f b c) -> p f b c", b=2, c=64)[:, :, c0[1], :]
                else:
                    dst = RAW[r][:, :, c0:c0 + src.shape[2]]
                t = l_raw[r].go(sp, lambda e, s=src, d=dst: e.dma_start(d, s), raw_free[r], dep)
            unit_tok[i] = t

        def convert_next():
            i = st_["conv"]
            if i >= len(units):
                return
            assert i < st_["load"] and i - NHL in released
            st_["conv"] += 1
            w = units[i][2]
            r, s = i % NRAW, i % NHL
            th = copy_act(HI[s][:, :, 0:w], RAW[r][:, :, 0:w], unit_tok[i], hl_free[s])
            tl = tt(dve, LO[s][:, :, 0:w], RAW[r][:, :, 0:w], HI[s][:, :, 0:w].bitcast(F32), ALU.subtract, th, hl_free[s])
            raw_free[r] = [th, tl]
            unit_tok[i] = [th, tl]
            load_next()

        def take_unit(tag):
            i = st_["use"]
            assert units[i][0] == tag, (units[i][0], tag)
            st_["use"] += 1
            while st_["conv"] <= i:
                convert_next()
            return i, HI[i % NHL], LO[i % NHL], unit_tok[i]

        released = set(range(-NHL, 0))

        def release(i, tok):
            hl_free[i % NHL] = tok
            released.add(i)

        def look_ahead():
            if st_["conv"] < st_["use"] + AHEAD and st_["conv"] - NHL in released:
                convert_next()

        bg = deque()

        def pump(n=1):
            while n > 0 and bg:
                try:
                    next(bg[0])
                    n -= 1
                except StopIteration:
                    bg.popleft()

        def drain():
            while bg:
                pump(1)

        def fm_block(tag, nu, nf, act_h, act_l, a_tok, evac, rate=0, N=S):
            banks = [main.take() for _ in range(nf)]
            for u in range(nu):
                look_ahead()
                i, wh, wl, wt = take_unit(tag)
                for f in range(nf):
                    bank, bt = banks[f]
                    for kk in range(2):
                        k = 2 * u + kk
                        first, last = k == 0, k == 2 * nu - 1
                        w_h, w_l = wh[:, kk, 128 * f:128 * f + 128], wl[:, kk, 128 * f:128 * f + 128]
                        mm(bank[:, 0:N], w_h, act_h[:, k, 0:N], first, False, wt, a_tok, bt if first else None)
                        mm(bank[:, 0:N], w_h, act_l[:, k, 0:N], False, False)
                        t = mm(bank[:, 0:N], w_l, act_h[:, k, 0:N], False, last, sig=last or (f == nf - 1 and kk == 1))
                    if last:
                        main.give(bank, evac(f, bank, t))
                release(i, t)
                pump(rate)
            return t

        def tm_mms(bank, ntok, nu, u, kk, w, wh, wl, act_h, act_l, t, *tok, sig=False):
            k = 2 * u + kk
            first, last = k == 0, k == 2 * nu - 1
            a_h, a_l = act_h[:, k, 128 * t:128 * t + 128], act_l[:, k, 128 * t:128 * t + 128]
            mm(bank, a_h, wh[:, kk, w[0]:w[1]], first, False, *tok)
            mm(bank, a_h, wl[:, kk, w[0]:w[1]], False, False)
            return mm(bank, a_l, wh[:, kk, w[0]:w[1]], False, last, sig=sig or last)

        def tm_block(tag, nu, act_h, act_l, a_tok, evac, rate=0, ntok=4, tail=False):
            banks = [main.take() for _ in range(ntok)]
            if tail:
                us = []
                for u in range(nu):
                    look_ahead()
                    us.append(take_unit(tag))
                for t in range(ntok):
                    bank, bt = banks[t]
                    for u in range(nu):
                        i, wh, wl, wt = us[u]
                        for kk in range(2):
                            tok = tm_mms(bank[:, :], ntok, nu, u, kk, (0, 512), wh, wl, act_h, act_l, t, wt, a_tok, bt, sig=(t == ntok - 1 and kk == 1))
                        if t == ntok - 1:
                            release(i, tok)
                            look_ahead()
                    main.give(bank, evac(t, bank, tok))
                return tok
            for u in range(nu):
                look_ahead()
                i, wh, wl, wt = take_unit(tag)
                for t in range(ntok):
                    bank, bt = banks[t]
                    for kk in range(2):
                        first = u == 0 and kk == 0
                        tok = tm_mms(bank[:, :], ntok, nu, u, kk, (0, 512), wh, wl, act_h, act_l, t, wt, a_tok, bt if first else None, sig=(t == ntok - 1 and kk == 1))
                    if u == nu - 1:
                        main.give(bank, evac(t, bank, tok))
                release(i, tok)
                pump(rate)
            return tok

        hn_ring = Ring([sb(f"hn{i}", [128, D]) for i in range(2)])
        l_gain = [line(f"l_gain{i}") for i in range(3)]
        gains = Ring([(sb(f"gain{i}", [128, D]), l_gain[i]) for i in range(2)])

        def load_gain(*parts):
            (g, ln), free = gains.take()
            c = 0
            for p in parts:
                n = p.shape[-1]
                t = ln.go(sp, lambda e, p=p, c=c, n=n: e.dma_start(g[:, c:c + n], p.partition_broadcast(128)), free)
                c += n
            return (g, ln), t

        def square_sum(o, x, *tok):
            hn, ht = hn_ring.take()
            t = fn_act(hn[:, 0:x.shape[1]], x, ACT.Square, ht, *tok, accum_out=o)
            hn_ring.give(hn, t)
            return t

        def turn(src, nk, hi, lo, t0, h_free, *tok):
            done = []
            for b in range(0, nk, 4):
                n = min(4, nk - b)
                bank, bt = side.take()
                for k in range(n):
                    t = tr(bank[:, 128 * k:128 * k + 128], src[:, 128 * (b + k):128 * (b + k) + 128], 128, t_cst, bt if k == 0 else None, *tok, sig=k == n - 1)
                v = bank[:, 0:128 * n].rearrange("p (k t) -> p k t", k=n)
                th, tl = split_from(v, hi[:, b:b + n, t0:t0 + 128], lo[:, b:b + n, t0:t0 + 128], t, h_free)
                side.give(bank, [th, tl])
                done += [th, tl]
            return done, t

        def norm_turn(x, gain, g_tok, t0, hi, lo, h_free, *tok):
            ss = small(1)
            t = square_sum(ss, x, *tok)
            t = rstd(ss, ss, D, RMS_EPS, t)
            (hn, ht) = hn_ring.take()
            t = stt(hn[:, :], x, ss, gain[:, :], ALU.mult, ALU.mult, t, ht, g_tok)
            done, last = turn(hn, 8, hi, lo, t0, h_free, t)
            hn_ring.give(hn, last)
            return done, t

        for _ in range(NRAW):
            load_next()
        P0 = ExitStack()
        MEMX = sb("MEMX", [128, 2, D], c=P0)
        KM0 = sb("KM0", [128, 4, 256], c=P0)
        VM0 = sb("VM0", [128, 2, 512], c=P0)
        mH = sb("mH", [128, 8, 256], F32R, c=P0)
        mL = sb("mL", [128, 8, 256], F32R, c=P0)
        l_x = [line(f"l_x{i}") for i in range(6)]
        t_mem = [l_x[4 + t].go(act, lambda e, t=t: e.dma_start(MEMX[:, t, :], A["mem_2"][0, 128 * t:128 * t + 128, :])) for t in range(2)]
        g_mem, tg_mem = load_gain(A["norm_mem_2"][0])
        g_pre, tg_pre = load_gain(A["pre_mix_norm"][0])
        t_x = [l_x[t].go(act, lambda e, t=t: e.dma_start(X[:, t, :], A["x"][0, 128 * t:128 * t + 128, :])) for t in range(4)]
        mtok = []
        for t in range(2):
            d, last = norm_turn(MEMX[:, t, :], g_mem[0], tg_mem, 128 * t, mH, mL, None, t_mem[t])
            mtok += d
        gains.give(g_mem, last)

        km_tok, vm_tok = [], []

        def evac_km(f, bank, t):
            r = copy_act(KM0[:, f, :], bank[:, 0:256], t)
            km_tok.append(r)
            return r

        def evac_vm(t_, bank, t):
            r = copy_act(VM0[:, t_, :], bank[:, :], t)
            vm_tok.append(r)
            return r

        fm_block("xk", 4, 4, mH, mL, mtok, evac_km, N=256)
        mem_mm = tm_block("xv", 4, mH, mL, mtok, evac_vm, ntok=2)
        l_kv = line("l_kv")
        l_kv.go(act, lambda e: e.dma_start(scr["km"], KM0[:, :, :].rearrange("p f t -> p (f t)")), km_tok)
        kv_saved = l_kv.go(act, lambda e: e.dma_start(scr["vm"], VM0[:, :, :].rearrange("p f t -> p (f t)")), vm_tok)
        mem_free = [mem_mm, kv_saved]

        htok = []
        for t in range(4):
            d, last = norm_turn(X[:, t, :], g_pre[0], tg_pre, 128 * t, hH, hL, None, t_x[t])
            htok += d
        gains.give(g_pre, last)
        P0.close()

        P1 = ExitStack()
        Q = sb("Q", [128, 4, S], c=P1)
        K = sb("K", [128, 4, S], c=P1)
        V = sb("V", [128, 4, 512], c=P1)
        VS = sb("VS", [128, 4, 512], c=P1)
        MIX = sb("MIX", [128, 4, D], c=P1)
        RC = sb("RC", [128, S], c=P1)
        RS = sb("RS", [128, S], c=P1)
        TMPA = [sb(f"tmpa{i}", [128, 512], c=P1) for i in range(4)]
        tmp = Ring(TMPA)
        WS = MIX[:, 0:2, 0:512]
        WT = sb("WT", [128, 8, 128], c=P1)
        SB_ = sb("SBs", [128, 8], c=P1)
        l_p1 = line("l_p1")
        
        def ld(o, i, *tok, slow=False):
            return l_p1.go(sp, lambda e: e.dma_start(o, i, allow_slow_non_contiguous=slow), *tok)

        g_ln, tg_ln = load_gain(A["sgu_ln_gain"][0], A["sgu_ln_bias"][0])
        posi, pt_ = tmp.take()
        ld(SB_[:, :], A["sgu_b_spatial"][0].rearrange("g i -> i g"), mem_free, mtok, slow=True)
        POSI = posi[:, :].bitcast(I32)
        ld(POSI, A["positions"][0].partition_broadcast(128))
        ld(MIX[:, 0, :].rearrange("p (g j) -> p g j", g=8), A["sgu_w_spatial"][0].rearrange("g i j -> i g j"))
        t_p1 = (l_p1.sem, l_p1.n)

        def rotary_tables():
            a, at = tmp.take()
            b, bt_ = tmp.take()
            t = dve.do(lambda e: e.tensor_copy(a[:, :], POSI), t_p1, at, mem_free)
            tmp.give(posi, t)
            t = ts(dve, a[:, :], a[:, :], CST[:, C_AF:C_AF + 1], None, ALU.mult, None, t, t_cst)
            t = ts(dve, b[:, :], a[:, :], float(np.float32(1.0 / TWO_PI)), MAGIC, ALU.mult, ALU.add, t, bt_)
            t = ts(dve, b[:, :], b[:, :], MAGIC, None, ALU.subtract, None, t)
            for c in (PI_C1, PI_C2, PI_C3):
                t = stt(a[:, :], b[:, :], -c, a[:, :], ALU.mult, ALU.add, t)
            t = ts(dve, a[:, :], a[:, :], PI_IN, -PI_IN, ALU.min, ALU.max, t)
            yield
            t1 = act.do(lambda e: e.activation(RS[:, :], a[:, :], ACT.Sin), t)
            t2 = act.do(lambda e: e.activation(b[:, :], a[:, :], ACT.Abs), t)
            t2 = ts(dve, b[:, :], b[:, :], -1.0, float(np.pi / 2), ALU.mult, ALU.add, t2)
            t2 = act.do(lambda e: e.activation(RC[:, :], b[:, :], ACT.Sin), t2)
            t1 = ts(dve, RS[:, :], RS[:, :], CST[:, C_SF:C_SF + 1], None, ALU.mult, None, t1)
            rot_tok.extend([t1, t2])
            tmp.give(a, [t1, t2])
            tmp.give(b, t2)
            yield

        rot_tok = []
        bg.append(rotary_tables())
        pump(2)
        q_tok, k_tok, v_tok = {}, {}, {}

        def rope(dst, f, tok_d, t0):
            bank, bt = side.take()
            t = mm(bank[:, :], CST[:, C_PERM:C_PERM + 128], dst[:, f, :], True, True, t0, bt, t_cst, sig=True)
            a, at = tmp.take()
            t1 = tt(dve, a[:, :], bank[:, :], RS[:, :], ALU.mult, t, at, rot_tok)
            side.give(bank, t1)
            t2 = tt(pool, dst[:, f, :], dst[:, f, :], RC[:, :], ALU.mult, t, rot_tok)
            t3 = tt(pool, dst[:, f, :], dst[:, f, :], a[:, :], ALU.add, t1, t2)
            tmp.give(a, t3)
            tok_d[f] = t3
            yield

        def evac_rope(dst, tok_d, scale):
            def evac(f, bank, t):
                r = copy_act(dst[:, f, :], bank[:, :], t, mem_free, mtok, scale=scale)
                bg.append(rope(dst, f, tok_d, r))
                return r
            return evac

        def evac_v(t_, bank, t):
            v_tok[t_] = copy_act(V[:, t_, :], bank[:, :], t)
            return v_tok[t_]

        fm_block("in_q", 4, 4, hH, hL, htok, evac_rope(Q, q_tok, 0.125), rate=1)
        fm_block("in_k", 4, 4, hH, hL, htok, evac_rope(K, k_tok, 1.0), rate=1)
        tm_block("in_v", 4, hH, hL, htok, evac_v, rate=1)

        SCO = tmp
        PT = Ring([sb(f"pt{i}", [128, 512], c=P1) for i in range(2)])
        oacc = {}
        att_tok = []
        g_mix, tg_mix = load_gain(A["attn_out_norm"][0], A["sgu_out_norm"][0])

        def attention1():
            for qt in range(4):
                obank, ot = side.take()
                den = small(8)
                prev = []
                n = 128 * (qt + 1)
                for h in range(8):
                    f, p0 = h // 2, 64 * (h % 2)
                    bank, bt = side.take()
                    t = mm(bank[:, 0:n], Q[p0:p0 + 64, f, 128 * qt:128 * qt + 128], K[p0:p0 + 64, f, 0:n], True, True, q_tok[f], k_tok[f], bt, sig=True)
                    s, s_t = SCO.take()
                    m = small(2)
                    t = ttr(s[:, 0:n], bank[:, 0:n], CST[:, C_BT + 128 * (3 - qt):C_BT + 512], -3e38, ALU.add, ALU.max, m[:, 0:1], t, s_t)
                    side.give(bank, t)
                    t = ts(dve, m[:, 1:2], m[:, 0:1], -1.0, None, ALU.mult, None, t)
                    t = fn_act(s[:, 0:n], s[:, 0:n], ACT.Exp, t, bias=m[:, 1:2], accum_out=den[:, h:h + 1])
                    td = t
                    prev.append((s, t, h))
                    yield
                    if h % 2 == 1:
                        for s, t, hh in prev:
                            bank, bt = side.take()
                            for k in range(qt + 1):
                                t = tr(bank[:, 128 * k:128 * k + 128], s[:, 128 * k:128 * k + 128], 128, t, bt, sig=k == qt)
                            SCO.give(s, t)
                            pt, pt_t = PT.take()
                            if hh % 2:
                                t = copy_act(pt[:, 0:n], bank[:, 0:n], t, pt_t)
                            else:
                                t = copy_dve(pt[:, 0:n], bank[:, 0:n], t, pt_t)
                            side.give(bank, t)
                            for k in range(qt + 1):
                                t = mm(obank[:, 64 * hh:64 * hh + 64], pt[:, 128 * k:128 * k + 128], V[:, k, 64 * hh:64 * hh + 64], k == 0, k == qt, t, v_tok[k], ot, sig=k == qt)
                            PT.give(pt, t)
                        prev = []
                        yield
                r = recip(den, den, td)
                o = MIX[:, qt, 0:512]
                t = tt(dve, o.rearrange("p (h d) -> p h d", h=8), obank[:, :].rearrange("p (h d) -> p h d", h=8), bc(den, 64), ALU.mult, r, t, wt_tok)
                side.give(obank, t)
                ss = small(1)
                t = square_sum(ss, o, t)
                t = rstd(ss, ss, 512, RMS_EPS, t)
                t = stt(o, o, ss, g_mix[0][:, 0:512], ALU.mult, ALU.mult, t, tg_mix)
                att_tok.append(t)
                yield

        wt_tok = []

        def spatial_weights():
            w = MIX[:, 0, :].rearrange("p (g j) -> p g j", g=8)
            t = tt(pool, w, w, mid(CST[:, C_TB:C_TB + 128], 8), ALU.mult, t_p1, t_cst)
            for b in range(2):
                bank, bt = side.take()
                for g in range(4):
                    t2 = tr(bank[:, 128 * g:128 * g + 128], w[:, 4 * b + g, :], 128, t, bt, sig=g == 3)
                t2 = copy_act(WT[:, 4 * b:4 * b + 4, :].rearrange("p g i -> p (g i)"), bank[:, :], t2)
                side.give(bank, t2)
                wt_tok.append(t2)
            yield

        bg.append(spatial_weights())
        drain()
        bg.append(attention1())

        vs_tok, u_tok = {}, {}

        def ln_tile(t_, t0):
            v = VS[:, t_, :]
            st6, mv = small(6), small(2)
            t = dve.do(lambda e: e.bn_stats(st6, v), t0)
            t = dve.do(lambda e: e.bn_aggr(mv, st6), t)
            t = rstd(mv[:, 1:2], mv[:, 1:2], 1.0, LN_EPS, t)
            t = ts(dve, v, v, mv[:, 0:1], mv[:, 1:2], ALU.subtract, ALU.mult, t)
            t = tt(pool, v, v, g_ln[0][:, 0:512], ALU.mult, t, tg_ln)
            t = tt(pool, v, v, g_ln[0][:, 512:1024], ALU.add, t)
            vs_tok[t_] = t

        def evac_vs(t_, bank, t):
            t = act.do(lambda e: e.activation(VS[:, t_, :], bank[:, :], ACT.Gelu), t)
            ln_tile(t_, t)
            return t

        def evac_u(t_, bank, t):
            u_tok[t_] = act.do(lambda e: e.activation(MIX[:, t_, 512:1024], bank[:, :], ACT.Gelu), t, wt_tok)
            return u_tok[t_]

        tm_block("in_vs", 4, hH, hL, htok, evac_vs, rate=5)
        in_done = tm_block("in_u", 4, hH, hL, htok, evac_u, rate=5)

        sgu_tok = []

        def spatial():
            for g in range(8):
                bank, bt = side.take()
                t = mm(bank[:, 0:256].rearrange("p (n c) -> p n c", n=4), WT[:, g, :], VS[:, :, 64 * g:64 * g + 64], True, True,
                       [vs_tok[i] for i in range(4)], wt_tok, bt, sig=True)
                u = MIX[:, :, 512 + 64 * g:576 + 64 * g]
                t = stt(u, bank[:, 0:256].rearrange("p (n c) -> p n c", n=4), SB_[:, g:g + 1], u, ALU.add, ALU.mult, t, [u_tok[i] for i in range(4)], t_p1)
                side.give(bank, t)
                if g % 2:
                    yield
            for t_ in range(4):
                ss = small(1)
                o = MIX[:, t_, 512:1024]
                t2 = square_sum(ss, o, t)
                t2 = rstd(ss, ss, 512, RMS_EPS, t2)
                sgu_tok.append(stt(o, o, ss, g_mix[0][:, 512:1024], ALU.mult, ALU.mult, t2, tg_mix))
                yield

        drain()
        bg.append(spatial())
        drain()
        gains.give(g_mix, [sgu_tok, att_tok])
        gains.give(g_ln, [vs_tok[i] for i in range(4)])
        dump("mix", MIX[:, :, :], sgu_tok, att_tok)

        mtk = []
        for t_ in range(4):
            d, _ = turn(MIX[:, t_, :], 8, hH, hL, 128 * t_, in_done, sgu_tok[t_], att_tok[t_])
            mtk += d
        turned = _
        P1.close()

        def project(P, tag, nu, a_h, a_l, a_tok, Y, yfree, tail_fn, add=False, tail=True, rate=0):
            ytok = {}

            def evac(h):
                def f(t_, bank, t):
                    y = Y[:, t_, 512 * h:512 * h + 512]
                    if add:
                        r = tt(dve, y, bank[:, :], y, ALU.add, t, yfree)
                    else:
                        r = copy_act(y, bank[:, :], t, yfree)
                    ytok.setdefault(t_, []).append(r)
                    if h == 1 and tail_fn:
                        pend.append((t_, list(ytok[t_])))
                    return r
                return f

            pend = []
            tm_block(tag, nu, a_h, a_l, a_tok, evac(0), rate=rate)
            if not tail:
                last = tm_block(tag, nu, a_h, a_l, a_tok, evac(1), rate=rate)
                return last, ytok
            fn = evac(1)

            def evac_tail(t_, bank, t):
                r = fn(t_, bank, t)
                while len(pend) > 1:
                    a = pend.pop(0)
                    tail_fn(*a, t)
                return r
            last = tm_block(tag, nu, a_h, a_l, a_tok, evac_tail, tail=True)
            while pend:
                a = pend.pop(0)
                tail_fn(*a, last)
            return last, ytok

        def post_add(t_, tok, y, gain, g_tok):
            ss = small(1)
            t = square_sum(ss, y, tok)
            t = rstd(ss, ss, D, RMS_EPS, t)
            t = stt(y, y, ss, gain[:, :], ALU.mult, ALU.mult, t, g_tok)
            return tt(dve, X[:, t_, :], X[:, t_, :], y, ALU.add, t)

        P2 = ExitStack()
        Y = sb("Y", [128, 4, D], c=P2)
        aH = sb("aH", [128, 8, S], F32R, c=P2)
        aL = sb("aL", [128, 8, S], F32R, c=P2)
        SG = Ring([sb(f"sg{i}", [128, 512], c=P2) for i in range(2)])
        g_post, tg_post = load_gain(A["post_mix_norm"][0])
        g_ffn, tg_ffn = load_gain(A["pre_ffn_norm"][0])
        htok = []
        xtok = {}

        def tail1(t_, tok, mm_tok):
            xtok[t_] = post_add(t_, tok, Y[:, t_, :], g_post[0], tg_post)
            d, l = norm_turn(X[:, t_, :], g_ffn[0], tg_ffn, 128 * t_, hH, hL, mm_tok, xtok[t_])
            htok.extend(d)
            xtok[t_] = l

        project(P2, "wout", 4, hH, hL, mtk, Y, turned, tail1)
        gains.give(g_post, xtok[3])
        gains.give(g_ffn, xtok[3])
        dump("x1", X[:, :, :], [xtok[i] for i in range(4)])

        g_pf, tg_pf = load_gain(A["post_ffn_norm"][0])
        g_nm, tg_nm = load_gain(A["norm_mix_2"][0])
        a_free = [turned]

        def split_evac(dst_f, src, t):
            th, tl = split_from(src, aH[:, dst_f, :], aL[:, dst_f, :], t)
            return th, tl

        for c, (b0, nb) in enumerate(FF1):
            atok = []
            for b in range(nb):
                gate = {}

                def evac_gu(f, bank, t, b=b):
                    if f < 2:
                        s, st = SG.take()
                        r = fn_act(s[:, :], bank[:, :], ACT.Sigmoid, t, st, turned)
                        r = tt(dve, s[:, :], s[:, :], bank[:, :], ALU.mult, r)
                        gate[f] = (s, r)
                        return r
                    s, r = gate[f - 2]
                    r1 = tt(dve, s[:, :], s[:, :], bank[:, :], ALU.mult, r, t)
                    th, tl = split_from(s[:, :], aH[:, 2 * b + f - 2, :], aL[:, 2 * b + f - 2, :], r1, a_free)
                    SG.give(s, [th, tl])
                    atok.extend([th, tl])
                    return r1

                hdone = fm_block("gu", 4, 4, hH, hL, htok, evac_gu)
            if c < len(FF1) - 1:
                last, yt = project(P2, "down", nb, aH, aL, atok, Y, [xtok[i] for i in range(4)], None, add=c > 0, tail=False)
                a_free = [last]
                yfree = [yt[i] for i in range(4)]
            else:
                htok = []

                def tail2(t_, tok, mm_tok):
                    xtok[t_] = post_add(t_, tok, Y[:, t_, :], g_pf[0], tg_pf)
                    d, l = norm_turn(X[:, t_, :], g_nm[0], tg_nm, 128 * t_, hH, hL, hdone, xtok[t_])
                    htok.extend(d)
                    xtok[t_] = l
                last, yt = project(P2, "down", nb, aH, aL, atok, Y, yfree, tail2, add=True)
        gains.give(g_pf, xtok[3])
        gains.give(g_nm, xtok[3])
        dump("x2", X[:, :, :], [xtok[i] for i in range(4)])
        p2_done = [last, htok, [xtok[i] for i in range(4)]]
        P2.close()

        PA = ExitStack()
        XS0 = sb("XS0", [128, 4, 512], c=PA)
        BF0 = sb("BF0", [128, 2, 512], c=PA)
        CF0 = sb("CF0", [128, 2, 512], c=PA)
        BT0 = sb("BT0", [128, 2, 4, 128], c=PA)
        KF = sb("KF", [128, 2, 512], c=PA)
        P3 = ExitStack()
        bt1_gain, bt1_free = gains.take()
        BT1 = bt1_gain[0][:, :].rearrange("p (a c n) -> p a c n", a=2, c=4)
        xs_buf = [XS0, X[:, 0:2, :].rearrange("p a (b c) -> p (a b) c", b=2)]
        bf_buf = [BF0, X[:, 2, :].rearrange("p (b c) -> p b c", b=2)]
        cf_buf = [CF0, X[:, 3, :].rearrange("p (b c) -> p b c", b=2)]
        bt_buf = [BT0, BT1]
        buf_free = [[p2_done], [p2_done]]
        ZS = sb("ZS", [128, 4, 512], c=P3)
        YS = sb("YS", [128, 4, 512], c=P3)
        tmp = Ring([sb(f"tb{i}", [128, 512], c=P3) for i in range(NTB)])
        for i in range(NTB):
            tmp.free[i] = (tmp.free[i][0], p2_done)
        CBU = sb("CBU", [128, 4, 128], c=P3)
        CBL = sb("CBL", [128, 4, 128], c=P3)
        PREV = sb("PREV", [128, 2, 3, 256], c=P3)
        DT = sb("DT", [128, 4, 64], c=P3)
        CS = sb("CS", [128, 4, 64], c=P3)
        ECS = sb("ECS", [128, 4, 64], c=P3)
        WST = sb("WST", [128, 4, 64], c=P3)
        CDEC = sb("CDEC", [128, 4, 64], c=P3)
        PAR = sb("PAR", [128, 160], c=P3)
        CW = sb("CW", [128, 192], c=P3)
        DTB, ALOG, DSK = PAR[:, 0:64], PAR[:, 64:128], PAR[:, 128:160]

        l_xs = line("l_xs")
        x_saved = l_xs.go(act, lambda e: e.dma_start(scr["x"], X[:, :, :].rearrange("p t d -> p (t d)")), [xtok[i] for i in range(4)])
        buf_free[1] += [x_saved, bt1_free]
        l_par = line("l_par")

        def ldp(o, i, *tok):
            return l_par.go(act, lambda e: e.dma_start(o, i), *tok)

        cr, cr_t = tmp.take()
        wrows = A["conv_w_2"][0].rearrange("k (t p) -> (k t) p", p=128)
        ldp(cr[:, 0:128], wrows[0:128, :], cr_t)
        ldp(cr[0:32, 128:256], wrows[128:160, :])
        ldp(cr[32:64, 128:256], A["conv_b_2"][0].rearrange("(t p) -> t p", p=128))
        ldp(DTB, A["dt_bias_2"][0].rearrange("a h -> (a h)").partition_broadcast(128), p2_done)
        ldp(ALOG, A["a_log_2"][0].rearrange("a h -> (a h)").partition_broadcast(128))
        t_par = ldp(DSK, A["d_skip_2"][0].partition_broadcast(128))
        bank, bt = side.take()
        tr(bank[:, 0:128], cr[:, 0:128], 128, t_par, bt)
        t = tr(bank[:, 128:192], cr[0:64, 128:256], 64, sig=True)
        cw_tok = copy_act(CW[:, :], bank[:, 0:192], t, p2_done, scale=0.5)
        side.give(bank, cw_tok)
        tmp.give(cr, t)

        bank, bt = side.take()
        us = []
        for u in range(4):
            look_ahead()
            us.append(take_unit("dt"))
        for t_ in range(4):
            for u in range(4):
                i, wh, wl, wt = us[u]
                for kk in range(2):
                    tk = tm_mms(bank[:, 64 * t_:64 * t_ + 64], 4, 4, u, kk, (0, 64), wh, wl, hH, hL, t_, wt, htok, bt, sig=(t_ == 3 and kk == 1))
                if t_ == 3:
                    release(i, tk)
        dt_bank, dt_t = bank, tk

        dts = {}

        def steps_dt():
            c4 = lambda ap: ap[:, 0:256].rearrange("p (c h) -> p c h", c=4)
            x1, a0 = tmp.take()
            e1, a1 = tmp.take()
            u1, a2 = tmp.take()
            x_, e_, u_ = c4(x1), c4(e1), c4(u1)
            t = tt(dve, x_, c4(dt_bank), mid(DTB, 4), ALU.add, dt_t, a0, t_par)
            side.give(dt_bank, t)
            t2 = fn_act(e_, x_, ACT.Abs, t, a1)
            t2 = fn_act(e_, e_, ACT.Exp, t2, scale=-1.0)
            t3 = ts(dve, u_, e_, 1.0, None, ALU.add, None, t2, a2)
            t4 = fn_act(DT[:, :, :], u_, ACT.Ln, t3, p2_done)
            tx = ts(dve, x_, x_, 0.0, None, ALU.max, None, t2)
            yield
            d1, a3 = tmp.take()
            d_ = c4(d1)
            t5 = ts(dve, d_, u_, 1.0, None, ALU.subtract, None, t3, a3)
            t5 = tt(dve, d_, e_, d_, ALU.subtract, t5)
            t6 = recip(u_, u_, t4, t5)
            t6 = tt(dve, d_, d_, u_, ALU.mult, t6)
            t6 = tt(dve, d_, d_, x_, ALU.add, t6, tx)
            tdt = tt(dve, DT[:, :, :], DT[:, :, :], d_, ALU.add, t6, t4)
            yield
            ta = fn_act(ALOG, ALOG, ACT.Exp, t_par)
            ta = ts(dve, ALOG, ALOG, -1.0, None, ALU.mult, None, ta)
            ta = tt(dve, x_, DT[:, :, :], mid(ALOG, 4), ALU.mult, ta, tdt)
            sbuf = None
            f1, b1 = tmp.take()
            f2, b2 = tmp.take()
            ft = []
            for d, (dst, dstt) in enumerate(((f1, b1), (f2, b2))):
                bank, bt = side.take()
                tri = CST[:, (C_TF, C_TB)[d]:(C_TF, C_TB)[d] + 128]
                for c in range(4):
                    t = mm(bank[0:32, 128 * c:128 * c + 128], x_[:, c, 32 * d:32 * d + 32], tri, True, True, ta, bt, sig=c == 3)
                t = copy_act(dst[0:32, :], bank[0:32, :], t, dstt)
                side.give(bank, t)
                ft.append(t)
                l_cs.go(act, lambda e, dst=dst, d=d: e.dma_start(scr["cs"][:, 512 * d:512 * d + 512], dst[0:32, :]), t)
            dts["cs"] = (l_cs.sem, l_cs.n)
            yield
            bank, bt = side.take()
            for d, dst in enumerate((f1, f2)):
                for c in range(4):
                    t = tr(bank[:, 64 * c + 32 * d:64 * c + 32 * d + 32], dst[0:32, 128 * c:128 * c + 128], 32, ft[d], bt, sig=c == 3)
            tcs = copy_act(CS[:, :, :], c4(bank), t)
            side.give(bank, tcs)
            bank, bt = side.take()
            for d in range(2):
                t = mm(bank[:, 128 * d:128 * d + 128].rearrange("p (c h) -> p c h", c=4), CST[:, (C_LL, C_FF)[d]:(C_LL, C_FF)[d] + 128],
                       CS[:, :, 32 * d:32 * d + 32], True, True, tcs, bt, sig=True)
            tot = bank[:, 0:256].rearrange("p (d c h) -> p d c h", d=2, c=4)
            td = []
            for d in range(2):
                v = lambda ap: ap[:, :, 32 * d:32 * d + 32]
                t1 = copy_act(v(CDEC), tot[:, d], t)
                td.append(tt(dve, v(WST), v(CDEC), v(CS), ALU.subtract, t1, tcs))
            side.give(bank, t1)
            td.append(fn_act(CDEC[:, :, :], CDEC[:, :, :], ACT.Exp, td))
            t1 = fn_act(WST[:, :, :], WST[:, :, :], ACT.Exp, td)
            t1 = tt(dve, WST[:, :, :], WST[:, :, :], DT[:, :, :], ALU.mult, t1, tdt)
            t2 = fn_act(ECS[:, :, :], CS[:, :, :], ACT.Exp, tcs)
            for b in (x1, e1, u1, d1):
                tmp.give(b, [ta, t6, tdt, t])
            tmp.give(f1, [t, dts["cs"]])
            tmp.give(f2, [t, dts["cs"]])
            dts["small"] = [t1, t2, tcs, td, tdt]
            yield

        l_cs = line("l_cs")
        bg.append(steps_dt())

        def conv(bank, t, ct, dst, dst_free):
            w = lambda k: CW[:, 32 * k + ct:32 * k + ct + 1]
            u, ut = tmp.take()
            t = fn_act(u[:, :], bank[:, :], ACT.Identity, t, ut, cw_tok, scale=w(2), bias=CW[:, 160 + ct:161 + ct])
            t = stt(u[:, 2:512], bank[:, 0:510], w(0), u[:, 2:512], ALU.mult, ALU.add, t)
            t = stt(u[:, 1:512], bank[:, 0:511], w(1), u[:, 1:512], ALU.mult, ALU.add, t)
            t = stt(u[:, 0:511], bank[:, 1:512], w(3), u[:, 0:511], ALU.mult, ALU.add, t)
            tb = stt(u[:, 0:510], bank[:, 2:512], w(4), u[:, 0:510], ALU.mult, ALU.add, t)
            h, ht = tmp.take()
            t = fn_act(h[:, :], u[:, :], ACT.Tanh, tb, ht)
            t = stt(dst, h[:, :], 1.0, u[:, :], ALU.add, ALU.mult, t, dst_free)
            tmp.give(u, t)
            tmp.give(h, t)
            return tb, t

        bf_tok, cf_tok, bt_tok, xs_tok, zs_tok = {}, {}, {}, {}, {}
        zs_free = [p2_done]
        ys_free = [p2_done]

        def turn_b(j, f):
            bank, bt = side.take()
            for c in range(4):
                t = tr(bank[:, 128 * c:128 * c + 128], bf_buf[j % 2][:, f, 128 * c:128 * c + 128], 128, bf_tok[j, f], bt, sig=c == 3)
            t = copy_act(bt_buf[j % 2][:, f, :, :].rearrange("p c n -> p (c n)"), bank[:, :], t, buf_free[j % 2])
            side.give(bank, t)
            bt_tok[j, f] = t
            yield

        def turn_xs(j, f, src, t0):
            bank, bt = side.take()
            for c in range(4):
                t = tr(bank[:, 128 * c:128 * c + 128], src[:, 128 * c:128 * c + 128], 128, t0, bt, sig=c == 3)
            tmp.give(src, t)
            t = copy_act(xs_buf[j % 2][:, :, 128 * f:128 * f + 128], bank[:, :].rearrange("p (c n) -> p c n", c=4), t, buf_free[j % 2])
            side.give(bank, t)
            xs_tok[j, f] = t
            yield

        def evac_bc(j):
            def evac(f, bank, t):
                if f < 2:
                    tb, t = conv(bank, t, 16 + 2 * j + f, bf_buf[j % 2][:, f, :], buf_free[j % 2])
                    bf_tok[j, f] = t
                    bg.appendleft(turn_b(j, f))
                else:
                    tb, t = conv(bank, t, 24 + 2 * j + f - 2, cf_buf[j % 2][:, f - 2, :], buf_free[j % 2])
                    cf_tok[j, f - 2] = t
                return tb
            return evac

        def evac_xs(j):
            def evac(f, bank, t):
                o, ot = tmp.take()
                tb, t = conv(bank, t, 4 * j + f, o[:, :], ot)
                bg.appendleft(turn_xs(j, f, o, t))
                return tb
            return evac

        def evac_z(j):
            def evac(t_, bank, t):
                z = ZS[:, t_, :]
                t = copy_act(z, bank[:, :], t, zs_free, scale=0.5)
                h, ht = tmp.take()
                t2 = fn_act(h[:, :], z, ACT.Tanh, t, ht)
                t2 = stt(z, h[:, :], 1.0, z, ALU.add, ALU.mult, t2)
                tmp.give(h, t2)
                zs_tok[j, t_] = t2
                return t
            return evac

        r64 = lambda ap: ap.rearrange("p (r d) -> p r d", d=64)
        l_cb = [line(f"l_cb{i}") for i in range(2)]
        cb_n = [0]
        prev_free = [p2_done]
        cb_free = [p2_done]
        l_ys = [line(f"l_ys{f}") for f in range(4)]
        gn = {}

        def ssd(j):
            XSb, BFb, CFb, BTb = xs_buf[j % 2], bf_buf[j % 2], cf_buf[j % 2], bt_buf[j % 2]
            xt = [xs_tok[j, f] for f in range(4)]
            small_t = dts["small"]
            gn[j] = load_gain(A["ssd_norm_2"][0][512 * j:512 * j + 512])
            readers = []
            yt = {}
            for gg in range(2):
                g = 2 * j + gg
                co = slice(256 * gg, 256 * gg + 256)
                bank, bt = side.take()
                for c in range(4):
                    t = mm(bank[:, 128 * c:128 * c + 128], BFb[:, gg, 128 * c:128 * c + 128], CFb[:, gg, 128 * c:128 * c + 128], True, True,
                           bf_tok[j, gg], cf_tok[j, gg], bt, sig=c == 3)
                b4 = bank[:, :].rearrange("p (c l) -> p c l", c=4)
                tu = tt(dve, CBU[:, :, :], b4, mid(CST[:, C_TF:C_TF + 128], 4), ALU.mult, t, cb_free)
                tl = tt(dve, CBL[:, :, :], b4, mid(CST[:, C_TB:C_TB + 128], 4), ALU.mult, t, cb_free)
                side.give(bank, [tu, tl])
                yield
                pv = {}
                for d in range(2):
                    for n in range(3):
                        c = n if d == 0 else 3 - n
                        hs = slice(32 * d + 4 * g, 32 * d + 4 * g + 4)
                        xw, xwt = tmp.take()
                        t = tt(pool, r64(xw[:, 0:256]), r64(XSb[:, c, co]), bc(WST[:, c, hs], 64), ALU.mult, xwt, xt, small_t)
                        bank, bt = side.take()
                        t = mm(bank[:, 0:256], BTb[:, gg, c, :], xw[:, 0:256], True, True, t, bt, bt_tok[j, gg], sig=True)
                        tmp.give(xw, t)
                        if n == 0:
                            t = copy_act(PREV[:, d, 0, :], bank[:, 0:256], t, prev_free)
                        else:
                            pd, pdt = tmp.take()
                            t2 = tt(pool, r64(pd[:, 0:256]), r64(PREV[:, d, n - 1, :]), bc(CDEC[:, c, hs], 64), ALU.mult, pv[d, n - 1], pdt, small_t)
                            t = tt(dve, PREV[:, d, n, :], bank[:, 0:256], pd[:, 0:256], ALU.add, t, t2, prev_free)
                            tmp.give(pd, t)
                        side.give(bank, t)
                        pv[d, n] = t
                        if n % 2:
                            yield
                yb = [side.take(), side.take()]
                for r in range(4):
                    h = 4 * g + r
                    cb, cbt = hn_ring.take()
                    ln = l_cb[cb_n[0] % 2]
                    cb_n[0] += 1
                    tc = ln.go(CSQ, lambda e, cb=cb, h=h: e.dma_start(cb[:, :], scr["cs"][h].partition_broadcast(128)), cbt, dts["cs"])
                    c4 = lambda ap: ap.rearrange("p (c l) -> p c l", c=4)
                    a, at = tmp.take()
                    b, bt_ = tmp.take()
                    t1 = tt(pool, c4(a[:, :]), c4(cb[:, 0:512]), bc(CS[:, :, h], 128), ALU.subtract, tc, at, small_t)
                    t2 = tt(dve, c4(b[:, :]), c4(cb[:, 512:1024]), bc(CS[:, :, 32 + h], 128), ALU.subtract, tc, bt_, small_t)
                    hn_ring.give(cb, [t1, t2])
                    t = tt(dve, b[:, :], a[:, :], b[:, :], ALU.min, t1, t2)
                    te = fn_act(b[:, :], b[:, :], ACT.Exp, t)
                    w, wt_ = tmp.take()
                    t3 = tt(pool, c4(a[:, :]), CBL[:, :, :], bc(DT[:, :, 32 + h], 128), ALU.mult, tl, t)
                    t4 = tt(dve, c4(w[:, :]), CBU[:, :, :], bc(DT[:, :, h], 128), ALU.mult, tu, wt_)
                    t4 = tt(dve, w[:, :], w[:, :], a[:, :], ALU.add, t4, t3)
                    t4 = tt(dve, w[:, :], w[:, :], b[:, :], ALU.mult, t4, te)
                    tmp.give(a, t4)
                    tmp.give(b, t4)
                    for c in range(4):
                        yo = yb[c // 2][0][:, 256 * (c % 2) + 64 * r:256 * (c % 2) + 64 * r + 64]
                        t = mm(yo, w[:, 128 * c:128 * c + 128], XSb[:, c, 256 * gg + 64 * r:256 * gg + 64 * r + 64], True, True, t4, xt, yb[c // 2][1], sig=c == 3)
                    tmp.give(w, t)
                    yield
                cb_free[:] = [t4]
                t_diag = t
                first = {}
                lastp = {}
                for d in range(2):
                    for n in range(3):
                        c = n + 1 if d == 0 else 2 - n
                        hs = slice(32 * d + 4 * g, 32 * d + 4 * g + 4)
                        bank, bt = side.take()
                        t = mm(bank[:, 0:256], CFb[:, gg, 128 * c:128 * c + 128], PREV[:, d, n, :], True, True, pv[d, n], bt, sig=True)
                        o, ot = tmp.take()
                        t2 = tt(dve, r64(o[:, 0:256]), r64(bank[:, 0:256]), bc(ECS[:, c, hs], 64), ALU.mult, t, ot)
                        side.give(bank, t2)
                        y = YS[:, c, co]
                        if c not in first:
                            t2 = tt(dve, y, yb[c // 2][0][:, 256 * (c % 2):256 * (c % 2) + 256], o[:, 0:256], ALU.add, t2, t_diag, ys_free)
                            first[c] = t2
                        else:
                            t2 = tt(pool, y, y, o[:, 0:256], ALU.add, t2, first[c])
                        lastp[c] = t2
                        tmp.give(o, t2)
                        if n % 2:
                            yield
                prev_free[:] = [t]
                side.give(yb[0][0], [first[c] for c in range(4)])
                side.give(yb[1][0], [first[c] for c in range(4)])
                while (j, 3) not in zs_tok:
                    yield
                rs = small(4)
                for c in range(4):
                    o, ot = tmp.take()
                    y = YS[:, c, co]
                    t = tt(pool, r64(o[:, 0:256]), r64(XSb[:, c, co]), bc(DSK[:, 4 * g:4 * g + 4], 64), ALU.mult, ot, xt)
                    t = tt(pool, y, y, o[:, 0:256], ALU.add, t, lastp[c])
                    readers.append(t)
                    t = tt(dve, y, y, ZS[:, c, co], ALU.mult, t, zs_tok[j, c])
                    t = fn_act(o[:, 0:256], y, ACT.Square, t, accum_out=rs[:, c:c + 1])
                    tmp.give(o, t)
                    yt[gg, c] = t
                t = rstd(rs, rs, 256, RMS_EPS, t)
                for c in range(4):
                    y = YS[:, c, co]
                    yt[gg, c] = stt(y, y, rs[:, c:c + 1], gn[j][0][0][:, co], ALU.mult, ALU.mult, t, gn[j][1])
                yield
            zs_free[:] = [yt[1, 3]]
            gains.give(gn[j][0], [yt[1, 3]])
            buf_free[j % 2][:] = [readers, t_diag, prev_free[0]]
            for f in range(4):
                bank, bt = side.take()
                for c in range(4):
                    t = tr(bank[:, 128 * c:128 * c + 128], YS[:, c, 128 * f:128 * f + 128], 128, yt[f // 2, c], bt, sig=c == 3)
                o, ot = tmp.take()
                t2 = copy_act(o[:, :], bank[:, :], t, ot)
                side.give(bank, t2)
                td = l_ys[f].go(CSQ, lambda e, o=o, f=f: e.dma_start(scr["ys"][128 * (4 * j + f):128 * (4 * j + f) + 128, :], o[:, :]), t2)
                tmp.give(o, td)
                yield
            ys_free[:] = [t]
            if j == 3:
                ys_done.extend([(ln.sem, ln.n) for ln in l_ys])

        for j in range(4):
            fm_block("bc", 4, 4, hH, hL, htok, evac_bc(j), rate=RA[0])
            fm_block("xs", 4, 4, hH, hL, htok, evac_xs(j), rate=RA[1])
            drain()
            bg.append(ssd(j))
            tm_block("z", 4, hH, hL, htok, evac_z(j), rate=RA[2])
        V2 = BT0[:, :, :, :].rearrange("p a c n -> p (a c n)").rearrange("p (t d) -> p t d", t=4)
        Q2 = [XS0[:, i, :] for i in range(4)] + [BF0[:, i, :] for i in range(2)] + [CF0[:, i, :] for i in range(2)]
        kf_tok, v2_tok, q2_tok = {}, {}, {}
        free0 = list(buf_free[0])

        banks = [main.take() for _ in range(4)]
        us = []
        for u in range(4):
            look_ahead()
            i, wh, wl, wt = take_unit("kv2")
            for f in range(2):
                for kk in range(2):
                    k = 2 * u + kk
                    w_h, w_l = wh[:, kk, 128 * f:128 * f + 128], wl[:, kk, 128 * f:128 * f + 128]
                    mm(banks[f][0][:, :], w_h, hH[:, k, :], k == 0, False, wt, htok, banks[f][1])
                    mm(banks[f][0][:, :], w_h, hL[:, k, :], False, False)
                    t = mm(banks[f][0][:, :], w_l, hH[:, k, :], False, k == 7, sig=k == 7)
                if u == 3:
                    kf_tok[f] = copy_act(KF[:, f, :], banks[f][0][:, :], t, p2_done)
                    main.give(banks[f][0], kf_tok[f])
            us.append((i, wh, wl, wt))
            pump(RA[3])
        for t_ in range(4):
            b = banks[2 + t_ // 2]
            for u in range(4):
                i, wh, wl, wt = us[u]
                for kk in range(2):
                    t = tm_mms(b[0][:, 256 * (t_ % 2):256 * (t_ % 2) + 256], 4, 4, u, kk, (256, 512), wh, wl, hH, hL, t_, wt, b[1], sig=(t_ == 3 and kk == 1))
                if t_ == 3:
                    release(i, t)
            if t_ % 2:
                r = copy_act(V2[:, t_ - 1:t_ + 1, :].rearrange("p t d -> p (t d)"), b[0][:, :], t, free0)
                v2_tok[t_ - 1] = v2_tok[t_] = r
                main.give(b[0], r)

        def evac_q2(j):
            def evac(f, bank, t):
                q2_tok[4 * j + f] = copy_act(Q2[4 * j + f], bank[:, :], t, free0, scale=0.125)
                return q2_tok[4 * j + f]
            return evac

        for j in range(2):
            fm_block("q2", 4, 4, hH, hL, htok, evac_q2(j), rate=RA[3])
        drain()
        P3.close()
        gains.give(bt1_gain, buf_free[1])

        ssd_done = [ys_free[0], buf_free[1], ys_done, zs_free[0]]
        SIGA = X[:, :, :].rearrange("p a (b c) -> p (a b) c", b=2)
        P4 = ExitStack()
        SIGB = sb("SIGB", [128, 8, 512], c=P4)
        P5 = ExitStack()
        ATT = [sb(f"ATT{i}", [128, D], c=P5) for i in range(2)]
        att_ring = Ring(ATT)
        SC2 = [sb(f"SC2{i}", [128, 4, 384], c=P5) for i in range(2)]
        sc_ring = Ring(SC2)
        BIAS = sb("BIAS", [128, 4, 384], c=P5)
        pt_ring = Ring([sb(f"PTb{i}", [128, 512], c=P5) for i in range(2)])
        SINK = sb("SINK", [128, 16], c=P5)
        for rg in (att_ring, sc_ring, pt_ring):
            for i in range(len(rg.free)):
                rg.free[i] = (rg.free[i][0], ssd_done)
        l_sink = line("l_sink")
        t_sink = l_sink.go(act, lambda e: e.dma_start(SINK[:, :], A["attn_sink_2"][0].partition_broadcast(128)), ssd_done)

        sg_tok = {}

        def evac_gate(j):
            def evac(f, bank, t):
                dst = (SIGA, SIGB)[j // 2][:, 4 * (j % 2) + f, :]
                t = fn_act(dst, bank[:, :], ACT.Tanh, t, ssd_done, scale=0.5)
                sg_tok[4 * j + f] = ts(pool, dst, dst, 0.5, 0.5, ALU.mult, ALU.add, t)
                return t
            return evac

        at_tok = []
        bias_free = [ssd_done]
        gates_mm = []

        def attention2():
            for kv in range(4):
                tb = []
                for r in range(4):
                    h = 4 * kv + r
                    tb.append(ts(pool, BIAS[:, r, :], CST[:, C_NB:C_NB + 384], float(2.0 ** (-8.0 * (h + 1) / 16)), None, ALU.mult, None, bias_free))
                f0 = 4 * (kv // 2)
                p0 = 64 * (kv % 2)
                for qt in range(4):
                    lo_k, hi_k = max(0, qt - 1), min(3, qt + 1)
                    n = 128 * (hi_k - lo_k + 1)
                    bo = 128 * (lo_k - (qt - 1))
                    s, st = sc_ring.take()
                    m = small(16)
                    mx, nm, den, sk = m[:, 0:4], m[:, 4:8], m[:, 8:12], m[:, 12:16]
                    for r in range(4):
                        bank, bt = side.take()
                        t = mm(bank[:, 0:n], Q2[f0 + r][p0:p0 + 64, 128 * qt:128 * qt + 128], KF[p0:p0 + 64, kv // 2, 128 * lo_k:128 * lo_k + n], True, True,
                               q2_tok[f0 + r], kf_tok[kv // 2], bt, sig=True)
                        t = ttr(s[:, r, 0:n], bank[:, 0:n], BIAS[:, r, bo:bo + n], SINK[:, 4 * kv + r:4 * kv + r + 1], ALU.add, ALU.max, mx[:, r:r + 1], t, st, tb, t_sink)
                        side.give(bank, t)
                    if qt == 3:
                        bias_free[:] = [t]
                    t = ts(dve, nm, mx, -1.0, None, ALU.mult, None, t)
                    t5 = tt(dve, sk, SINK[:, 4 * kv:4 * kv + 4], mx, ALU.subtract, t)
                    te = [fn_act(s[:, r, 0:n], s[:, r, 0:n], ACT.Exp, t, bias=nm[:, r:r + 1], accum_out=den[:, r:r + 1]) for r in range(4)]
                    t5 = fn_act(sk, sk, ACT.Exp, t5)
                    t5 = tt(dve, den, den, sk, ALU.add, t5, te)
                    t5 = recip(den, den, t5)
                    yield
                    obank, ot = side.take()
                    for r in range(4):
                        bank, bt = side.take()
                        nk = n // 128
                        for k in range(nk):
                            t = tr(bank[:, 128 * k:128 * k + 128], s[:, r, 128 * k:128 * k + 128], 128, te[r], bt, sig=k == nk - 1)
                        pt, ptt = pt_ring.take()
                        t2 = (copy_act if r % 2 else copy_dve)(pt[:, 0:n], bank[:, 0:n], t, ptt)
                        side.give(bank, t2)
                        for k in range(nk):
                            t2 = mm(obank[:, 64 * r:64 * r + 64], pt[:, 128 * k:128 * k + 128], V2[:, lo_k + k, 64 * kv:64 * kv + 64], k == 0, k == nk - 1,
                                    t2, v2_tok[lo_k + k], ot, sig=k == nk - 1)
                        pt_ring.give(pt, t2)
                        if r == 1:
                            yield
                    sc_ring.give(s, t)
                    o, oft = att_ring.take()
                    t3 = tt(dve, r64(o[:, 0:256]), r64(obank[:, 0:256]), bc(den, 64), ALU.mult, t2, t5, oft)
                    side.give(obank, t3)
                    yield
                    bank, bt = side.take()
                    for k in range(2):
                        t = tr(bank[:, 128 * k:128 * k + 128], o[:, 128 * k:128 * k + 128], 128, t3, bt, sig=k == 1)
                    att_ring.give(o, t)
                    v = bank[:, 0:256].rearrange("p (k t) -> p k t", k=2)
                    th, tl = split_from(v, hH[:, 2 * kv:2 * kv + 2, 128 * qt:128 * qt + 128], hL[:, 2 * kv:2 * kv + 2, 128 * qt:128 * qt + 128], t, gates_mm)
                    side.give(bank, [th, tl])
                    at_tok.extend([th, tl])
                    yield

        for j in range(4):
            gt = fm_block("gate", 4, 4, hH, hL, htok, evac_gate(j), rate=0)
        gates_mm.append(gt)
        bg.append(attention2())

        mg_tok = {}
        for j in range(2):
            banks = [main.take() for _ in range(4)]
            for u in range(8):
                look_ahead()
                i, wh, wl, wt = take_unit("wssd")
                look_ahead()
                i2, yh, yl, ytk = take_unit("ys")
                for f in range(4):
                    for kk in range(2):
                        first, last = u == 0 and kk == 0, u == 7 and kk == 1
                        w_h, w_l = wh[:, kk, 128 * f:128 * f + 128], wl[:, kk, 128 * f:128 * f + 128]
                        mm(banks[f][0][:, :], w_h, yh[:, kk, :], first, False, wt, ytk, banks[f][1])
                        mm(banks[f][0][:, :], w_h, yl[:, kk, :], False, False)
                        t = mm(banks[f][0][:, :], w_l, yh[:, kk, :], False, last, sig=last or (f == 3 and kk == 1))
                    if last:
                        dst = SIGB[:, 4 * j + f, :]
                        mg_tok[4 * j + f] = tt(dve, dst, dst, banks[f][0][:, :], ALU.mult, t, sg_tok[8 + 4 * j + f])
                        main.give(banks[f][0], mg_tok[4 * j + f])
                release(i, t)
                release(i2, t)
                pump(RA[4])
        drain()
        P5.close()
        P6 = ExitStack()
        gH = sb("gH", [128, 8, S], F32R, c=P6)
        gL = sb("gL", [128, 8, S], F32R, c=P6)
        merged = []

        def evac_attn(j):
            def evac(f, bank, t):
                k = 4 * j + f
                a = SIGA[:, k, :]
                t1 = tt(dve, a, a, bank[:, :], ALU.mult, t, sg_tok[k])
                t2 = tt(pool, a, a, SIGB[:, k, :], ALU.add, t1, mg_tok[k])
                th, tl = split_from(a, gH[:, k, :], gL[:, k, :], t2, at_tok)
                merged.extend([th, tl])
                return t1
            return evac

        for j in range(2):
            at_mm = fm_block("wattn", 4, 4, hH, hL, at_tok, evac_attn(j))
        dump("merged", SIGA, merged)
        l_xr = line("l_xr")
        x_back = l_xr.go(act, lambda e: e.dma_start(X[:, :, :].rearrange("p t d -> p (t d)"), scr["x"]), merged, x_saved)
        g_nc, tg_nc = load_gain(A["norm_cross_2"][0])
        htok = []

        def tail3(t_, tok, mm_tok):
            d, xtok[t_] = norm_turn(X[:, t_, :], g_nc[0], tg_nc, 128 * t_, hH, hL, at_mm, tok)
            htok.extend(d)

        wout_mm, _ = project(P6, "wout2", 4, gH, gL, merged, X, x_back, tail3, add=True)
        gains.give(g_nc, xtok[3])
        dump("x3", X[:, :, :], [xtok[i] for i in range(4)])
        p6_done = [wout_mm, merged]
        P6.close()
        P4.close()
        PA.close()

        P7 = ExitStack()
        QX = sb("QX", [128, 4, S], c=P7)
        KM = sb("KM", [128, 4, 256], c=P7)
        VM = sb("VM", [128, 2, 512], c=P7)
        oH = sb("oH", [128, 4, S], F32R, c=P7)
        oL = sb("oL", [128, 4, S], F32R, c=P7)
        OX = [sb(f"OX{i}", [128, 512], c=P7) for i in range(2)]
        ox_ring = Ring(OX)
        px_ring = Ring([sb(f"PX{i}", [128, 4, 256], c=P7) for i in range(2)])
        pxt_ring = Ring([sb(f"PXT{i}", [128, 512], c=P7) for i in range(2)])
        for rg in (ox_ring, px_ring, pxt_ring):
            for i in range(len(rg.free)):
                rg.free[i] = (rg.free[i][0], p6_done)
        l_k2 = line("l_k2")
        l_k2.go(act, lambda e: e.dma_start(KM[:, :, :].rearrange("p f t -> p (f t)"), scr["km"]), p6_done, kv_saved)
        kv_back = l_k2.go(act, lambda e: e.dma_start(VM[:, :, :].rearrange("p f t -> p (f t)"), scr["vm"]), p6_done)
        qx_tok = {}

        def evac_qx(f, bank, t):
            qx_tok[f] = copy_act(QX[:, f, :], bank[:, :], t, p6_done, scale=float(128 ** -0.5))
            return qx_tok[f]

        qx_mm = fm_block("xq", 4, 4, hH, hL, htok, evac_qx)
        g_nf, tg_nf = load_gain(A["norm_ffn_2"][0])
        us = []
        for u in range(4):
            look_ahead()
            us.append(take_unit("xo"))
        ftok = []

        def cross(qt):
            pair = []
            m = small(12)
            mx, nm, den = m[:, 0:4], m[:, 4:8], m[:, 8:12]
            for b in range(2):
                bank, bt = side.take()
                for r in range(2):
                    h = 2 * b + r
                    t = mm(bank[:, 256 * r:256 * r + 256], QX[:, h, 128 * qt:128 * qt + 128], KM[:, h, :], True, True, qx_tok[h], kv_back, bt, sig=r == 1)
                t1 = dve.do(lambda e, bank=bank, b=b: e.tensor_reduce(mx[:, 2 * b:2 * b + 2], bank[:, :].rearrange("p (h k) -> p h k", h=2), AX.X, ALU.max), t)
                pair.append((bank, t1))
            t = ts(dve, nm, mx, -1.0, None, ALU.mult, None, t1)
            p, pt_ = px_ring.take()
            te = []
            for h in range(4):
                te.append(fn_act(p[:, h, :], pair[h // 2][0][:, 256 * (h % 2):256 * (h % 2) + 256], ACT.Exp, t, pt_, bias=nm[:, h:h + 1], accum_out=den[:, h:h + 1]))
            side.give(pair[0][0], te[1])
            side.give(pair[1][0], te[3])
            rt = recip(den, den, te)
            yield
            ob, obt = side.take()
            for b in range(2):
                bank, bt = side.take()
                for r in range(2):
                    for k in range(2):
                        h = 2 * b + r
                        c = 256 * r + 128 * k
                        t = tr(bank[:, c:c + 128], p[:, h, 128 * k:128 * k + 128], 128, te[h], bt, sig=r == 1 and k == 1)
                q, qt_ = pxt_ring.take()
                t2 = (copy_act, copy_dve)[b](q[:, :], bank[:, :], t, qt_)
                side.give(bank, t2)
                for r in range(2):
                    h = 2 * b + r
                    for k in range(2):
                        c = 256 * r + 128 * k
                        t3 = mm(ob[:, 128 * h:128 * h + 128], q[:, c:c + 128], VM[:, k, 128 * h:128 * h + 128], k == 0, k == 1, t2, obt, kv_back, sig=r == 1 and k == 1)
                pxt_ring.give(q, t3)
            px_ring.give(p, t)
            o, ot = ox_ring.take()
            t = tt(dve, o[:, :].rearrange("p (h d) -> p h d", h=4), ob[:, :].rearrange("p (h d) -> p h d", h=4), bc(den, 128), ALU.mult, t3, rt, ot)
            side.give(ob, t)
            yield
            d, last = turn(o, 4, oH, oL, 128 * qt, p6_done, t)
            ox_ring.give(o, last)
            yield
            ad = []
            for h in range(2):
                bank, bt = main.take()
                for u in range(2):
                    i, wh, wl, wt = us[2 * h + u]
                    for kk in range(2):
                        t = tm_mms(bank[:, :], 4, 2, u, kk, (0, 512), wh, wl, oH, oL, qt, wt, d, bt, sig=qt == 3)
                    if qt == 3:
                        release(i, t)
                x = X[:, qt, 512 * h:512 * h + 512]
                ad.append(tt(dve, x, bank[:, :], x, ALU.add, t, xtok[qt]))
                main.give(bank, ad[-1])
            yield
            dd, xtok[qt] = norm_turn(X[:, qt, :], g_nf[0], tg_nf, 128 * qt, hH, hL, qx_mm, ad)
            ftok.extend(dd)

        def together(gens):
            gens = list(gens)
            live = []
            while gens or live:
                if gens:
                    live.append(gens.pop(0))
                for g in list(live):
                    try:
                        next(g)
                    except StopIteration:
                        live.remove(g)

        together(cross(qt) for qt in range(4))
        gains.give(g_nf, xtok[3])
        dump("x4", X[:, :, :], [xtok[i] for i in range(4)])
        p7_done = [ftok, [xtok[i] for i in range(4)]]
        P7.close()

        P8 = ExitStack()
        fH = sb("fH", [128, 8, S], F32R, c=P8)
        fL = sb("fL", [128, 8, S], F32R, c=P8)
        rl = Ring([sb(f"rl{i}", [128, 512], c=P8) for i in range(3)])
        for i in range(3):
            rl.free[i] = (rl.free[i][0], p7_done)
        g_fi, tg_fi = load_gain(A["norm_final_2"])
        f_free = [p7_done]
        xfree = [xtok[i] for i in range(4)]
        l_out = line("l_out")

        def tail4(t_, tok, mm_tok):
            ss = small(1)
            x = X[:, t_, :]
            t = square_sum(ss, x, tok)
            t = rstd(ss, ss, D, RMS_EPS, t)
            t = stt(x, x, ss, g_fi[0][:, :], ALU.mult, ALU.mult, t, tg_fi)
            l_out.go(sp, lambda e, t_=t_: e.dma_start(out[0, 128 * t_:128 * t_ + 128, :], X[:, t_, :]), t)

        for fc in range(NFF2):
            atok = []
            for b in range(2):
                def evac_up(f, bank, t, b=b):
                    s, st = rl.take()
                    tr1 = fn_act(s[:, :], bank[:, :], ACT.Relu, t, st)
                    r = tt(dve, s[:, :], s[:, :], bank[:, :], ALU.mult, tr1)
                    th, tl = split_from(s[:, :], fH[:, 4 * b + f, :], fL[:, 4 * b + f, :], r, f_free)
                    rl.give(s, [th, tl])
                    atok.extend([th, tl])
                    return r
                fm_block("up2", 4, 4, hH, hL, ftok, evac_up)
            if fc < NFF2 - 1:
                last, yt = project(P8, "down2", 4, fH, fL, atok, X, xfree, None, add=True, tail=False)
                f_free = [last]
                xfree = [yt[i] for i in range(4)]
            else:
                last, yt = project(P8, "down2", 4, fH, fL, atok, X, xfree, tail4, add=True)
        P8.close()
        sp.wait((l_out.sem, l_out.n), *ys_done, (l_cs.sem, l_cs.n), (l_kv.sem, l_kv.n), (l_xs.sem, l_xs.n))
        assert st_["use"] == len(units), (st_, len(units))

        block = ctx.enter_context(nc.Block())

        @block.sync
        def _(e):
            sp.emit(e)

        @block.gpsimd
        def _(e):
            pool.emit(e)

        @block.scalar
        def _(e):
            act.emit(e)

        @block.vector
        def _(e):
            dve.emit(e)

        @block.tensor
        def _(e):
            pe.emit(e)


_INS = ['x', 'positions', 'pre_mix_norm', 'w_in', 'sgu_ln_gain', 'sgu_ln_bias', 'sgu_w_spatial', 'sgu_b_spatial', 'attn_out_norm', 'sgu_out_norm', 'w_out', 'post_mix_norm', 'pre_ffn_norm', 'w_gate', 'w_up', 'w_down', 'post_ffn_norm', 'mem_2', 'norm_mix_2', 'w_in_2', 'attn_sink_2', 'conv_w_2', 'conv_b_2', 'dt_bias_2', 'a_log_2', 'd_skip_2', 'ssd_norm_2', 'w_attn_branch_2', 'w_ssd_branch_2', 'w_out_2', 'norm_cross_2', 'norm_mem_2', 'w_xq_2', 'w_xkv_2', 'w_xo_2', 'norm_ffn_2', 'w_up_2', 'w_down_2', 'norm_final_2']


def kernel(**inputs):
    import numpy as _np
    import concourse.bacc as _bacc
    from concourse import mybir as _mybir
    from concourse.bass_utils import run_bass_kernel_spmd as _run

    nc = _bacc.Bacc("TRN2", target_bir_lowering=False, num_devices=1)
    arrays, args = {}, {}
    for name in _INS + ["consts"]:
        a = constants() if name == "consts" else _np.ascontiguousarray(inputs[name])
        arrays[f"in_{name}_dram"] = a
        args[name] = nc.dram_tensor(f"in_{name}_dram", a.shape, _mybir.dt.from_np(a.dtype), kind="ExternalInput").ap()
    out = nc.dram_tensor("out_0_dram", (1, S, D), F32, kind="ExternalOutput").ap()
    scr = {n: nc.dram_tensor(f"scr_{n}_dram", shape, F32, kind="Internal").ap() for n, shape in SCRATCH.items()}
    build(nc, args, out, scr)
    r = _run(nc, [arrays], core_ids=[0])
    return r.results[0]["out_0_dram"]
```

```python
from collections import deque
from contextlib import ExitStack

import numpy as np

import concourse.bass as bass
from concourse import mybir

ALU = mybir.AluOpType
ACT = mybir.ActivationFunctionType
AX = mybir.AxisListType
F32 = mybir.dt.float32
F32R = mybir.dt.float32r
I32 = mybir.dt.int32

S = 512
D = 1024
RMS_EPS = 1e-6
LN_EPS = 1e-5
NEG = -1e30
TWO_PI = 2.0 * np.pi
PI_C1 = 6.28125
PI_C2 = float(np.float32(np.round((TWO_PI - PI_C1) * 2.0 ** 20) / 2.0 ** 20))
PI_C3 = float(np.float32(TWO_PI - PI_C1 - PI_C2))
MAGIC = 12582912.0
PI_IN = 3.1415925

NRAW, NHL, AHEAD = 3, 6, 4
NTB = 7
LIVE = 4
RA = (2, 2, 2, 2, 2, 3)
SCRATCH = {"ys": (2048, 512), "cs": (32, 1024), "km": (128, 1024), "vm": (128, 1024), "x": (128, 4096)}
FF1 = [(0, 4), (4, 4), (8, 3)]
NFF2 = 4

C_ID, C_PERM, C_BT, C_NB, C_TF, C_TB, C_LL, C_FF, C_SF, C_AF = 0, 128, 256, 768, 1152, 1280, 1408, 1536, 1664, 1665
C_W = 1672


def constants():
    c = np.zeros((128, C_W), np.float32)
    i = np.arange(128)
    c[:, C_ID:C_ID + 128] = np.eye(128)
    perm = np.zeros((128, 128), np.float32)
    for p in range(128):
        m = p % 64
        if m < 16:
            perm[p - m + (m + 8) % 16, p] = 1.0
    c[:, C_PERM:C_PERM + 128] = perm
    for n, delta in enumerate((3, 2, 1, 0)):
        dist = 128 * delta + i[:, None] - i[None, :]
        count = ((dist >= 0) & (dist <= 128)).astype(int) + ((dist >= 0) & (dist % 4 == 0)) + ((dist >= 0) & (dist % 16 == 0))
        c[:, C_BT + 128 * n:C_BT + 128 * (n + 1)] = np.where(count > 0, np.log(np.maximum(count, 1)), NEG)
    rel = 128 + i[:, None] - np.arange(384)[None, :]
    c[:, C_NB:C_NB + 384] = np.where(np.abs(rel) <= 128, -np.abs(rel), NEG)
    c[:, C_TF:C_TF + 128] = i[:, None] <= i[None, :]
    c[:, C_TB:C_TB + 128] = i[:, None] >= i[None, :]
    c[127, C_LL:C_LL + 128] = 1.0
    c[0, C_FF:C_FF + 128] = 1.0
    inv = np.float32(500000.0) ** (-np.arange(0, 16, 2, dtype=np.float32) / np.float32(16))
    for p in range(128):
        m = p % 64
        if m < 16:
            c[p, C_AF] = inv[m % 8]
            c[p, C_SF] = -1.0 if m < 8 else 1.0
    return c


class Engine:

    def __init__(self, sem):
        self.sem, self.n, self.steps, self.seen = sem, 0, [], {}

    def wait(self, *tokens):
        for t in tokens:
            if t is None:
                continue
            if isinstance(t, list):
                self.wait(*t)
                continue
            sem, value = t
            key = id(sem)
            if self.seen.get(key, 0) < value:
                self.seen[key] = value
                self.steps.append(lambda e, s=sem, v=value: e.wait_ge(s, v))

    def do(self, fn, *tokens, sig=True):
        self.wait(*tokens)
        if not sig:
            self.steps.append(fn)
            return None
        self.n += 1
        self.steps.append(lambda e: fn(e).then_inc(self.sem, 1))
        return (self.sem, self.n)

    def emit(self, e):
        for s in self.steps:
            s(e)


class Line:

    def __init__(self, sem):
        self.sem, self.n = sem, 0

    def go(self, eng, fn, *tokens):
        eng.wait(*tokens)
        self.n += 16
        eng.steps.append(lambda e: fn(e).then_inc(self.sem, 16))
        return (self.sem, self.n)


class Ring:

    def __init__(self, bufs):
        self.free = deque((b, None) for b in bufs)

    def take(self):
        return self.free.popleft()

    def give(self, buf, tok):
        self.free.append((buf, tok))


def bc(ap, n):
    a, b = ap.shape[0], ap.shape[1]
    return ap.unsqueeze(2).to_broadcast([a, b, n])


def mid(ap, n):
    a, b = ap.shape[0], ap.shape[1]
    return ap.unsqueeze(1).to_broadcast([a, n, b])


def build(nc, A, out, scr, dbg=None):
    ctx = ExitStack()
    with ctx:
        def sem(name):
            return ctx.enter_context(nc.semaphore(name))

        def sb(name, shape, dt=F32, c=ctx):
            return c.enter_context(nc.sbuf_tensor(name, shape, dt))

        pe, act, dve, pool, sp = (Engine(sem(f"s_{n}")) for n in ("pe", "act", "dve", "pool", "sp"))
        psum = [ctx.enter_context(nc.psum_tensor(f"ps{i}", [128, 512], F32)) for i in range(8)]
        main = Ring(psum[:4])
        side = Ring(psum[4:])

        RAW = [sb(f"raw{i}", [128, 2, 512]) for i in range(NRAW)]
        HI = [sb(f"hi{i}", [128, 2, 512], F32R) for i in range(NHL)]
        LO = [sb(f"lo{i}", [128, 2, 512], F32R) for i in range(NHL)]
        hH = sb("hH", [128, 8, S], F32R)
        hL = sb("hL", [128, 8, S], F32R)
        X = sb("X", [128, 4, D])
        CST = sb("CST", [128, C_W])
        ST = sb("ST", [128, 256])
        half = sb("half", [128, 16])

        ident = CST[:, C_ID:C_ID + 128]

        def line(name):
            return Line(sem(name))

        l_cst = line("l_cst")
        CSQ = pool
        t_cst = l_cst.go(sp, lambda e: e.dma_start(CST[:, :], A["consts"]))
        t_half = pool.do(lambda e: e.memset(half[:, :], -0.5))

        stat = [0]

        def small(n):
            if stat[0] + n > 256:
                stat[0] = 0
            a = stat[0]
            stat[0] += n
            return ST[:, a:a + n]

        small_tok = []

        def mm(outp, lhsT, rhs, start, stop, *tok, sig=False):
            return pe.do(lambda e: e.matmul(outp, lhsT, rhs, start=start, stop=stop), *tok, sig=sig)

        def tr(outp, inp, n, *tok, sig=False):
            return pe.do(lambda e: e.transpose(outp, inp, ident[0:n, 0:n]), *tok, sig=sig)

        def copy_act(o, i, *tok, func=ACT.Copy, **kw):
            return act.do(lambda e: e.activation(o, i, func, **kw), *tok)

        def tt(eng, o, a, b, op, *tok):
            return eng.do(lambda e: e.tensor_tensor(o, a, b, op), *tok)

        def ts(eng, o, a, s1, s2, op0, op1, *tok):
            if s2 is None:
                return eng.do(lambda e: e.tensor_scalar(o, a, s1, None, op0), *tok)
            return eng.do(lambda e: e.tensor_scalar(o, a, s1, s2, op0, op1), *tok)

        def stt(o, a, s, b, op0, op1, *tok):
            return dve.do(lambda e: e.scalar_tensor_tensor(out=o, in0=a, scalar=s, in1=b, op0=op0, op1=op1), *tok)

        def fn_act(o, i, func, *tok, **kw):
            return act.do(lambda e: e.activation(o, i, func, **kw), *tok)

        def ttr(o, a, b, init, op0, op1, acc, *tok):
            return dve.do(lambda e: e.tensor_tensor_reduce(o, a, b, 1.0, init, op0, op1, acc), *tok)

        def copy_dve(o, i, *tok):
            return dve.do(lambda e: e.tensor_copy(o, i), *tok)

        def recip(o, i, *tok):
            return dve.do(lambda e: e.reciprocal(o, i), *tok)

        def rstd(o, ss, n, eps, *tok):
            k = ss.shape[1]
            t = ts(pool, o, ss, 1.0 / n, eps, ALU.mult, ALU.add, *tok)
            return tt(pool, o, o, half[:, 0:k], ALU.pow, t, t_half)

        def split_from(src, hi, lo, *tok):
            th = copy_act(hi, src, *tok)
            tl = tt(dve, lo, src, hi.bitcast(F32), ALU.subtract, th, *tok)
            return th, tl

        dumps = line("l_dbg") if dbg is not None else None

        def dump(name, ap, *tok):
            if dbg is not None and name in dbg:
                pool_wait = dumps.go(pool, lambda e: e.dma_start(dbg[name], ap), *tok)
                for q in (pool, act, dve, pe, sp):
                    q.wait(pool_wait)

        units = []

        def plan(tag, parts_of, n, cols=512):
            for u in range(n):
                units.append((tag, parts_of(u), cols))

        def rows(w, u, c0, c1):
            return w[256 * u:256 * u + 256, c0:c1].rearrange("(k p) n -> p k n", p=128)

        def cols_of(name, c0, c1):
            w = A[name][0]
            return lambda u: [(0, rows(w, u, c0, c1))]

        def cols2(n1, a0, a1, n2, b0, b1):
            w1, w2 = A[n1][0], A[n2][0]
            return lambda u: [(0, rows(w1, u, a0, a1)), (a1 - a0, rows(w2, u, b0, b1))]

        XBC = 1536 + 2048
        B0, C0 = XBC + 2048, XBC + 3072
        DT0 = XBC + 4096
        G0 = DT0 + 64
        plan("xk", cols_of("w_xkv_2", 0, 512), 4)
        plan("xv", cols_of("w_xkv_2", 512, 1024), 4)
        for n, c in (("q", 0), ("k", 512), ("v", 1024), ("vs", 2048), ("u", 1536)):
            plan("in_" + n, cols_of("w_in", c, c + 512), 4)
        for h in range(2):
            plan("wout", cols_of("w_out", 512 * h, 512 * h + 512), 4)
        for b0, nb in FF1:
            for b in range(b0, b0 + nb):
                plan("gu", cols2("w_gate", 256 * b, 256 * b + 256, "w_up", 256 * b, 256 * b + 256), 4)
            for h in range(2):
                w = A["w_down"][0][256 * b0:256 * (b0 + nb), 512 * h:512 * h + 512]
                plan("down", lambda u, w=w: [(0, w[256 * u:256 * u + 256, :].rearrange("(k p) n -> p k n", p=128))], nb)
        plan("dt", cols_of("w_in_2", DT0, DT0 + 64), 4, 64)
        for j in range(4):
            plan("bc", cols2("w_in_2", B0 + 256 * j, B0 + 256 * j + 256, "w_in_2", C0 + 256 * j, C0 + 256 * j + 256), 4)
            plan("xs", cols_of("w_in_2", XBC + 512 * j, XBC + 512 * j + 512), 4)
            plan("z", cols_of("w_in_2", 1536 + 512 * j, 1536 + 512 * j + 512), 4)
        plan("kv2", cols_of("w_in_2", 1024, 1536), 4)
        for j in range(2):
            wq = A["w_in_2"][0]
            for u in range(4):
                units.append(("q2", [((k, b), wq[256 * u + 128 * k:256 * u + 128 * k + 128, 512 * j + 256 * b:512 * j + 256 * b + 256].rearrange(
                    "p (f c) -> p f c", c=64)) for k in range(2) for b in range(2)], 512))
        for j in range(4):
            plan("gate", cols_of("w_in_2", G0 + 512 * j, G0 + 512 * j + 512), 4)
        for j in range(2):
            w = A["w_ssd_branch_2"][0]
            for u in range(8):
                units.append(("wssd", [(0, rows(w, u, 512 * j, 512 * j + 512))], 512))
                units.append(("ys", [(0, rows(scr["ys"], u, 0, 512))], 512))
        for j in range(2):
            plan("wattn", cols_of("w_attn_branch_2", 512 * j, 512 * j + 512), 4)
        for h in range(2):
            plan("wout2", cols_of("w_out_2", 512 * h, 512 * h + 512), 4)
        plan("xq", cols_of("w_xq_2", 0, 512), 4)
        for h in range(2):
            plan("xo", cols_of("w_xo_2", 512 * h, 512 * h + 512), 2)
        for f in range(NFF2):
            for b in range(2):
                c = 1024 * f + 512 * b
                plan("up2", cols_of("w_up_2", c, c + 512), 4)
            for h in range(2):
                w = A["w_down_2"][0][1024 * f:1024 * f + 1024, 512 * h:512 * h + 512]
                plan("down2", lambda u, w=w: [(0, w[256 * u:256 * u + 256, :].rearrange("(k p) n -> p k n", p=128))], 4)

        l_raw = [line(f"l_raw{i}") for i in range(NRAW)]
        raw_free = [None] * NRAW
        hl_free = [None] * NHL
        unit_tok = {}
        ys_done = []
        st_ = {"load": 0, "conv": 0, "use": 0}

        def load_next():
            i = st_["load"]
            if i >= len(units):
                return
            st_["load"] += 1
            tag, parts, _ = units[i]
            r = i % NRAW
            dep = ys_done if tag == "ys" else None
            for c0, src in parts:
                if tag == "q2":
                    dst = RAW[r][:, c0[0], :].rearrange("p (f b c) -> p f b c", b=2, c=64)[:, :, c0[1], :]
                else:
                    dst = RAW[r][:, :, c0:c0 + src.shape[2]]
                t = l_raw[r].go(sp, lambda e, s=src, d=dst: e.dma_start(d, s), raw_free[r], dep)
            unit_tok[i] = t

        def convert_next():
            i = st_["conv"]
            if i >= len(units):
                return
            assert i < st_["load"] and i - NHL in released
            st_["conv"] += 1
            w = units[i][2]
            r, s = i % NRAW, i % NHL
            th = copy_act(HI[s][:, :, 0:w], RAW[r][:, :, 0:w], unit_tok[i], hl_free[s])
            tl = tt(dve, LO[s][:, :, 0:w], RAW[r][:, :, 0:w], HI[s][:, :, 0:w].bitcast(F32), ALU.subtract, th, hl_free[s])
            raw_free[r] = [th, tl]
            unit_tok[i] = [th, tl]
            load_next()

        def take_unit(tag):
            i = st_["use"]
            assert units[i][0] == tag, (units[i][0], tag)
            st_["use"] += 1
            while st_["conv"] <= i:
                convert_next()
            return i, HI[i % NHL], LO[i % NHL], unit_tok[i]

        released = set(range(-NHL, 0))

        def release(i, tok):
            hl_free[i % NHL] = tok
            released.add(i)

        def look_ahead():
            if st_["conv"] < st_["use"] + AHEAD and st_["conv"] - NHL in released:
                convert_next()

        waiting = deque()
        live = deque()

        def task(*gens):
            waiting.extend(gens)

        def soon(gen):
            live.appendleft(gen)

        def pump(n=1):
            while n > 0:
                while len(live) < LIVE and waiting:
                    live.append(waiting.popleft())
                if not live:
                    return
                n -= 1
                g = live.popleft()
                try:
                    next(g)
                    live.append(g)
                except StopIteration:
                    pass

        def drain(until=lambda: False):
            n = 0
            while (live or waiting) and not until():
                pump(1)
                n += 1
                assert n < 5000

        def room(ring, n=1):
            while len(ring.free) < n:
                yield

        def fm_block(tag, nu, nf, act_h, act_l, a_tok, evac, rate=0, N=S):
            banks = [main.take() for _ in range(nf)]
            for u in range(nu):
                look_ahead()
                i, wh, wl, wt = take_unit(tag)
                for f in range(nf):
                    bank, bt = banks[f]
                    for kk in range(2):
                        k = 2 * u + kk
                        first, last = k == 0, k == 2 * nu - 1
                        w_h, w_l = wh[:, kk, 128 * f:128 * f + 128], wl[:, kk, 128 * f:128 * f + 128]
                        mm(bank[:, 0:N], w_h, act_h[:, k, 0:N], first, False, wt, a_tok, bt if first else None)
                        mm(bank[:, 0:N], w_h, act_l[:, k, 0:N], False, False)
                        t = mm(bank[:, 0:N], w_l, act_h[:, k, 0:N], False, last, sig=last or (f == nf - 1 and kk == 1))
                    if last:
                        main.give(bank, evac(f, bank, t))
                    if f == nf - 1:
                        release(i, t)
                    pump(rate)
            return t

        def tm_mms(bank, ntok, nu, u, kk, w, wh, wl, act_h, act_l, t, *tok, sig=False):
            k = 2 * u + kk
            first, last = k == 0, k == 2 * nu - 1
            a_h, a_l = act_h[:, k, 128 * t:128 * t + 128], act_l[:, k, 128 * t:128 * t + 128]
            mm(bank, a_h, wh[:, kk, w[0]:w[1]], first, False, *tok)
            mm(bank, a_h, wl[:, kk, w[0]:w[1]], False, False)
            return mm(bank, a_l, wh[:, kk, w[0]:w[1]], False, last, sig=sig or last)

        def tm_block(tag, nu, act_h, act_l, a_tok, evac, rate=0, ntok=4, tail=False):
            banks = [main.take() for _ in range(ntok)]
            if tail:
                us = []
                for u in range(nu):
                    look_ahead()
                    us.append(take_unit(tag))
                for t in range(ntok):
                    bank, bt = banks[t]
                    for u in range(nu):
                        i, wh, wl, wt = us[u]
                        for kk in range(2):
                            tok = tm_mms(bank[:, :], ntok, nu, u, kk, (0, 512), wh, wl, act_h, act_l, t, wt, a_tok, bt, sig=(t == ntok - 1 and kk == 1))
                        if t == ntok - 1:
                            release(i, tok)
                            look_ahead()
                    main.give(bank, evac(t, bank, tok))
                return tok
            for u in range(nu):
                look_ahead()
                i, wh, wl, wt = take_unit(tag)
                for t in range(ntok):
                    bank, bt = banks[t]
                    for kk in range(2):
                        first = u == 0 and kk == 0
                        tok = tm_mms(bank[:, :], ntok, nu, u, kk, (0, 512), wh, wl, act_h, act_l, t, wt, a_tok, bt if first else None, sig=(t == ntok - 1 and kk == 1))
                    if u == nu - 1:
                        main.give(bank, evac(t, bank, tok))
                    if t == ntok - 1:
                        release(i, tok)
                    pump(rate)
            return tok

        hn_ring = Ring([sb(f"hn{i}", [128, D]) for i in range(2)])
        l_gain = [line(f"l_gain{i}") for i in range(3)]
        gains = Ring([(sb(f"gain{i}", [128, D]), l_gain[i]) for i in range(2)])

        def load_gain(*parts):
            (g, ln), free = gains.take()
            c = 0
            for p in parts:
                n = p.shape[-1]
                t = ln.go(sp, lambda e, p=p, c=c, n=n: e.dma_start(g[:, c:c + n], p.partition_broadcast(128)), free)
                c += n
            return (g, ln), t

        def square_sum(o, x, *tok):
            hn, ht = hn_ring.take()
            t = fn_act(hn[:, 0:x.shape[1]], x, ACT.Square, ht, *tok, accum_out=o)
            hn_ring.give(hn, t)
            return t

        def turn(src, nk, hi, lo, t0, h_free, *tok):
            done = []
            for b in range(0, nk, 4):
                n = min(4, nk - b)
                bank, bt = side.take()
                for k in range(n):
                    t = tr(bank[:, 128 * k:128 * k + 128], src[:, 128 * (b + k):128 * (b + k) + 128], 128, t_cst, bt if k == 0 else None, *tok, sig=k == n - 1)
                v = bank[:, 0:128 * n].rearrange("p (k t) -> p k t", k=n)
                th, tl = split_from(v, hi[:, b:b + n, t0:t0 + 128], lo[:, b:b + n, t0:t0 + 128], t, h_free)
                side.give(bank, [th, tl])
                done += [th, tl]
            return done, t

        def norm_turn(x, gain, g_tok, t0, hi, lo, h_free, *tok):
            ss = small(1)
            t = square_sum(ss, x, *tok)
            t = rstd(ss, ss, D, RMS_EPS, t)
            (hn, ht) = hn_ring.take()
            t = stt(hn[:, :], x, ss, gain[:, :], ALU.mult, ALU.mult, t, ht, g_tok)
            done, last = turn(hn, 8, hi, lo, t0, h_free, t)
            hn_ring.give(hn, last)
            return done, t

        for _ in range(NRAW):
            load_next()
        P0 = ExitStack()
        MEMX = sb("MEMX", [128, 2, D], c=P0)
        KM0 = sb("KM0", [128, 4, 256], c=P0)
        VM0 = sb("VM0", [128, 2, 512], c=P0)
        mH = sb("mH", [128, 8, 256], F32R, c=P0)
        mL = sb("mL", [128, 8, 256], F32R, c=P0)
        l_x = [line(f"l_x{i}") for i in range(6)]
        t_mem = [l_x[4 + t].go(act, lambda e, t=t: e.dma_start(MEMX[:, t, :], A["mem_2"][0, 128 * t:128 * t + 128, :])) for t in range(2)]
        g_mem, tg_mem = load_gain(A["norm_mem_2"][0])
        g_pre, tg_pre = load_gain(A["pre_mix_norm"][0])
        t_x = [l_x[t].go(act, lambda e, t=t: e.dma_start(X[:, t, :], A["x"][0, 128 * t:128 * t + 128, :])) for t in range(4)]
        mtok = []
        for t in range(2):
            d, last = norm_turn(MEMX[:, t, :], g_mem[0], tg_mem, 128 * t, mH, mL, None, t_mem[t])
            mtok += d
        gains.give(g_mem, last)

        km_tok, vm_tok = [], []

        def evac_km(f, bank, t):
            r = copy_act(KM0[:, f, :], bank[:, 0:256], t)
            km_tok.append(r)
            return r

        def evac_vm(t_, bank, t):
            r = copy_act(VM0[:, t_, :], bank[:, :], t)
            vm_tok.append(r)
            return r

        fm_block("xk", 4, 4, mH, mL, mtok, evac_km, N=256)
        mem_mm = tm_block("xv", 4, mH, mL, mtok, evac_vm, ntok=2)
        l_kv = line("l_kv")
        l_kv.go(act, lambda e: e.dma_start(scr["km"], KM0[:, :, :].rearrange("p f t -> p (f t)")), km_tok)
        kv_saved = l_kv.go(act, lambda e: e.dma_start(scr["vm"], VM0[:, :, :].rearrange("p f t -> p (f t)")), vm_tok)
        mem_free = [mem_mm, kv_saved]

        htok = []
        for t in range(4):
            d, last = norm_turn(X[:, t, :], g_pre[0], tg_pre, 128 * t, hH, hL, None, t_x[t])
            htok += d
        gains.give(g_pre, last)
        P0.close()

        P1 = ExitStack()
        Q = sb("Q", [128, 4, S], c=P1)
        K = sb("K", [128, 4, S], c=P1)
        V = sb("V", [128, 4, 512], c=P1)
        VS = sb("VS", [128, 4, 512], c=P1)
        MIX = sb("MIX", [128, 4, D], c=P1)
        RC = sb("RC", [128, S], c=P1)
        RS = sb("RS", [128, S], c=P1)
        TMPA = [sb(f"tmpa{i}", [128, 512], c=P1) for i in range(4)]
        tmp = Ring(TMPA)
        WS = MIX[:, 0:2, 0:512]
        WT = sb("WT", [128, 8, 128], c=P1)
        SB_ = sb("SBs", [128, 8], c=P1)
        l_p1 = line("l_p1")
        
        def ld(o, i, *tok, slow=False):
            return l_p1.go(sp, lambda e: e.dma_start(o, i, allow_slow_non_contiguous=slow), *tok)

        g_ln, tg_ln = load_gain(A["sgu_ln_gain"][0], A["sgu_ln_bias"][0])
        posi, pt_ = tmp.take()
        ld(SB_[:, :], A["sgu_b_spatial"][0].rearrange("g i -> i g"), mem_free, mtok, slow=True)
        POSI = posi[:, :].bitcast(I32)
        ld(POSI, A["positions"][0].partition_broadcast(128))
        ld(MIX[:, 0, :].rearrange("p (g j) -> p g j", g=8), A["sgu_w_spatial"][0].rearrange("g i j -> i g j"))
        t_p1 = (l_p1.sem, l_p1.n)

        def rotary_tables():
            a, at = tmp.take()
            b, bt_ = tmp.take()
            t = dve.do(lambda e: e.tensor_copy(a[:, :], POSI), t_p1, at, mem_free)
            tmp.give(posi, t)
            t = ts(dve, a[:, :], a[:, :], CST[:, C_AF:C_AF + 1], None, ALU.mult, None, t, t_cst)
            t = ts(dve, b[:, :], a[:, :], float(np.float32(1.0 / TWO_PI)), MAGIC, ALU.mult, ALU.add, t, bt_)
            t = ts(dve, b[:, :], b[:, :], MAGIC, None, ALU.subtract, None, t)
            for c in (PI_C1, PI_C2, PI_C3):
                t = stt(a[:, :], b[:, :], -c, a[:, :], ALU.mult, ALU.add, t)
            t = ts(dve, a[:, :], a[:, :], PI_IN, -PI_IN, ALU.min, ALU.max, t)
            yield
            t1 = act.do(lambda e: e.activation(RS[:, :], a[:, :], ACT.Sin), t)
            t2 = act.do(lambda e: e.activation(b[:, :], a[:, :], ACT.Abs), t)
            t2 = ts(dve, b[:, :], b[:, :], -1.0, float(np.pi / 2), ALU.mult, ALU.add, t2)
            t2 = act.do(lambda e: e.activation(RC[:, :], b[:, :], ACT.Sin), t2)
            t1 = ts(dve, RS[:, :], RS[:, :], CST[:, C_SF:C_SF + 1], None, ALU.mult, None, t1)
            rot_tok.extend([t1, t2])
            tmp.give(a, [t1, t2])
            tmp.give(b, t2)
            yield

        rot_tok = []
        task(rotary_tables())
        drain()
        q_tok, k_tok, v_tok = {}, {}, {}

        def rope(dst, f, tok_d, t0):
            yield
            yield from room(side)
            bank, bt = side.take()
            t = mm(bank[:, :], CST[:, C_PERM:C_PERM + 128], dst[:, f, :], True, True, t0, bt, t_cst, sig=True)
            yield from room(tmp)
            a, at = tmp.take()
            t1 = tt(dve, a[:, :], bank[:, :], RS[:, :], ALU.mult, t, at, rot_tok)
            side.give(bank, t1)
            t2 = tt(pool, dst[:, f, :], dst[:, f, :], RC[:, :], ALU.mult, t, rot_tok)
            t3 = tt(pool, dst[:, f, :], dst[:, f, :], a[:, :], ALU.add, t1, t2)
            tmp.give(a, t3)
            tok_d[f] = t3
            yield

        def evac_rope(dst, tok_d, scale):
            def evac(f, bank, t):
                r = copy_act(dst[:, f, :], bank[:, :], t, mem_free, mtok, scale=scale)
                task(rope(dst, f, tok_d, r))
                return r
            return evac

        def evac_v(t_, bank, t):
            v_tok[t_] = copy_act(V[:, t_, :], bank[:, :], t)
            return v_tok[t_]

        fm_block("in_q", 4, 4, hH, hL, htok, evac_rope(Q, q_tok, 0.125), rate=1)
        fm_block("in_k", 4, 4, hH, hL, htok, evac_rope(K, k_tok, 1.0), rate=1)
        tm_block("in_v", 4, hH, hL, htok, evac_v, rate=1)

        SCO = tmp
        PT = Ring([sb(f"pt{i}", [128, 512], c=P1) for i in range(3)])
        att_tok = []
        g_mix, tg_mix = load_gain(A["attn_out_norm"][0], A["sgu_out_norm"][0])

        def attend(qt, h):
            n = 128 * (qt + 1)
            f, p0 = h // 2, 64 * (h % 2)
            yield from room(side)
            yield from room(SCO, 2)
            bank, bt = side.take()
            t = mm(bank[:, 0:n], Q[p0:p0 + 64, f, 128 * qt:128 * qt + 128], K[p0:p0 + 64, f, 0:n], True, True, q_tok[f], k_tok[f], bt, sig=True)
            s, s_t = SCO.take()
            m = small(3)
            t = ttr(s[:, 0:n], bank[:, 0:n], CST[:, C_BT + 128 * (3 - qt):C_BT + 512], -3e38, ALU.add, ALU.max, m[:, 0:1], t, s_t)
            side.give(bank, t)
            t = ts(dve, m[:, 1:2], m[:, 0:1], -1.0, None, ALU.mult, None, t)
            te = fn_act(s[:, 0:n], s[:, 0:n], ACT.Exp, t, bias=m[:, 1:2], accum_out=m[:, 2:3])
            yield
            r = recip(m[:, 2:3], m[:, 2:3], te)
            yield from room(side)
            yield from room(PT)
            bank, bt = side.take()
            for k in range(qt + 1):
                t = tr(bank[:, 128 * k:128 * k + 128], s[:, 128 * k:128 * k + 128], 128, te, bt, sig=k == qt)
            SCO.give(s, t)
            pt, pt_t = PT.take()
            t = (copy_act if h % 2 else copy_dve)(pt[:, 0:n], bank[:, 0:n], t, pt_t)
            side.give(bank, t)
            yield
            yield from room(side)
            bank, bt = side.take()
            for k in range(qt + 1):
                t2 = mm(bank[:, 0:64], pt[:, 128 * k:128 * k + 128], V[:, k, 64 * h:64 * h + 64], k == 0, k == qt, t, v_tok[k], bt, sig=k == qt)
            PT.give(pt, t2)
            t = ts(dve, MIX[:, qt, 64 * h:64 * h + 64], bank[:, 0:64], m[:, 2:3], None, ALU.mult, None, t2, r, wt_tok)
            side.give(bank, t)
            head_tok[qt, h] = t
            yield

        def attend_norm(qt):
            while (qt, 7) not in head_tok:
                yield
            o = MIX[:, qt, 0:512]
            ss = small(1)
            t = square_sum(ss, o, [head_tok[qt, h] for h in range(8)])
            t = rstd(ss, ss, 512, RMS_EPS, t)
            yield
            att_tok.append(stt(o, o, ss, g_mix[0][:, 0:512], ALU.mult, ALU.mult, t, tg_mix))
            yield

        head_tok = {}
        wt_tok = []

        def spatial_weights():
            w = MIX[:, 0, :].rearrange("p (g j) -> p g j", g=8)
            t = tt(pool, w, w, mid(CST[:, C_TB:C_TB + 128], 8), ALU.mult, t_p1, t_cst)
            for b in range(2):
                bank, bt = side.take()
                for g in range(4):
                    t2 = tr(bank[:, 128 * g:128 * g + 128], w[:, 4 * b + g, :], 128, t, bt, sig=g == 3)
                t2 = copy_act(WT[:, 4 * b:4 * b + 4, :].rearrange("p g i -> p (g i)"), bank[:, :], t2)
                side.give(bank, t2)
                wt_tok.append(t2)
            yield

        task(spatial_weights())
        drain()
        for qt in range(4):
            task(*[attend(qt, h) for h in range(8)], attend_norm(qt))

        vs_tok, u_tok = {}, {}

        def ln_tile(t_, t0):
            v = VS[:, t_, :]
            st6, mv = small(6), small(2)
            t = dve.do(lambda e: e.bn_stats(st6, v), t0)
            t = dve.do(lambda e: e.bn_aggr(mv, st6), t)
            t = rstd(mv[:, 1:2], mv[:, 1:2], 1.0, LN_EPS, t)
            t = ts(dve, v, v, mv[:, 0:1], mv[:, 1:2], ALU.subtract, ALU.mult, t)
            t = tt(pool, v, v, g_ln[0][:, 0:512], ALU.mult, t, tg_ln)
            t = tt(pool, v, v, g_ln[0][:, 512:1024], ALU.add, t)
            vs_tok[t_] = t

        def evac_vs(t_, bank, t):
            t = act.do(lambda e: e.activation(VS[:, t_, :], bank[:, :], ACT.Gelu), t)
            ln_tile(t_, t)
            return t

        def evac_u(t_, bank, t):
            u_tok[t_] = act.do(lambda e: e.activation(MIX[:, t_, 512:1024], bank[:, :], ACT.Gelu), t, wt_tok)
            return u_tok[t_]

        tm_block("in_vs", 4, hH, hL, htok, evac_vs, rate=RA[5])
        in_done = tm_block("in_u", 4, hH, hL, htok, evac_u, rate=RA[5])

        sgu_tok = {}

        sp_tok = {}

        def spatial(g):
            yield from room(side)
            bank, bt = side.take()
            t = mm(bank[:, 0:256].rearrange("p (n c) -> p n c", n=4), WT[:, g, :], VS[:, :, 64 * g:64 * g + 64], True, True,
                   [vs_tok[i] for i in range(4)], wt_tok, bt, sig=True)
            u = MIX[:, :, 512 + 64 * g:576 + 64 * g]
            t = stt(u, bank[:, 0:256].rearrange("p (n c) -> p n c", n=4), SB_[:, g:g + 1], u, ALU.add, ALU.mult, t, [u_tok[i] for i in range(4)], t_p1)
            side.give(bank, t)
            sp_tok[g] = t
            yield

        def spatial_norm(t_):
            while len(sp_tok) < 8:
                yield
            ss = small(1)
            o = MIX[:, t_, 512:1024]
            t2 = square_sum(ss, o, [sp_tok[g] for g in range(8)])
            t2 = rstd(ss, ss, 512, RMS_EPS, t2)
            yield
            sgu_tok[t_] = stt(o, o, ss, g_mix[0][:, 512:1024], ALU.mult, ALU.mult, t2, tg_mix)
            yield

        task(*[spatial(g) for g in range(8)], *[spatial_norm(t_) for t_ in range(4)])
        drain()
        gains.give(g_mix, [list(sgu_tok.values()), att_tok])
        gains.give(g_ln, [vs_tok[i] for i in range(4)])
        dump("mix", MIX[:, :, :], list(sgu_tok.values()), att_tok)

        mtk = []
        for t_ in range(4):
            d, _ = turn(MIX[:, t_, :], 8, hH, hL, 128 * t_, in_done, sgu_tok[t_], att_tok[t_])
            mtk += d
        turned = _
        P1.close()

        def project(P, tag, nu, a_h, a_l, a_tok, Y, yfree, tail_fn, add=False, tail=True, rate=0):
            ytok = {}

            def evac(h):
                def f(t_, bank, t):
                    y = Y[:, t_, 512 * h:512 * h + 512]
                    if add:
                        r = tt(dve, y, bank[:, :], y, ALU.add, t, yfree)
                    else:
                        r = copy_act(y, bank[:, :], t, yfree)
                    ytok.setdefault(t_, []).append(r)
                    if h == 1 and tail_fn:
                        pend.append((t_, list(ytok[t_])))
                    return r
                return f

            pend = []
            tm_block(tag, nu, a_h, a_l, a_tok, evac(0), rate=rate)
            if not tail:
                last = tm_block(tag, nu, a_h, a_l, a_tok, evac(1), rate=rate)
                return last, ytok
            fn = evac(1)

            def evac_tail(t_, bank, t):
                r = fn(t_, bank, t)
                while len(pend) > 1:
                    a = pend.pop(0)
                    tail_fn(*a, t)
                return r
            last = tm_block(tag, nu, a_h, a_l, a_tok, evac_tail, tail=True)
            while pend:
                a = pend.pop(0)
                tail_fn(*a, last)
            return last, ytok

        def post_add(t_, tok, y, gain, g_tok):
            ss = small(1)
            t = square_sum(ss, y, tok)
            t = rstd(ss, ss, D, RMS_EPS, t)
            t = stt(y, y, ss, gain[:, :], ALU.mult, ALU.mult, t, g_tok)
            return tt(dve, X[:, t_, :], X[:, t_, :], y, ALU.add, t)

        P2 = ExitStack()
        Y = sb("Y", [128, 4, D], c=P2)
        aH = sb("aH", [128, 8, S], F32R, c=P2)
        aL = sb("aL", [128, 8, S], F32R, c=P2)
        SG = Ring([sb(f"sg{i}", [128, 512], c=P2) for i in range(2)])
        g_post, tg_post = load_gain(A["post_mix_norm"][0])
        g_ffn, tg_ffn = load_gain(A["pre_ffn_norm"][0])
        htok = []
        xtok = {}

        def tail1(t_, tok, mm_tok):
            xtok[t_] = post_add(t_, tok, Y[:, t_, :], g_post[0], tg_post)
            d, l = norm_turn(X[:, t_, :], g_ffn[0], tg_ffn, 128 * t_, hH, hL, mm_tok, xtok[t_])
            htok.extend(d)
            xtok[t_] = l

        project(P2, "wout", 4, hH, hL, mtk, Y, turned, tail1)
        gains.give(g_post, xtok[3])
        gains.give(g_ffn, xtok[3])
        dump("x1", X[:, :, :], [xtok[i] for i in range(4)])

        g_pf, tg_pf = load_gain(A["post_ffn_norm"][0])
        g_nm, tg_nm = load_gain(A["norm_mix_2"][0])
        a_free = [turned]

        def split_evac(dst_f, src, t):
            th, tl = split_from(src, aH[:, dst_f, :], aL[:, dst_f, :], t)
            return th, tl

        for c, (b0, nb) in enumerate(FF1):
            atok = []
            for b in range(nb):
                gate = {}

                def evac_gu(f, bank, t, b=b):
                    if f < 2:
                        s, st = SG.take()
                        r = fn_act(s[:, :], bank[:, :], ACT.Sigmoid, t, st, turned)
                        r = tt(dve, s[:, :], s[:, :], bank[:, :], ALU.mult, r)
                        gate[f] = (s, r)
                        return r
                    s, r = gate[f - 2]
                    r1 = tt(dve, s[:, :], s[:, :], bank[:, :], ALU.mult, r, t)
                    th, tl = split_from(s[:, :], aH[:, 2 * b + f - 2, :], aL[:, 2 * b + f - 2, :], r1, a_free)
                    SG.give(s, [th, tl])
                    atok.extend([th, tl])
                    return r1

                hdone = fm_block("gu", 4, 4, hH, hL, htok, evac_gu)
            if c < len(FF1) - 1:
                last, yt = project(P2, "down", nb, aH, aL, atok, Y, [xtok[i] for i in range(4)], None, add=c > 0, tail=False)
                a_free = [last]
                yfree = [yt[i] for i in range(4)]
            else:
                htok = []

                def tail2(t_, tok, mm_tok):
                    xtok[t_] = post_add(t_, tok, Y[:, t_, :], g_pf[0], tg_pf)
                    d, l = norm_turn(X[:, t_, :], g_nm[0], tg_nm, 128 * t_, hH, hL, hdone, xtok[t_])
                    htok.extend(d)
                    xtok[t_] = l
                last, yt = project(P2, "down", nb, aH, aL, atok, Y, yfree, tail2, add=True)
        gains.give(g_pf, xtok[3])
        gains.give(g_nm, xtok[3])
        dump("x2", X[:, :, :], [xtok[i] for i in range(4)])
        p2_done = [last, htok, [xtok[i] for i in range(4)]]
        P2.close()

        PA = ExitStack()
        XS0 = sb("XS0", [128, 4, 512], c=PA)
        BF0 = sb("BF0", [128, 2, 512], c=PA)
        CF0 = sb("CF0", [128, 2, 512], c=PA)
        BT0 = sb("BT0", [128, 2, 4, 128], c=PA)
        KF = sb("KF", [128, 2, 512], c=PA)
        P3 = ExitStack()
        bt1_gain, bt1_free = gains.take()
        BT1 = bt1_gain[0][:, :].rearrange("p (a c n) -> p a c n", a=2, c=4)
        xs_buf = [XS0, X[:, 0:2, :].rearrange("p a (b c) -> p (a b) c", b=2)]
        bf_buf = [BF0, X[:, 2, :].rearrange("p (b c) -> p b c", b=2)]
        cf_buf = [CF0, X[:, 3, :].rearrange("p (b c) -> p b c", b=2)]
        bt_buf = [BT0, BT1]
        buf_free = [[p2_done], [p2_done]]
        ZS = sb("ZS", [128, 4, 512], c=P3)
        YS = sb("YS", [128, 4, 512], c=P3)
        tmp = Ring([sb(f"tb{i}", [128, 512], c=P3) for i in range(NTB)])
        for i in range(NTB):
            tmp.free[i] = (tmp.free[i][0], p2_done)
        cb_sets = Ring([(sb(f"CBU{i}", [128, 4, 128], c=P3), sb(f"CBL{i}", [128, 4, 128], c=P3)) for i in range(2)])
        for i in range(2):
            cb_sets.free[i] = (cb_sets.free[i][0], p2_done)
        NCS = sb("NCS", [128, 4, 32], c=P3)
        PREV = sb("PREV", [128, 2, 3, 256], c=P3)
        DT = sb("DT", [128, 4, 64], c=P3)
        CS = sb("CS", [128, 4, 64], c=P3)
        ECS = sb("ECS", [128, 4, 64], c=P3)
        WST = sb("WST", [128, 4, 64], c=P3)
        CDEC = sb("CDEC", [128, 4, 64], c=P3)
        PAR = sb("PAR", [128, 160], c=P3)
        CW = sb("CW", [128, 192], c=P3)
        DTB, ALOG, DSK = PAR[:, 0:64], PAR[:, 64:128], PAR[:, 128:160]

        l_xs = line("l_xs")
        x_saved = l_xs.go(act, lambda e: e.dma_start(scr["x"], X[:, :, :].rearrange("p t d -> p (t d)")), [xtok[i] for i in range(4)])
        buf_free[1] += [x_saved, bt1_free]
        l_par = line("l_par")

        def ldp(o, i, *tok):
            return l_par.go(act, lambda e: e.dma_start(o, i), *tok)

        cr, cr_t = tmp.take()
        wrows = A["conv_w_2"][0].rearrange("k (t p) -> (k t) p", p=128)
        ldp(cr[:, 0:128], wrows[0:128, :], cr_t)
        ldp(cr[0:32, 128:256], wrows[128:160, :])
        ldp(cr[32:64, 128:256], A["conv_b_2"][0].rearrange("(t p) -> t p", p=128))
        ldp(DTB, A["dt_bias_2"][0].rearrange("a h -> (a h)").partition_broadcast(128), p2_done)
        ldp(ALOG, A["a_log_2"][0].rearrange("a h -> (a h)").partition_broadcast(128))
        t_par = ldp(DSK, A["d_skip_2"][0].partition_broadcast(128))
        bank, bt = side.take()
        tr(bank[:, 0:128], cr[:, 0:128], 128, t_par, bt)
        t = tr(bank[:, 128:192], cr[0:64, 128:256], 64, sig=True)
        cw_tok = copy_act(CW[:, :], bank[:, 0:192], t, p2_done, scale=0.5)
        side.give(bank, cw_tok)
        tmp.give(cr, t)

        bank, bt = side.take()
        us = []
        for u in range(4):
            look_ahead()
            us.append(take_unit("dt"))
        for t_ in range(4):
            for u in range(4):
                i, wh, wl, wt = us[u]
                for kk in range(2):
                    tk = tm_mms(bank[:, 64 * t_:64 * t_ + 64], 4, 4, u, kk, (0, 64), wh, wl, hH, hL, t_, wt, htok, bt, sig=(t_ == 3 and kk == 1))
                if t_ == 3:
                    release(i, tk)
        dt_bank, dt_t = bank, tk

        dts = {}

        def steps_dt():
            c4 = lambda ap: ap[:, 0:256].rearrange("p (c h) -> p c h", c=4)
            x1, a0 = tmp.take()
            e1, a1 = tmp.take()
            u1, a2 = tmp.take()
            x_, e_, u_ = c4(x1), c4(e1), c4(u1)
            t = tt(dve, x_, c4(dt_bank), mid(DTB, 4), ALU.add, dt_t, a0, t_par)
            side.give(dt_bank, t)
            t2 = fn_act(e_, x_, ACT.Abs, t, a1)
            t2 = fn_act(e_, e_, ACT.Exp, t2, scale=-1.0)
            t3 = ts(dve, u_, e_, 1.0, None, ALU.add, None, t2, a2)
            t4 = fn_act(DT[:, :, :], u_, ACT.Ln, t3, p2_done)
            tx = ts(dve, x_, x_, 0.0, None, ALU.max, None, t2)
            yield
            d1, a3 = tmp.take()
            d_ = c4(d1)
            t5 = ts(dve, d_, u_, 1.0, None, ALU.subtract, None, t3, a3)
            t5 = tt(dve, d_, e_, d_, ALU.subtract, t5)
            t6 = recip(u_, u_, t4, t5)
            t6 = tt(dve, d_, d_, u_, ALU.mult, t6)
            t6 = tt(dve, d_, d_, x_, ALU.add, t6, tx)
            tdt = tt(dve, DT[:, :, :], DT[:, :, :], d_, ALU.add, t6, t4)
            yield
            ta = fn_act(ALOG, ALOG, ACT.Exp, t_par)
            ta = ts(dve, ALOG, ALOG, -1.0, None, ALU.mult, None, ta)
            ta = tt(dve, x_, DT[:, :, :], mid(ALOG, 4), ALU.mult, ta, tdt)
            sbuf = None
            f1, b1 = tmp.take()
            f2, b2 = tmp.take()
            ft = []
            for d, (dst, dstt) in enumerate(((f1, b1), (f2, b2))):
                bank, bt = side.take()
                tri = CST[:, (C_TF, C_TB)[d]:(C_TF, C_TB)[d] + 128]
                for c in range(4):
                    t = mm(bank[0:32, 128 * c:128 * c + 128], x_[:, c, 32 * d:32 * d + 32], tri, True, True, ta, bt, sig=c == 3)
                t = copy_act(dst[0:32, :], bank[0:32, :], t, dstt)
                side.give(bank, t)
                ft.append(t)
                l_cs.go(act, lambda e, dst=dst, d=d: e.dma_start(scr["cs"][:, 512 * d:512 * d + 512], dst[0:32, :]), t)
            dts["cs"] = (l_cs.sem, l_cs.n)
            yield
            bank, bt = side.take()
            for d, dst in enumerate((f1, f2)):
                for c in range(4):
                    t = tr(bank[:, 64 * c + 32 * d:64 * c + 32 * d + 32], dst[0:32, 128 * c:128 * c + 128], 32, ft[d], bt, sig=c == 3)
            tcs = copy_act(CS[:, :, :], c4(bank), t)
            side.give(bank, tcs)
            bank, bt = side.take()
            for d in range(2):
                t = mm(bank[:, 128 * d:128 * d + 128].rearrange("p (c h) -> p c h", c=4), CST[:, (C_LL, C_FF)[d]:(C_LL, C_FF)[d] + 128],
                       CS[:, :, 32 * d:32 * d + 32], True, True, tcs, bt, sig=True)
            tot = bank[:, 0:256].rearrange("p (d c h) -> p d c h", d=2, c=4)
            td = []
            for d in range(2):
                v = lambda ap: ap[:, :, 32 * d:32 * d + 32]
                t1 = copy_act(v(CDEC), tot[:, d], t)
                td.append(tt(dve, v(WST), v(CDEC), v(CS), ALU.subtract, t1, tcs))
            side.give(bank, t1)
            td.append(fn_act(CDEC[:, :, :], CDEC[:, :, :], ACT.Exp, td))
            t1 = fn_act(WST[:, :, :], WST[:, :, :], ACT.Exp, td)
            t1 = tt(dve, WST[:, :, :], WST[:, :, :], DT[:, :, :], ALU.mult, t1, tdt)
            t2 = fn_act(ECS[:, :, :], CS[:, :, :], ACT.Exp, tcs)
            tn = fn_act(NCS[:, :, :], CS[:, :, 0:32], ACT.Copy, tcs, scale=-1.0)
            for b in (x1, e1, u1, d1):
                tmp.give(b, [ta, t6, tdt, t])
            tmp.give(f1, [t, dts["cs"]])
            tmp.give(f2, [t, dts["cs"]])
            dts["small"] = [t1, t2, tcs, td, tdt, tn]
            yield

        l_cs = line("l_cs")
        task(steps_dt())

        def conv(bank, t, ct, dst, dst_free):
            drain(lambda: len(tmp.free) >= 3)
            w = lambda k: CW[:, 32 * k + ct:32 * k + ct + 1]
            u, ut = tmp.take()
            t = fn_act(u[:, :], bank[:, :], ACT.Identity, t, ut, cw_tok, scale=w(2), bias=CW[:, 160 + ct:161 + ct])
            t = stt(u[:, 2:512], bank[:, 0:510], w(0), u[:, 2:512], ALU.mult, ALU.add, t)
            t = stt(u[:, 1:512], bank[:, 0:511], w(1), u[:, 1:512], ALU.mult, ALU.add, t)
            t = stt(u[:, 0:511], bank[:, 1:512], w(3), u[:, 0:511], ALU.mult, ALU.add, t)
            tb = stt(u[:, 0:510], bank[:, 2:512], w(4), u[:, 0:510], ALU.mult, ALU.add, t)
            h, ht = tmp.take()
            t = fn_act(h[:, :], u[:, :], ACT.Tanh, tb, ht)
            t = stt(dst, h[:, :], 1.0, u[:, :], ALU.add, ALU.mult, t, dst_free)
            tmp.give(u, t)
            tmp.give(h, t)
            return tb, t

        bf_tok, cf_tok, bt_tok, xs_tok, zs_tok = {}, {}, {}, {}, {}
        zs_free = [p2_done]
        ys_free = [p2_done]

        def turn_b(j, f):
            yield
            yield from room(side)
            bank, bt = side.take()
            for c in range(4):
                t = tr(bank[:, 128 * c:128 * c + 128], bf_buf[j % 2][:, f, 128 * c:128 * c + 128], 128, bf_tok[j, f], bt, sig=c == 3)
            t = copy_act(bt_buf[j % 2][:, f, :, :].rearrange("p c n -> p (c n)"), bank[:, :], t, buf_free[j % 2])
            side.give(bank, t)
            bt_tok[j, f] = t
            yield

        def turn_xs(j, f, src, t0):
            yield
            yield from room(side)
            bank, bt = side.take()
            for c in range(4):
                t = tr(bank[:, 128 * c:128 * c + 128], src[:, 128 * c:128 * c + 128], 128, t0, bt, sig=c == 3)
            tmp.give(src, t)
            t = copy_act(xs_buf[j % 2][:, :, 128 * f:128 * f + 128], bank[:, :].rearrange("p (c n) -> p c n", c=4), t, buf_free[j % 2])
            side.give(bank, t)
            xs_tok[j, f] = t
            yield

        def evac_bc(j):
            def evac(f, bank, t):
                if f < 2:
                    tb, t = conv(bank, t, 16 + 2 * j + f, bf_buf[j % 2][:, f, :], buf_free[j % 2])
                    bf_tok[j, f] = t
                    soon(turn_b(j, f))
                else:
                    tb, t = conv(bank, t, 24 + 2 * j + f - 2, cf_buf[j % 2][:, f - 2, :], buf_free[j % 2])
                    cf_tok[j, f - 2] = t
                return tb
            return evac

        def evac_xs(j):
            def evac(f, bank, t):
                drain(lambda: len(tmp.free) >= 3)
                o, ot = tmp.take()
                tb, t = conv(bank, t, 4 * j + f, o[:, :], ot)
                soon(turn_xs(j, f, o, t))
                return tb
            return evac

        def evac_z(j):
            def evac(t_, bank, t):
                z = ZS[:, t_, :]
                t = copy_act(z, bank[:, :], t, zs_free, scale=0.5)
                drain(lambda: len(tmp.free) >= 2)
                h, ht = tmp.take()
                t2 = fn_act(h[:, :], z, ACT.Tanh, t, ht)
                t2 = stt(z, h[:, :], 1.0, z, ALU.add, ALU.mult, t2)
                tmp.give(h, t2)
                zs_tok[j, t_] = t2
                return t
            return evac

        r64 = lambda ap: ap.rearrange("p (r d) -> p r d", d=64)
        l_cb = [line(f"l_cb{i}") for i in range(2)]
        cb_n = [0]
        prev_free = [p2_done]
        cb_free = [p2_done]
        l_ys = [line(f"l_ys{f}") for f in range(4)]
        gn = {}

        def cb_steps(j, gg, S_):
            while "small" not in dts or (j, 3) not in xs_tok or (j, gg) not in bt_tok:
                yield
            yield from room(side)
            yield from room(cb_sets)
            bank, bt = side.take()
            for c in range(4):
                t = mm(bank[:, 128 * c:128 * c + 128], bf_buf[j % 2][:, gg, 128 * c:128 * c + 128], cf_buf[j % 2][:, gg, 128 * c:128 * c + 128], True, True,
                       bf_tok[j, gg], cf_tok[j, gg], bt, sig=c == 3)
            b4 = bank[:, :].rearrange("p (c l) -> p c l", c=4)
            S_["cb"], free = cb_sets.take()
            S_["tu"] = tt(dve, S_["cb"][0][:, :, :], b4, mid(CST[:, C_TF:C_TF + 128], 4), ALU.mult, t, free)
            S_["tl"] = tt(dve, S_["cb"][1][:, :, :], b4, mid(CST[:, C_TB:C_TB + 128], 4), ALU.mult, t, free)
            side.give(bank, [S_["tu"], S_["tl"]])
            yield

        def state_steps(j, gg, d, S_, before):
            g = 2 * j + gg
            co = slice(256 * gg, 256 * gg + 256)
            while "small" not in dts or (j, 3) not in xs_tok or (before is not None and "off" not in before):
                yield
            xt = [xs_tok[j, f] for f in range(4)]
            for n in range(3):
                c = n if d == 0 else 3 - n
                hs = slice(32 * d + 4 * g, 32 * d + 4 * g + 4)
                yield from room(tmp, 5)
                xw, xwt = tmp.take()
                t = tt(pool, r64(xw[:, 0:256]), r64(xs_buf[j % 2][:, c, co]), bc(WST[:, c, hs], 64), ALU.mult, xwt, xt, dts["small"])
                if n:
                    pd, pdt = tmp.take()
                    t2 = tt(pool, r64(pd[:, 0:256]), r64(PREV[:, d, n - 1, :]), bc(CDEC[:, c, hs], 64), ALU.mult, S_["pv", d, n - 1], pdt)
                yield
                yield from room(side)
                bank, bt = side.take()
                t = mm(bank[:, 0:256], bt_buf[j % 2][:, gg, c, :], xw[:, 0:256], True, True, t, bt, bt_tok[j, gg], sig=True)
                tmp.give(xw, t)
                if n == 0:
                    t = copy_act(PREV[:, d, 0, :], bank[:, 0:256], t, prev_free)
                else:
                    t = tt(dve, PREV[:, d, n, :], bank[:, 0:256], pd[:, 0:256], ALU.add, t, t2, prev_free)
                    tmp.give(pd, t)
                side.give(bank, t)
                S_["pv", d, n] = t
                yield

        def head_steps(j, gg, r, S_):
            g = 2 * j + gg
            h = 4 * g + r
            yield from room(hn_ring)
            cb, cbt = hn_ring.take()
            ln = l_cb[h % 2]
            while "cs" not in dts:
                yield
            tc = ln.go(CSQ, lambda e: e.dma_start(cb[:, :], scr["cs"][h].partition_broadcast(128)), cbt, dts["cs"])
            yield
            while "tl" not in S_:
                yield
            small_t = dts["small"]
            yield from room(tmp, 5)
            a, at = tmp.take()
            b, bt_ = tmp.take()
            for c in range(4):
                k = slice(128 * c, 128 * c + 128)
                t1 = fn_act(a[:, k], cb[:, k], ACT.Identity, tc, at, small_t, bias=NCS[:, c, h:h + 1])
            for c in range(4):
                k = slice(128 * c, 128 * c + 128)
                t = stt(b[:, k], cb[:, 512 + 128 * c:640 + 128 * c], CS[:, c, 32 + h:33 + h], a[:, k], ALU.subtract, ALU.min, tc, t1, bt_)
            hn_ring.give(cb, [t1, t])
            yield
            te = fn_act(b[:, :], b[:, :], ACT.Exp, t)
            cbu, cbl = S_["cb"]
            for c in range(4):
                k = slice(128 * c, 128 * c + 128)
                t3 = fn_act(a[:, k], cbl[:, c, :], ACT.Copy, S_["tl"], t, scale=DT[:, c, 32 + h:33 + h])
            for c in range(4):
                k = slice(128 * c, 128 * c + 128)
                t4 = stt(a[:, k], cbu[:, c, :], DT[:, c, h:h + 1], a[:, k], ALU.mult, ALU.add, S_["tu"], t3)
            t4 = tt(dve, b[:, :], a[:, :], b[:, :], ALU.mult, t4, te)
            tmp.give(a, t4)
            yield
            yield from room(side)
            bank, bt = side.take()
            x = xs_buf[j % 2][:, :, 256 * gg + 64 * r:256 * gg + 64 * r + 64]
            for c in range(4):
                t = mm(bank[:, 64 * c:64 * c + 64], b[:, 128 * c:128 * c + 128], x[:, c, :], True, True, t4, [xs_tok[j, f] for f in range(4)], bt, sig=c == 3)
            tmp.give(b, t)
            y = YS[:, :, 256 * gg + 64 * r:256 * gg + 64 * r + 64]
            t = stt(y, x, DSK[:, h:h + 1], r64(bank[:, 0:256]), ALU.mult, ALU.add, t, ys_free)
            side.give(bank, t)
            S_["y", r] = t
            if all(("y", i) in S_ for i in range(4)):
                cb_sets.give(S_["cb"], [t3, t4])
            yield

        def off_steps(j, gg, d, S_):
            g = 2 * j + gg
            co = slice(256 * gg, 256 * gg + 256)
            for n in range(3):
                c = n + 1 if d == 0 else 2 - n
                hs = slice(32 * d + 4 * g, 32 * d + 4 * g + 4)
                while ("pv", d, n) not in S_ or not all(("y", i) in S_ for i in range(4)):
                    yield
                yield from room(side)
                yield from room(tmp, 4)
                bank, bt = side.take()
                t = mm(bank[:, 0:256], cf_buf[j % 2][:, gg, 128 * c:128 * c + 128], PREV[:, d, n, :], True, True, S_["pv", d, n], bt, sig=True)
                S_["pe", d] = t
                o, ot = tmp.take()
                t2 = tt(dve, r64(o[:, 0:256]), r64(bank[:, 0:256]), bc(ECS[:, c, hs], 64), ALU.mult, t, ot)
                side.give(bank, t2)
                y = YS[:, c, co]
                t2 = tt(pool, y, y, o[:, 0:256], ALU.add, t2, S_.get(("off", c)), [S_["y", i] for i in range(4)])
                S_["off", c] = t2
                tmp.give(o, t2)
                yield
            S_["done", d] = True
            if ("done", 0) in S_ and ("done", 1) in S_:
                S_["off"] = True
                prev_free[:] = [S_["pe", 0], S_["pe", 1]]

        def fin_steps(j, gg, S_):
            g = 2 * j + gg
            co = slice(256 * gg, 256 * gg + 256)
            while (j, 3) not in zs_tok or "off" not in S_:
                yield
            if gg == 0:
                gn[j] = load_gain(A["ssd_norm_2"][0][512 * j:512 * j + 512])
            rs = small(4)
            yield from room(tmp, 4)
            o, ot = tmp.take()
            for c in range(4):
                y = YS[:, c, co]
                t = tt(dve, y, y, ZS[:, c, co], ALU.mult, S_["off", c], zs_tok[j, c])
                t = fn_act(o[:, 0:256], y, ACT.Square, t, ot, accum_out=rs[:, c:c + 1])
                ot = t
            tmp.give(o, t)
            t = rstd(rs, rs, 256, RMS_EPS, t)
            yield
            yield
            for c in range(4):
                y = YS[:, c, co]
                yt[j, gg, c] = stt(y, y, rs[:, c:c + 1], gn[j][0][0][:, co], ALU.mult, ALU.mult, t, gn[j][1])
            yield
            if gg == 1:
                zs_free[:] = [yt[j, 1, 3]]
                gains.give(gn[j][0], [yt[j, 1, 3]])
                buf_free[j % 2][:] = [yt[j, 0, 3], yt[j, 1, 3], prev_free, S_["y", 3]]
                if j % 2:
                    buf_free[1].append(bt1_free)

        def out_steps(j, f):
            while (j, 1, 3) not in yt:
                yield
            yield from room(side)
            yield from room(tmp, 4)
            bank, bt = side.take()
            for c in range(4):
                t = tr(bank[:, 128 * c:128 * c + 128], YS[:, c, 128 * f:128 * f + 128], 128, yt[j, f // 2, c], bt, sig=c == 3)
            o, ot = tmp.take()
            t2 = copy_act(o[:, :], bank[:, :], t, ot)
            side.give(bank, t2)
            td = l_ys[f].go(CSQ, lambda e: e.dma_start(scr["ys"][128 * (4 * j + f):128 * (4 * j + f) + 128, :], o[:, :]), t2)
            tmp.give(o, td)
            yr.setdefault(j, []).append(t)
            if len(yr[j]) == 4:
                ys_free[:] = [yr[j]]
                if j == 3:
                    ys_done.extend([(ln.sem, ln.n) for ln in l_ys])
            yield

        yt, yr = {}, {}

        def ssd_tasks(j):
            if j:
                task(wait_for(lambda: len(yr.get(j - 1, [])) == 4))
            before = groups[-1] if groups else None
            for gg in range(2):
                S_ = {}
                groups.append(S_)
                task(cb_steps(j, gg, S_), state_steps(j, gg, 0, S_, before), state_steps(j, gg, 1, S_, before))
                task(*[head_steps(j, gg, r, S_) for r in range(4)])
                task(off_steps(j, gg, 0, S_), off_steps(j, gg, 1, S_), fin_steps(j, gg, S_))
                before = S_
            task(*[out_steps(j, f) for f in range(4)])

        def wait_for(cond):
            while not cond():
                yield

        groups = []
        for j in range(4):
            fm_block("bc", 4, 4, hH, hL, htok, evac_bc(j), rate=RA[0])
            fm_block("xs", 4, 4, hH, hL, htok, evac_xs(j), rate=RA[1])
            ssd_tasks(j)
            if j:
                drain(lambda: (j - 1, 1, 3) in yt)
            tm_block("z", 4, hH, hL, htok, evac_z(j), rate=RA[2])
        V2 = BT0[:, :, :, :].rearrange("p a c n -> p (a c n)").rearrange("p (t d) -> p t d", t=4)
        Q2 = [XS0[:, i, :] for i in range(4)] + [BF0[:, i, :] for i in range(2)] + [CF0[:, i, :] for i in range(2)]
        kf_tok, v2_tok, q2_tok = {}, {}, {}
        free0 = list(buf_free[0])

        banks = [main.take() for _ in range(4)]
        us = []
        for u in range(4):
            look_ahead()
            i, wh, wl, wt = take_unit("kv2")
            for f in range(2):
                for kk in range(2):
                    k = 2 * u + kk
                    w_h, w_l = wh[:, kk, 128 * f:128 * f + 128], wl[:, kk, 128 * f:128 * f + 128]
                    mm(banks[f][0][:, :], w_h, hH[:, k, :], k == 0, False, wt, htok, banks[f][1])
                    mm(banks[f][0][:, :], w_h, hL[:, k, :], False, False)
                    t = mm(banks[f][0][:, :], w_l, hH[:, k, :], False, k == 7, sig=k == 7)
                if u == 3:
                    kf_tok[f] = copy_act(KF[:, f, :], banks[f][0][:, :], t, p2_done)
                    main.give(banks[f][0], kf_tok[f])
                pump(RA[3])
            us.append((i, wh, wl, wt))
        for t_ in range(4):
            b = banks[2 + t_ // 2]
            for u in range(4):
                i, wh, wl, wt = us[u]
                for kk in range(2):
                    t = tm_mms(b[0][:, 256 * (t_ % 2):256 * (t_ % 2) + 256], 4, 4, u, kk, (256, 512), wh, wl, hH, hL, t_, wt, b[1], sig=(t_ == 3 and kk == 1))
                if t_ == 3:
                    release(i, t)
            if t_ % 2:
                r = copy_act(V2[:, t_ - 1:t_ + 1, :].rearrange("p t d -> p (t d)"), b[0][:, :], t, free0)
                v2_tok[t_ - 1] = v2_tok[t_] = r
                main.give(b[0], r)

        def evac_q2(j):
            def evac(f, bank, t):
                q2_tok[4 * j + f] = copy_act(Q2[4 * j + f], bank[:, :], t, free0, scale=0.125)
                return q2_tok[4 * j + f]
            return evac

        for j in range(2):
            fm_block("q2", 4, 4, hH, hL, htok, evac_q2(j), rate=RA[3])
        drain()
        P3.close()
        gains.give(bt1_gain, buf_free[1])

        ssd_done = [ys_free[0], buf_free[1], ys_done, zs_free[0]]
        SIGA = X[:, :, :].rearrange("p a (b c) -> p (a b) c", b=2)
        P4 = ExitStack()
        SIGB = sb("SIGB", [128, 8, 512], c=P4)
        P5 = ExitStack()
        ATT = sb("ATT", [128, 4, D], c=P5)
        sc_ring = Ring([sb(f"SC2{i}", [128, 384], c=P5) for i in range(4)])
        bias_ring = Ring([sb(f"BI2{i}", [128, 384], c=P5) for i in range(2)])
        pt_ring = Ring([sb(f"PTb{i}", [128, 384], c=P5) for i in range(3)])
        SINK = sb("SINK", [128, 16], c=P5)
        for rg in (sc_ring, bias_ring, pt_ring):
            for i in range(len(rg.free)):
                rg.free[i] = (rg.free[i][0], ssd_done)
        l_sink = line("l_sink")
        t_sink = l_sink.go(act, lambda e: e.dma_start(SINK[:, :], A["attn_sink_2"][0].partition_broadcast(128)), ssd_done)

        sg_tok = {}

        def evac_gate(j):
            def evac(f, bank, t):
                dst = (SIGA, SIGB)[j // 2][:, 4 * (j % 2) + f, :]
                t = fn_act(dst, bank[:, :], ACT.Tanh, t, ssd_done, scale=0.5)
                sg_tok[4 * j + f] = ts(pool, dst, dst, 0.5, 0.5, ALU.mult, ALU.add, t)
                return t
            return evac

        at_tok = []
        o2_tok = {}
        bias = {}

        def make_bias(h):
            yield from room(bias_ring)
            b, bt = bias_ring.take()
            t = ts(pool, b[:, :], CST[:, C_NB:C_NB + 384], float(2.0 ** (-8.0 * (h + 1) / 16)), None, ALU.mult, None, bt)
            bias[h] = [b, t, 0]
            yield

        def attend2(h, qt):
            kv = h // 4
            f, p0 = 4 * (kv // 2) + h % 4, 64 * (kv % 2)
            lo_k, hi_k = max(0, qt - 1), min(3, qt + 1)
            nk = hi_k - lo_k + 1
            n = 128 * nk
            bo = 128 * (lo_k - (qt - 1))
            while h not in bias:
                yield
            yield from room(side)
            yield from room(sc_ring)
            s, st = sc_ring.take()
            m = small(4)
            mx, nm, den, sk = m[:, 0:1], m[:, 1:2], m[:, 2:3], m[:, 3:4]
            bank, bt = side.take()
            t = mm(bank[:, 0:n], Q2[f][p0:p0 + 64, 128 * qt:128 * qt + 128], KF[p0:p0 + 64, kv // 2, 128 * lo_k:128 * lo_k + n], True, True,
                   q2_tok[f], kf_tok[kv // 2], bt, sig=True)
            t = ttr(s[:, 0:n], bank[:, 0:n], bias[h][0][:, bo:bo + n], SINK[:, h:h + 1], ALU.add, ALU.max, mx, t, st, bias[h][1], t_sink)
            side.give(bank, t)
            bias[h][2] += 1
            if bias[h][2] == 4:
                bias_ring.give(bias[h][0], t)
            t = ts(dve, nm, mx, -1.0, None, ALU.mult, None, t)
            te = fn_act(s[:, 0:n], s[:, 0:n], ACT.Exp, t, bias=nm, accum_out=den)
            t5 = fn_act(sk, SINK[:, h:h + 1], ACT.Exp, t, bias=nm)
            yield
            t5 = tt(dve, den, den, sk, ALU.add, t5, te)
            t5 = recip(den, den, t5)
            yield from room(side)
            yield from room(pt_ring)
            bank, bt = side.take()
            for k in range(nk):
                t = tr(bank[:, 128 * k:128 * k + 128], s[:, 128 * k:128 * k + 128], 128, te, bt, sig=k == nk - 1)
            sc_ring.give(s, t)
            pt, ptt = pt_ring.take()
            t2 = (copy_act if qt % 2 else copy_dve)(pt[:, 0:n], bank[:, 0:n], t, ptt)
            side.give(bank, t2)
            yield
            yield from room(side)
            bank, bt = side.take()
            for k in range(nk):
                t3 = mm(bank[:, 0:64], pt[:, 128 * k:128 * k + 128], V2[:, lo_k + k, 64 * kv:64 * kv + 64], k == 0, k == nk - 1,
                        t2, v2_tok[lo_k + k], bt, sig=k == nk - 1)
            pt_ring.give(pt, t3)
            t = ts(dve, ATT[:, qt, 64 * h:64 * h + 64], bank[:, 0:64], den, None, ALU.mult, None, t3, t5, ssd_done)
            side.give(bank, t)
            o2_tok[h, qt] = t
            yield

        for h in range(16):
            task(make_bias(h), *[attend2(h, qt) for qt in range(4)])
        for j in range(4):
            gates_mm = fm_block("gate", 4, 4, hH, hL, htok, evac_gate(j), rate=RA[4])

        mg_tok = {}
        for j in range(2):
            banks = [main.take() for _ in range(4)]
            for u in range(8):
                look_ahead()
                i, wh, wl, wt = take_unit("wssd")
                look_ahead()
                i2, yh, yl, ytk = take_unit("ys")
                for f in range(4):
                    for kk in range(2):
                        first, last = u == 0 and kk == 0, u == 7 and kk == 1
                        w_h, w_l = wh[:, kk, 128 * f:128 * f + 128], wl[:, kk, 128 * f:128 * f + 128]
                        mm(banks[f][0][:, :], w_h, yh[:, kk, :], first, False, wt, ytk, banks[f][1])
                        mm(banks[f][0][:, :], w_h, yl[:, kk, :], False, False)
                        t = mm(banks[f][0][:, :], w_l, yh[:, kk, :], False, last, sig=last or (f == 3 and kk == 1))
                    if last:
                        dst = SIGB[:, 4 * j + f, :]
                        mg_tok[4 * j + f] = tt(dve, dst, dst, banks[f][0][:, :], ALU.mult, t, sg_tok[8 + 4 * j + f])
                        main.give(banks[f][0], mg_tok[4 * j + f])
                    if f == 3:
                        release(i, t)
                        release(i2, t)
                    pump(RA[4])
        drain()
        for qt in range(4):
            d, _ = turn(ATT[:, qt, :], 8, hH, hL, 128 * qt, gates_mm, [o2_tok[h, qt] for h in range(16)])
            at_tok += d
        P5.close()
        P6 = ExitStack()
        gH = sb("gH", [128, 8, S], F32R, c=P6)
        gL = sb("gL", [128, 8, S], F32R, c=P6)
        merged = []

        def evac_attn(j):
            def evac(f, bank, t):
                k = 4 * j + f
                a = SIGA[:, k, :]
                t1 = tt(dve, a, a, bank[:, :], ALU.mult, t, sg_tok[k])
                t2 = tt(pool, a, a, SIGB[:, k, :], ALU.add, t1, mg_tok[k])
                th, tl = split_from(a, gH[:, k, :], gL[:, k, :], t2, at_tok)
                merged.extend([th, tl])
                return t1
            return evac

        for j in range(2):
            at_mm = fm_block("wattn", 4, 4, hH, hL, at_tok, evac_attn(j))
        dump("merged", SIGA, merged)
        l_xr = line("l_xr")
        x_back = l_xr.go(act, lambda e: e.dma_start(X[:, :, :].rearrange("p t d -> p (t d)"), scr["x"]), merged, x_saved)
        g_nc, tg_nc = load_gain(A["norm_cross_2"][0])
        htok = []

        def tail3(t_, tok, mm_tok):
            d, xtok[t_] = norm_turn(X[:, t_, :], g_nc[0], tg_nc, 128 * t_, hH, hL, at_mm, tok)
            htok.extend(d)

        wout_mm, _ = project(P6, "wout2", 4, gH, gL, merged, X, x_back, tail3, add=True)
        gains.give(g_nc, xtok[3])
        dump("x3", X[:, :, :], [xtok[i] for i in range(4)])
        p6_done = [wout_mm, merged]
        P6.close()
        P4.close()
        PA.close()

        P7 = ExitStack()
        QX = sb("QX", [128, 4, S], c=P7)
        KM = sb("KM", [128, 4, 256], c=P7)
        VM = sb("VM", [128, 2, 512], c=P7)
        oH = sb("oH", [128, 4, S], F32R, c=P7)
        oL = sb("oL", [128, 4, S], F32R, c=P7)
        OX = [sb(f"OX{i}", [128, 512], c=P7) for i in range(2)]
        ox_ring = Ring(OX)
        px_ring = Ring([sb(f"PX{i}", [128, 4, 256], c=P7) for i in range(2)])
        pxt_ring = Ring([sb(f"PXT{i}", [128, 512], c=P7) for i in range(2)])
        for rg in (ox_ring, px_ring, pxt_ring):
            for i in range(len(rg.free)):
                rg.free[i] = (rg.free[i][0], p6_done)
        l_k2 = line("l_k2")
        l_k2.go(act, lambda e: e.dma_start(KM[:, :, :].rearrange("p f t -> p (f t)"), scr["km"]), p6_done, kv_saved)
        kv_back = l_k2.go(act, lambda e: e.dma_start(VM[:, :, :].rearrange("p f t -> p (f t)"), scr["vm"]), p6_done)
        qx_tok = {}

        def evac_qx(f, bank, t):
            qx_tok[f] = copy_act(QX[:, f, :], bank[:, :], t, p6_done, scale=float(128 ** -0.5))
            return qx_tok[f]

        qx_mm = fm_block("xq", 4, 4, hH, hL, htok, evac_qx)
        g_nf, tg_nf = load_gain(A["norm_ffn_2"][0])
        us = []
        for u in range(4):
            look_ahead()
            us.append(take_unit("xo"))
        ftok = []

        def cross(qt):
            pair = []
            m = small(12)
            mx, nm, den = m[:, 0:4], m[:, 4:8], m[:, 8:12]
            for b in range(2):
                bank, bt = side.take()
                for r in range(2):
                    h = 2 * b + r
                    t = mm(bank[:, 256 * r:256 * r + 256], QX[:, h, 128 * qt:128 * qt + 128], KM[:, h, :], True, True, qx_tok[h], kv_back, bt, sig=r == 1)
                t1 = dve.do(lambda e, bank=bank, b=b: e.tensor_reduce(mx[:, 2 * b:2 * b + 2], bank[:, :].rearrange("p (h k) -> p h k", h=2), AX.X, ALU.max), t)
                pair.append((bank, t1))
            t = ts(dve, nm, mx, -1.0, None, ALU.mult, None, t1)
            p, pt_ = px_ring.take()
            te = []
            for h in range(4):
                te.append(fn_act(p[:, h, :], pair[h // 2][0][:, 256 * (h % 2):256 * (h % 2) + 256], ACT.Exp, t, pt_, bias=nm[:, h:h + 1], accum_out=den[:, h:h + 1]))
            side.give(pair[0][0], te[1])
            side.give(pair[1][0], te[3])
            rt = recip(den, den, te)
            yield
            ob, obt = side.take()
            for b in range(2):
                bank, bt = side.take()
                for r in range(2):
                    for k in range(2):
                        h = 2 * b + r
                        c = 256 * r + 128 * k
                        t = tr(bank[:, c:c + 128], p[:, h, 128 * k:128 * k + 128], 128, te[h], bt, sig=r == 1 and k == 1)
                q, qt_ = pxt_ring.take()
                t2 = (copy_act, copy_dve)[b](q[:, :], bank[:, :], t, qt_)
                side.give(bank, t2)
                for r in range(2):
                    h = 2 * b + r
                    for k in range(2):
                        c = 256 * r + 128 * k
                        t3 = mm(ob[:, 128 * h:128 * h + 128], q[:, c:c + 128], VM[:, k, 128 * h:128 * h + 128], k == 0, k == 1, t2, obt, kv_back, sig=r == 1 and k == 1)
                pxt_ring.give(q, t3)
            px_ring.give(p, t)
            o, ot = ox_ring.take()
            t = tt(dve, o[:, :].rearrange("p (h d) -> p h d", h=4), ob[:, :].rearrange("p (h d) -> p h d", h=4), bc(den, 128), ALU.mult, t3, rt, ot)
            side.give(ob, t)
            yield
            d, last = turn(o, 4, oH, oL, 128 * qt, p6_done, t)
            ox_ring.give(o, last)
            yield
            ad = []
            for h in range(2):
                bank, bt = main.take()
                for u in range(2):
                    i, wh, wl, wt = us[2 * h + u]
                    for kk in range(2):
                        t = tm_mms(bank[:, :], 4, 2, u, kk, (0, 512), wh, wl, oH, oL, qt, wt, d, bt, sig=qt == 3)
                    if qt == 3:
                        release(i, t)
                x = X[:, qt, 512 * h:512 * h + 512]
                ad.append(tt(dve, x, bank[:, :], x, ALU.add, t, xtok[qt]))
                main.give(bank, ad[-1])
            yield
            dd, xtok[qt] = norm_turn(X[:, qt, :], g_nf[0], tg_nf, 128 * qt, hH, hL, qx_mm, ad)
            ftok.extend(dd)

        def together(gens):
            gens = list(gens)
            live = []
            while gens or live:
                if gens:
                    live.append(gens.pop(0))
                for g in list(live):
                    try:
                        next(g)
                    except StopIteration:
                        live.remove(g)

        together(cross(qt) for qt in range(4))
        gains.give(g_nf, xtok[3])
        dump("x4", X[:, :, :], [xtok[i] for i in range(4)])
        p7_done = [ftok, [xtok[i] for i in range(4)]]
        P7.close()

        P8 = ExitStack()
        fH = sb("fH", [128, 8, S], F32R, c=P8)
        fL = sb("fL", [128, 8, S], F32R, c=P8)
        rl = Ring([sb(f"rl{i}", [128, 512], c=P8) for i in range(3)])
        for i in range(3):
            rl.free[i] = (rl.free[i][0], p7_done)
        g_fi, tg_fi = load_gain(A["norm_final_2"])
        f_free = [p7_done]
        xfree = [xtok[i] for i in range(4)]
        l_out = line("l_out")

        def tail4(t_, tok, mm_tok):
            ss = small(1)
            x = X[:, t_, :]
            t = square_sum(ss, x, tok)
            t = rstd(ss, ss, D, RMS_EPS, t)
            t = stt(x, x, ss, g_fi[0][:, :], ALU.mult, ALU.mult, t, tg_fi)
            l_out.go(sp, lambda e, t_=t_: e.dma_start(out[0, 128 * t_:128 * t_ + 128, :], X[:, t_, :]), t)

        for fc in range(NFF2):
            atok = []
            for b in range(2):
                def evac_up(f, bank, t, b=b):
                    s, st = rl.take()
                    tr1 = fn_act(s[:, :], bank[:, :], ACT.Relu, t, st)
                    r = tt(dve, s[:, :], s[:, :], bank[:, :], ALU.mult, tr1)
                    th, tl = split_from(s[:, :], fH[:, 4 * b + f, :], fL[:, 4 * b + f, :], r, f_free)
                    rl.give(s, [th, tl])
                    atok.extend([th, tl])
                    return r
                fm_block("up2", 4, 4, hH, hL, ftok, evac_up)
            if fc < NFF2 - 1:
                last, yt = project(P8, "down2", 4, fH, fL, atok, X, xfree, None, add=True, tail=False)
                f_free = [last]
                xfree = [yt[i] for i in range(4)]
            else:
                last, yt = project(P8, "down2", 4, fH, fL, atok, X, xfree, tail4, add=True)
        P8.close()
        sp.wait((l_out.sem, l_out.n), *ys_done, (l_cs.sem, l_cs.n), (l_kv.sem, l_kv.n), (l_xs.sem, l_xs.n))
        assert st_["use"] == len(units), (st_, len(units))

        block = ctx.enter_context(nc.Block())

        @block.sync
        def _(e):
            sp.emit(e)

        @block.gpsimd
        def _(e):
            pool.emit(e)

        @block.scalar
        def _(e):
            act.emit(e)

        @block.vector
        def _(e):
            dve.emit(e)

        @block.tensor
        def _(e):
            pe.emit(e)


_INS = ['x', 'positions', 'pre_mix_norm', 'w_in', 'sgu_ln_gain', 'sgu_ln_bias', 'sgu_w_spatial', 'sgu_b_spatial', 'attn_out_norm', 'sgu_out_norm', 'w_out', 'post_mix_norm', 'pre_ffn_norm', 'w_gate', 'w_up', 'w_down', 'post_ffn_norm', 'mem_2', 'norm_mix_2', 'w_in_2', 'attn_sink_2', 'conv_w_2', 'conv_b_2', 'dt_bias_2', 'a_log_2', 'd_skip_2', 'ssd_norm_2', 'w_attn_branch_2', 'w_ssd_branch_2', 'w_out_2', 'norm_cross_2', 'norm_mem_2', 'w_xq_2', 'w_xkv_2', 'w_xo_2', 'norm_ffn_2', 'w_up_2', 'w_down_2', 'norm_final_2']


def kernel(**inputs):
    import numpy as _np
    import concourse.bacc as _bacc
    from concourse import mybir as _mybir
    from concourse.bass_utils import run_bass_kernel_spmd as _run

    nc = _bacc.Bacc("TRN2", target_bir_lowering=False, num_devices=1)
    arrays, args = {}, {}
    for name in _INS + ["consts"]:
        a = constants() if name == "consts" else _np.ascontiguousarray(inputs[name])
        arrays[f"in_{name}_dram"] = a
        args[name] = nc.dram_tensor(f"in_{name}_dram", a.shape, _mybir.dt.from_np(a.dtype), kind="ExternalInput").ap()
    out = nc.dram_tensor("out_0_dram", (1, S, D), F32, kind="ExternalOutput").ap()
    scr = {n: nc.dram_tensor(f"scr_{n}_dram", shape, F32, kind="Internal").ap() for n, shape in SCRATCH.items()}
    build(nc, args, out, scr)
    r = _run(nc, [arrays], core_ids=[0])
    return r.results[0]["out_0_dram"]
```

```python
from collections import deque
from contextlib import ExitStack

import numpy as np

import concourse.bass as bass
from concourse import mybir

ALU = mybir.AluOpType
ACT = mybir.ActivationFunctionType
AX = mybir.AxisListType
F32 = mybir.dt.float32
F32R = mybir.dt.float32r
I32 = mybir.dt.int32

S = 512
D = 1024
RMS_EPS = 1e-6
LN_EPS = 1e-5
NEG = -1e30
TWO_PI = 2.0 * np.pi
PI_C1 = 6.28125
PI_C2 = float(np.float32(np.round((TWO_PI - PI_C1) * 2.0 ** 20) / 2.0 ** 20))
PI_C3 = float(np.float32(TWO_PI - PI_C1 - PI_C2))
MAGIC = 12582912.0
PI_IN = 3.1415925

NRAW, NHL, AHEAD = 3, 6, 4
NTB = 7
LIVE = 10
LAG = 0.2
SLACK = 0.3
CATCH = 2
CONV_ROOM = 2
RA = (5, 5, 5, 4, 4, 5)
SCRATCH = {"ys": (2048, 512), "cs": (32, 1024), "x": (128, 4096), "q": (128, 4096), "g": (128, 4096)}
EXTRA = ([], [("q", 0)], [("q", 1)], [("g", 0)], [("k", 0), ("g", 1)])
FF1 = [(0, 4), (4, 4), (8, 3)]
NFF2 = 4

C_ID, C_PERM, C_BT, C_NB, C_TF, C_TB, C_LL, C_FF, C_SF, C_AF = 0, 128, 256, 768, 1152, 1280, 1408, 1536, 1664, 1665
C_W = 1672


def constants():
    c = np.zeros((128, C_W), np.float32)
    i = np.arange(128)
    c[:, C_ID:C_ID + 128] = np.eye(128)
    perm = np.zeros((128, 128), np.float32)
    for p in range(128):
        m = p % 64
        if m < 16:
            perm[p - m + (m + 8) % 16, p] = 1.0
    c[:, C_PERM:C_PERM + 128] = perm
    for n, delta in enumerate((3, 2, 1, 0)):
        dist = 128 * delta + i[:, None] - i[None, :]
        count = ((dist >= 0) & (dist <= 128)).astype(int) + ((dist >= 0) & (dist % 4 == 0)) + ((dist >= 0) & (dist % 16 == 0))
        c[:, C_BT + 128 * n:C_BT + 128 * (n + 1)] = np.where(count > 0, np.log(np.maximum(count, 1)), NEG)
    rel = 128 + i[:, None] - np.arange(384)[None, :]
    c[:, C_NB:C_NB + 384] = np.where(np.abs(rel) <= 128, -np.abs(rel), NEG)
    c[:, C_TF:C_TF + 128] = i[:, None] <= i[None, :]
    c[:, C_TB:C_TB + 128] = i[:, None] >= i[None, :]
    c[127, C_LL:C_LL + 128] = 1.0
    c[0, C_FF:C_FF + 128] = 1.0
    inv = np.float32(500000.0) ** (-np.arange(0, 16, 2, dtype=np.float32) / np.float32(16))
    for p in range(128):
        m = p % 64
        if m < 16:
            c[p, C_AF] = inv[m % 8]
            c[p, C_SF] = -1.0 if m < 8 else 1.0
    return c


DUE = {}
CLOCK = [0.0]


def due(*tokens):
    t = 0.0
    for k in tokens:
        if isinstance(k, list):
            t = max(t, due(*k))
        elif k is not None:
            t = max(t, DUE.get((id(k[0]), k[1]), 0.0))
    return t


def width(ap):
    n = 1
    for d in ap.shape[1:]:
        n *= d
    return n


class Engine:

    def __init__(self, sem):
        self.sem, self.n, self.steps, self.seen = sem, 0, [], {}
        self.t = 0.0

    def wait(self, *tokens):
        self.t = max(self.t, due(*tokens))
        for t in tokens:
            if t is None:
                continue
            if isinstance(t, list):
                self.wait(*t)
                continue
            sem, value = t
            key = id(sem)
            if self.seen.get(key, 0) < value:
                self.seen[key] = value
                self.steps.append(lambda e, s=sem, v=value: e.wait_ge(s, v))

    def do(self, fn, *tokens, sig=True, cost=0.6):
        self.wait(*tokens)
        self.t += cost
        CLOCK[0] = max(CLOCK[0], self.t)
        if not sig:
            self.steps.append(fn)
            return None
        self.n += 1
        self.steps.append(lambda e: fn(e).then_inc(self.sem, 1))
        DUE[id(self.sem), self.n] = self.t + LAG
        return (self.sem, self.n)

    def emit(self, e):
        for s in self.steps:
            s(e)


class Line:

    def __init__(self, sem):
        self.sem, self.n = sem, 0

    def go(self, eng, fn, *tokens, cost=4.0):
        eng.wait(*tokens)
        self.n += 16
        eng.steps.append(lambda e: fn(e).then_inc(self.sem, 16))
        DUE[id(self.sem), self.n] = eng.t + cost
        CLOCK[0] = max(CLOCK[0], eng.t + cost)
        return (self.sem, self.n)


class Tiles(list):

    def __init__(self):
        super().__init__([] for _ in range(4))


class Parts(list):

    def __init__(self, n=8):
        super().__init__([] for _ in range(n))


def of(tok, *tiles, k=0):
    if isinstance(tok, Parts):
        return tok[k]
    return [tok[t] for t in tiles] if isinstance(tok, Tiles) else tok


class Ring:

    def __init__(self, bufs):
        self.free = deque((b, None) for b in bufs)

    def take(self):
        return self.free.popleft()

    def give(self, buf, tok):
        self.free.append((buf, tok))


def bc(ap, n):
    a, b = ap.shape[0], ap.shape[1]
    return ap.unsqueeze(2).to_broadcast([a, b, n])


def mid(ap, n):
    a, b = ap.shape[0], ap.shape[1]
    return ap.unsqueeze(1).to_broadcast([a, n, b])


def build(nc, A, out, scr):
    ctx = ExitStack()
    with ctx:
        def sem(name):
            return ctx.enter_context(nc.semaphore(name))

        def sb(name, shape, dt=F32, c=ctx):
            return c.enter_context(nc.sbuf_tensor(name, shape, dt))

        pe, act, dve, pool, sp = (Engine(sem(f"s_{n}")) for n in ("pe", "act", "dve", "pool", "sp"))
        psum = [ctx.enter_context(nc.psum_tensor(f"ps{i}", [128, 512], F32)) for i in range(8)]
        main = Ring(psum[:4])
        side = Ring(psum[4:])

        RAW = [sb(f"raw{i}", [128, 2, 512]) for i in range(NRAW)]
        HI = [sb(f"hi{i}", [128, 2, 512], F32R) for i in range(NHL)]
        LO = [sb(f"lo{i}", [128, 2, 512], F32R) for i in range(NHL)]
        hH = sb("hH", [128, 8, S], F32R)
        hL = sb("hL", [128, 8, S], F32R)
        X = sb("X", [128, 4, D])
        CST = sb("CST", [128, C_W])
        ST = sb("ST", [128, 256])
        half = sb("half", [128, 16])

        ident = CST[:, C_ID:C_ID + 128]

        def line(name):
            return Line(sem(name))

        l_cst = line("l_cst")
        l_id = line("l_id")
        CSQ = pool
        t_id = l_id.go(sp, lambda e: e.dma_start(CST[:, 0:128], A["consts"][:, 0:128]))
        t_half = pool.do(lambda e: e.memset(half[:, :], -0.5))

        stat = [0]

        def small(n):
            if stat[0] + n > 256:
                stat[0] = 0
            a = stat[0]
            stat[0] += n
            return ST[:, a:a + n]

        def mm(outp, lhsT, rhs, start, stop, *tok, sig=False):
            return pe.do(lambda e: e.matmul(outp, lhsT, rhs, start=start, stop=stop), *tok, sig=sig, cost=width(rhs) * (0.000417 if rhs.dtype == F32R else 0.00167))

        def tr(outp, inp, n, *tok, sig=False):
            return pe.do(lambda e: e.transpose(outp, inp, ident[0:n, 0:n]), *tok, sig=sig, cost=0.055)

        def copy_act(o, i, *tok, func=ACT.Copy, **kw):
            return act.do(lambda e: e.activation(o, i, func, **kw), *tok, cost=0.1 + 0.00083 * width(i) + 0.09 * len(kw))

        def tt(eng, o, a, b, op, *tok):
            return eng.do(lambda e: e.tensor_tensor(o, a, b, op), *tok, cost=0.1 + width(o) * (0.0022 if eng is pool else 0.00104))

        def ts(eng, o, a, s1, s2, op0, op1, *tok):
            if s2 is None:
                return eng.do(lambda e: e.tensor_scalar(o, a, s1, None, op0), *tok, cost=0.1 + 0.00104 * width(o))
            return eng.do(lambda e: e.tensor_scalar(o, a, s1, s2, op0, op1), *tok, cost=0.1 + 0.00104 * width(o))

        def stt(o, a, s, b, op0, op1, *tok):
            return dve.do(lambda e: e.scalar_tensor_tensor(out=o, in0=a, scalar=s, in1=b, op0=op0, op1=op1), *tok, cost=0.07 + 0.00104 * width(o))

        def fn_act(o, i, func, *tok, **kw):
            return act.do(lambda e: e.activation(o, i, func, **kw), *tok, cost=0.1 + 0.00083 * width(i) + 0.09 * len(kw))

        def ttr(o, a, b, init, op0, op1, acc, *tok):
            return dve.do(lambda e: e.tensor_tensor_reduce(o, a, b, 1.0, init, op0, op1, acc), *tok, cost=0.07 + 0.00104 * width(o))

        def copy_dve(o, i, *tok):
            return dve.do(lambda e: e.tensor_copy(o, i), *tok, cost=0.07 + 0.00104 * width(o))

        def recip(o, i, *tok):
            return dve.do(lambda e: e.reciprocal(o, i), *tok, cost=0.07 + 0.0064 * width(o))

        def rstd(o, ss, n, eps, *tok):
            k = ss.shape[1]
            t = ts(pool, o, ss, 1.0 / n, eps, ALU.mult, ALU.add, *tok)
            return tt(pool, o, o, half[:, 0:k], ALU.pow, t, t_half)

        def split_from(src, hi, lo, *tok):
            th = copy_act(hi, src, *tok)
            tl = tt(dve, lo, src, hi.bitcast(F32), ALU.subtract, th, *tok)
            return th, tl

        units = []

        def plan(tag, parts_of, n, cols=512):
            for u in range(n):
                units.append((tag, parts_of(u), cols))

        def rows(w, u, c0, c1):
            return w[256 * u:256 * u + 256, c0:c1].rearrange("(k p) n -> p k n", p=128)

        def cols_of(name, c0, c1):
            w = A[name][0]
            return lambda u: [(0, rows(w, u, c0, c1))]

        def cols2(n1, a0, a1, n2, b0, b1):
            w1, w2 = A[n1][0], A[n2][0]
            return lambda u: [(0, rows(w1, u, a0, a1)), (a1 - a0, rows(w2, u, b0, b1))]

        XBC = 1536 + 2048
        B0, C0 = XBC + 2048, XBC + 3072
        DT0 = XBC + 4096
        G0 = DT0 + 64
        for n, c in (("q", 0), ("k", 512), ("v", 1024), ("vs", 2048), ("u", 1536)):
            plan("in_" + n, cols_of("w_in", c, c + 512), 4)
        for h in range(2):
            plan("wout", cols_of("w_out", 512 * h, 512 * h + 512), 4)
        for b0, nb in FF1:
            for b in range(b0, b0 + nb):
                plan("gu", cols2("w_gate", 256 * b, 256 * b + 256, "w_up", 256 * b, 256 * b + 256), 4)
            for h in range(2):
                w = A["w_down"][0][256 * b0:256 * (b0 + nb), 512 * h:512 * h + 512]
                plan("down", lambda u, w=w: [(0, w[256 * u:256 * u + 256, :].rearrange("(k p) n -> p k n", p=128))], nb)
        def plan_q2(j):
            wq = A["w_in_2"][0]
            for u in range(4):
                units.append(("q2", [((k, b), wq[256 * u + 128 * k:256 * u + 128 * k + 128, 512 * j + 256 * b:512 * j + 256 * b + 256].rearrange(
                    "p (f c) -> p f c", c=64)) for k in range(2) for b in range(2)], 512))

        def plan_gate(j):
            plan("gate", cols_of("w_in_2", G0 + 512 * j, G0 + 512 * j + 512), 4)

        def plan_kv(_):
            plan("kv2", cols_of("w_in_2", 1024, 1536), 4)

        plan_extra = {"q": plan_q2, "g": plan_gate, "k": plan_kv}
        for j in range(4):
            plan("bc", cols2("w_in_2", B0 + 256 * j, B0 + 256 * j + 256, "w_in_2", C0 + 256 * j, C0 + 256 * j + 256), 4)
            if j == 0:
                plan("dt", cols_of("w_in_2", DT0, DT0 + 64), 4, 64)
            plan("xs", cols_of("w_in_2", XBC + 512 * j, XBC + 512 * j + 512), 4)
            for kind, n in EXTRA[j]:
                plan_extra[kind](n)
            plan("z", cols_of("w_in_2", 1536 + 512 * j, 1536 + 512 * j + 512), 4)
        for kind, n in EXTRA[4]:
            plan_extra[kind](n)
        for j in range(2, 4):
            plan_gate(j)
        for j in range(2):
            w = A["w_ssd_branch_2"][0]
            for u in range(8):
                units.append(("wssd", [(0, rows(w, u, 512 * j, 512 * j + 512))], 512))
                units.append(("ys", [(0, rows(scr["ys"], u, 0, 512))], 512))
        for j in range(2):
            plan("wattn", cols_of("w_attn_branch_2", 512 * j, 512 * j + 512), 4)
        for h in range(2):
            plan("wout2", cols_of("w_out_2", 512 * h, 512 * h + 512), 4)
        plan("xk", cols_of("w_xkv_2", 0, 512), 4)
        plan("xq", cols_of("w_xq_2", 0, 512), 4)
        plan("xv", cols_of("w_xkv_2", 512, 1024), 4)
        for h in range(2):
            plan("xo", cols_of("w_xo_2", 512 * h, 512 * h + 512), 2)
        for f in range(NFF2):
            for b in range(2):
                c = 1024 * f + 512 * b
                plan("up2", cols_of("w_up_2", c, c + 512), 4)
            for h in range(2):
                w = A["w_down_2"][0][1024 * f:1024 * f + 1024, 512 * h:512 * h + 512]
                plan("down2", lambda u, w=w: [(0, w[256 * u:256 * u + 256, :].rearrange("(k p) n -> p k n", p=128))], 4)

        l_raw = [line(f"l_raw{i}") for i in range(NRAW)]
        raw_free = [None] * NRAW
        hl_free = [None] * NHL
        unit_tok = {}
        ys_done = []
        st_ = {"load": 0, "conv": 0, "use": 0}

        def load_next():
            i = st_["load"]
            if i >= len(units):
                return
            st_["load"] += 1
            tag, parts, _ = units[i]
            r = i % NRAW
            dep = ys_done if tag == "ys" else None
            for c0, src in parts:
                if tag == "q2":
                    dst = RAW[r][:, c0[0], :].rearrange("p (f b c) -> p f b c", b=2, c=64)[:, :, c0[1], :]
                else:
                    dst = RAW[r][:, :, c0:c0 + src.shape[2]]
                t = l_raw[r].go(sp, lambda e, s=src, d=dst: e.dma_start(d, s), raw_free[r], dep)
            unit_tok[i] = t

        def convert_next():
            i = st_["conv"]
            if i >= len(units):
                return
            while half_done:
                finish_conversion()
            assert i < st_["load"] and i - NHL in released
            st_["conv"] += 1
            w = units[i][2]
            r, s = i % NRAW, i % NHL
            th = copy_act(HI[s][:, :, 0:w], RAW[r][:, :, 0:w], unit_tok[i], hl_free[s])
            half_done.append((i, r, s, w, th))

        half_done = deque()

        def finish_conversion():
            i, r, s, w, th = half_done.popleft()
            tl = tt(dve, LO[s][:, :, 0:w], RAW[r][:, :, 0:w], HI[s][:, :, 0:w].bitcast(F32), ALU.subtract, th, hl_free[s])
            raw_free[r] = [th, tl]
            unit_tok[i] = [th, tl]
            load_next()

        def take_unit(tag):
            i = st_["use"]
            assert units[i][0] == tag, (units[i][0], tag)
            st_["use"] += 1
            while st_["conv"] <= i:
                convert_next()
            while half_done and half_done[0][0] <= i:
                finish_conversion()
            return i, HI[i % NHL], LO[i % NHL], unit_tok[i]

        released = set(range(-NHL, 0))

        def release(i, tok):
            hl_free[i % NHL] = tok
            released.add(i)

        def look_ahead():
            n = 0
            while st_["conv"] < st_["use"] + AHEAD and st_["conv"] - NHL in released and n < CATCH and st_["conv"] < len(units):
                while half_done:
                    finish_conversion()
                if n and due(unit_tok[st_["conv"]]) > act.t:
                    break
                convert_next()
                n += 1

        waiting = deque()
        live = []
        urgent = [0]

        def task(*gens):
            waiting.extend(gens)

        def soon(gen, *tok):
            live.insert(min(urgent[0], len(live)), [gen, due(*tok)])
            urgent[0] += 1

        def queued():
            return pe.n + act.n + dve.n + pool.n + len(pe.steps) + len(pool.steps)

        def step(entry):
            n, CLOCK[0] = queued(), 0.0
            try:
                ready = next(entry[0])
                if ready is not None:
                    entry[1] = ready
                elif queued() > n:
                    entry[1] = CLOCK[0]
            except StopIteration:
                if live.index(entry) < urgent[0]:
                    urgent[0] -= 1
                live.remove(entry)
            return queued() > n

        def pump(n=1, any_time=False):
            if half_done and due(half_done[0][4]) <= dve.t + 0.1:
                finish_conversion()
            while n > 0:
                while len(live) < LIVE + urgent[0] and waiting:
                    live.append([waiting.popleft(), 0.0])
                cand = list(live)
                if any_time:
                    cand.sort(key=lambda a: a[1])
                for a in cand:
                    if (any_time or a[1] <= pe.t + SLACK) and step(a):
                        break
                else:
                    return
                n -= 1

        def drain(until=lambda: False):
            n = 0
            while (live or waiting) and not until():
                pump(1, True)
                n += 1
                assert n < 5000

        def room(ring, n=1):
            while len(ring.free) < n:
                yield

        tails = []

        def step_tails(last=3, force=False):
            moved = False
            for a in sorted((a for a in tails if a[0] <= last), key=lambda a: a[2]) if force else list(tails):
                if a[0] > last or (a[2] > pe.t + SLACK and (moved or not force)):
                    continue
                n, CLOCK[0] = queued(), 0.0
                try:
                    next(a[1])
                except StopIteration:
                    tails.remove(a)
                if queued() > n:
                    a[2], moved = CLOCK[0], True

        def end_tails(last=3):
            while any(a[0] <= last for a in tails):
                step_tails(last, True)

        def fm_halves(tag, nu, nf, act_h, act_l, a_tok, evac, rate=0, then=None):
            banks = [main.take() for _ in range(nf)]
            us = []
            end_tails(1)
            for hf in range(2):
                if hf:
                    end_tails()
                    if then:
                        then()
                q = slice(256 * hf, 256 * hf + 256)
                tok = of(a_tok, 2 * hf, 2 * hf + 1)
                for u in range(nu):
                    if not hf:
                        look_ahead()
                        us.append(take_unit(tag))
                    i, wh, wl, wt = us[u]
                    for f in range(nf):
                        bank, bt = banks[f]
                        for kk in range(2):
                            k = 2 * u + kk
                            first, last = k == 0, k == 2 * nu - 1
                            w_h, w_l = wh[:, kk, 128 * f:128 * f + 128], wl[:, kk, 128 * f:128 * f + 128]
                            mm(bank[:, q], w_h, act_h[:, k, q], first, False, wt, tok, bt if first else None)
                            mm(bank[:, q], w_h, act_l[:, k, q], False, False)
                            t = mm(bank[:, q], w_l, act_h[:, k, q], False, last, sig=hf and (last or (f == nf - 1 and kk == 1)))
                        if last and hf:
                            main.give(bank, evac(f, bank, t))
                        if f % 2:
                            pump(rate)
                        if not hf:
                            step_tails()
                    if hf:
                        release(i, t)
                        look_ahead()
            return t

        def fm_tiles(tag, nu, nf, act_h, act_l, a_tok, evac, rate=0):
            us = []
            for f in range(nf):
                bank, bt = main.take()
                for u in range(nu):
                    if f == 0:
                        look_ahead()
                        us.append(take_unit(tag))
                    i, wh, wl, wt = us[u]
                    for kk in range(2):
                        k = 2 * u + kk
                        first, last = k == 0, k == 2 * nu - 1
                        w_h, w_l = wh[:, kk, 128 * f:128 * f + 128], wl[:, kk, 128 * f:128 * f + 128]
                        mm(bank[:, :], w_h, act_h[:, k, :], first, False, wt, a_tok, bt if first else None)
                        mm(bank[:, :], w_h, act_l[:, k, :], False, False)
                        t = mm(bank[:, :], w_l, act_h[:, k, :], False, last, sig=last or (f == nf - 1 and kk == 1))
                    if f == nf - 1:
                        release(i, t)
                        look_ahead()
                    if u == nu - 1:
                        main.give(bank, evac(f, bank, t))
                    pump(rate)
            return t

        def fm_block(tag, nu, nf, act_h, act_l, a_tok, evac, rate=0, N=S, with_tails=False):
            banks = [main.take() for _ in range(nf)]
            for u in range(nu):
                look_ahead()
                i, wh, wl, wt = take_unit(tag)
                for f in range(nf):
                    bank, bt = banks[f]
                    for kk in range(2):
                        k = 2 * u + kk
                        first, last = k == 0, k == 2 * nu - 1
                        w_h, w_l = wh[:, kk, 128 * f:128 * f + 128], wl[:, kk, 128 * f:128 * f + 128]
                        mm(bank[:, 0:N], w_h, act_h[:, k, 0:N], first, False, wt, a_tok, bt if first else None)
                        mm(bank[:, 0:N], w_h, act_l[:, k, 0:N], False, False)
                        t = mm(bank[:, 0:N], w_l, act_h[:, k, 0:N], False, last, sig=last or (f == nf - 1 and kk == 1))
                    if last:
                        main.give(bank, evac(f, bank, t))
                    if f == nf - 1:
                        release(i, t)
                    if with_tails:
                        step_tails()
                    pump(rate)
            return t

        def tm_mms(bank, ntok, nu, u, kk, w, wh, wl, act_h, act_l, t, *tok, sig=False):
            k = 2 * u + kk
            first, last = k == 0, k == 2 * nu - 1
            a_h, a_l = act_h[:, k, 128 * t:128 * t + 128], act_l[:, k, 128 * t:128 * t + 128]
            mm(bank, a_h, wh[:, kk, w[0]:w[1]], first, False, *tok)
            mm(bank, a_h, wl[:, kk, w[0]:w[1]], False, False)
            return mm(bank, a_l, wh[:, kk, w[0]:w[1]], False, last, sig=sig or last)

        def tm_block(tag, nu, act_h, act_l, a_tok, evac, rate=0, ntok=4, tail=False):
            banks = [main.take() for _ in range(ntok)]
            if tail:
                us = []
                for u in range(nu):
                    look_ahead()
                    us.append(take_unit(tag))
                for t in range(ntok):
                    bank, bt = banks[t]
                    for u in range(nu):
                        i, wh, wl, wt = us[u]
                        for kk in range(2):
                            tok = tm_mms(bank[:, :], ntok, nu, u, kk, (0, 512), wh, wl, act_h, act_l, t, wt, of(a_tok, t, k=2 * u + kk), bt, sig=(t == ntok - 1 and kk == 1))
                        if t == ntok - 1:
                            release(i, tok)
                            look_ahead()
                        step_tails()
                    main.give(bank, evac(t, bank, tok))
                return tok
            for u in range(nu):
                look_ahead()
                i, wh, wl, wt = take_unit(tag)
                for t in range(ntok):
                    bank, bt = banks[t]
                    for kk in range(2):
                        first = u == 0 and kk == 0
                        tok = tm_mms(bank[:, :], ntok, nu, u, kk, (0, 512), wh, wl, act_h, act_l, t, wt, of(a_tok, t, k=2 * u + kk), bt if first else None, sig=(t == ntok - 1 and kk == 1))
                    if u == nu - 1:
                        main.give(bank, evac(t, bank, tok))
                    if t == ntok - 1:
                        release(i, tok)
                    pump(rate)
            return tok

        hn_ring = Ring([sb(f"hn{i}", [128, D]) for i in range(2)])
        l_gain = [line(f"l_gain{i}") for i in range(3)]
        gains = Ring([(sb(f"gain{i}", [128, D]), l_gain[i]) for i in range(2)])

        def load_gain(*parts):
            (g, ln), free = gains.take()
            c = 0
            for p in parts:
                n = p.shape[-1]
                t = ln.go(sp, lambda e, p=p, c=c, n=n: e.dma_start(g[:, c:c + n], p.partition_broadcast(128)), free)
                c += n
            return (g, ln), t

        junk = sb("junk", [128, D], mybir.dt.bfloat16)
        junk_tok = [None]

        def square_sum(o, x, *tok):
            junk_tok[0] = fn_act(junk[:, 0:x.shape[1]], x, ACT.Square, junk_tok[0], *tok, accum_out=o)
            return junk_tok[0]

        def turn(src, nk, hi, lo, t0, h_free, *tok):
            done = []
            for b in range(0, nk, 4):
                n = min(4, nk - b)
                bank, bt = side.take()
                for k in range(n):
                    t = tr(bank[:, 128 * k:128 * k + 128], src[:, 128 * (b + k):128 * (b + k) + 128], 128, t_id, bt if k == 0 else None, *tok, sig=k == n - 1)
                v = bank[:, 0:128 * n].rearrange("p (k t) -> p k t", k=n)
                th, tl = split_from(v, hi[:, b:b + n, t0:t0 + 128], lo[:, b:b + n, t0:t0 + 128], t, h_free)
                side.give(bank, [th, tl])
                done += [th, tl]
            return done, t

        def norm_steps(x, gain, g_tok, t0, hi, lo, h_free, dst, *tok):
            ss = small(1)
            t = square_sum(ss, x, *tok)
            t = rstd(ss, ss, D, RMS_EPS, t)
            yield
            yield from room(hn_ring)
            (hn, ht) = hn_ring.take()
            t = stt(hn[:, :], x, ss, gain[:, :], ALU.mult, ALU.mult, t, ht, g_tok)
            yield
            for b in range(2):
                yield from room(side)
                d, last = turn(hn[:, 512 * b:512 * b + 512], 4, hi[:, 4 * b:4 * b + 4, :], lo[:, 4 * b:4 * b + 4, :], t0, h_free, t)
                dst.extend(d)
                if b:
                    hn_ring.give(hn, last)
                yield

        def together(gens):
            gens = list(gens)
            running = []
            while gens or running:
                if gens:
                    running.append(gens.pop(0))
                for g in list(running):
                    try:
                        next(g)
                    except StopIteration:
                        running.remove(g)

        l_x = [line(f"l_x{i}") for i in range(4)]
        t_x = [l_x[t].go(act, lambda e, t=t: e.dma_start(X[:, t, :], A["x"][0, 128 * t:128 * t + 128, :])) for t in range(4)]
        g_pre, tg_pre = load_gain(A["pre_mix_norm"][0])
        for _ in range(NRAW):
            load_next()
        t_cst = l_cst.go(sp, lambda e: e.dma_start(CST[:, 128:C_W], A["consts"][:, 128:C_W]))
        htok = Tiles()
        together(norm_steps(X[:, t, :], g_pre[0], tg_pre, 128 * t, hH, hL, None, htok[t], t_x[t]) for t in range(4))
        gains.give(g_pre, list(htok))

        P1 = ExitStack()
        Q = sb("Q", [128, 4, S], c=P1)
        K = sb("K", [128, 4, S], c=P1)
        V = sb("V", [128, 4, 512], c=P1)
        VS = sb("VS", [128, 4, 512], c=P1)
        MIX = sb("MIX", [128, 4, D], c=P1)
        RC = sb("RC", [128, S], c=P1)
        RS = sb("RS", [128, S], c=P1)
        TMPA = [sb(f"tmpa{i}", [128, 512], c=P1) for i in range(4)]
        tmp = Ring(TMPA)
        WS = MIX[:, 0:2, 0:512]
        WT = sb("WT", [128, 8, 128], c=P1)
        SB_ = sb("SBs", [128, 8], c=P1)
        l_p1 = line("l_p1")
        def ld(o, i, *tok, slow=False):
            return l_p1.go(sp, lambda e: e.dma_start(o, i, allow_slow_non_contiguous=slow), *tok)

        g_ln, tg_ln = load_gain(A["sgu_ln_gain"][0], A["sgu_ln_bias"][0])
        posi, pt_ = tmp.take()
        ld(SB_[:, :], A["sgu_b_spatial"][0].rearrange("g i -> i g"), slow=True)
        POSI = posi[:, :].bitcast(I32)
        ld(POSI, A["positions"][0].partition_broadcast(128))
        ld(MIX[:, 0, :].rearrange("p (g j) -> p g j", g=8), A["sgu_w_spatial"][0].rearrange("g i j -> i g j"))
        t_p1 = (l_p1.sem, l_p1.n)

        def rotary_tables():
            a, at = tmp.take()
            b, bt_ = tmp.take()
            t = dve.do(lambda e: e.tensor_copy(a[:, :], POSI), t_p1, at)
            tmp.give(posi, t)
            t = ts(dve, a[:, :], a[:, :], CST[:, C_AF:C_AF + 1], None, ALU.mult, None, t, t_cst)
            t = ts(dve, b[:, :], a[:, :], float(np.float32(1.0 / TWO_PI)), MAGIC, ALU.mult, ALU.add, t, bt_)
            t = ts(dve, b[:, :], b[:, :], MAGIC, None, ALU.subtract, None, t)
            for c in (PI_C1, PI_C2, PI_C3):
                t = stt(a[:, :], b[:, :], -c, a[:, :], ALU.mult, ALU.add, t)
            t = ts(dve, a[:, :], a[:, :], PI_IN, -PI_IN, ALU.min, ALU.max, t)
            yield
            t1 = act.do(lambda e: e.activation(RS[:, :], a[:, :], ACT.Sin), t)
            t2 = act.do(lambda e: e.activation(b[:, :], a[:, :], ACT.Abs), t)
            t2 = ts(dve, b[:, :], b[:, :], -1.0, float(np.pi / 2), ALU.mult, ALU.add, t2)
            t2 = act.do(lambda e: e.activation(RC[:, :], b[:, :], ACT.Sin), t2)
            t1 = ts(dve, RS[:, :], RS[:, :], CST[:, C_SF:C_SF + 1], None, ALU.mult, None, t1)
            rot_tok.extend([t1, t2])
            tmp.give(a, [t1, t2])
            tmp.give(b, t2)
            yield

        rot_tok = []
        task(rotary_tables())
        q_tok, k_tok, v_tok = {}, {}, {}

        def rope(dst, f, tok_d, t0):
            while not rot_tok:
                yield
            yield from room(side)
            bank, bt = side.take()
            t = mm(bank[:, :], CST[:, C_PERM:C_PERM + 128], dst[:, f, :], True, True, t0, bt, t_cst, sig=True)
            yield from room(tmp)
            a, at = tmp.take()
            t1 = tt(dve, a[:, :], bank[:, :], RS[:, :], ALU.mult, t, at, rot_tok)
            side.give(bank, t1)
            t2 = tt(pool, dst[:, f, :], dst[:, f, :], RC[:, :], ALU.mult, t, rot_tok)
            t3 = tt(pool, dst[:, f, :], dst[:, f, :], a[:, :], ALU.add, t1, t2)
            tmp.give(a, t3)
            tok_d[f] = t3
            yield

        def evac_rope(dst, tok_d, scale):
            def evac(f, bank, t):
                r = copy_act(dst[:, f, :], bank[:, :], t, scale=scale)
                task(rope(dst, f, tok_d, r))
                return r
            return evac

        def evac_v(t_, bank, t):
            v_tok[t_] = copy_act(V[:, t_, :], bank[:, :], t)
            return v_tok[t_]

        fm_halves("in_q", 4, 4, hH, hL, htok, evac_rope(Q, q_tok, 0.125), rate=1)
        fm_block("in_k", 4, 4, hH, hL, htok, evac_rope(K, k_tok, 1.0), rate=1)
        tm_block("in_v", 4, hH, hL, htok, evac_v, rate=1)

        SCO = tmp
        PT = Ring([sb(f"pt{i}", [128, 512], c=P1) for i in range(3)])
        att_tok = {}
        g_mix, tg_mix = load_gain(A["attn_out_norm"][0], A["sgu_out_norm"][0])

        def attend(qt, h):
            n = 128 * (qt + 1)
            f, p0 = h // 2, 64 * (h % 2)
            while f not in q_tok or f not in k_tok or qt not in v_tok:
                yield
            yield due(q_tok[f], k_tok[f])
            yield from room(side)
            yield from room(SCO, 2)
            bank, bt = side.take()
            t = mm(bank[:, 0:n], Q[p0:p0 + 64, f, 128 * qt:128 * qt + 128], K[p0:p0 + 64, f, 0:n], True, True, q_tok[f], k_tok[f], bt, sig=True)
            s, s_t = SCO.take()
            m = small(3)
            t = ttr(s[:, 0:n], bank[:, 0:n], CST[:, C_BT + 128 * (3 - qt):C_BT + 512], -3e38, ALU.add, ALU.max, m[:, 0:1], t, s_t)
            side.give(bank, t)
            t = ts(dve, m[:, 1:2], m[:, 0:1], -1.0, None, ALU.mult, None, t)
            yield
            te = fn_act(s[:, 0:n], s[:, 0:n], ACT.Exp, t, bias=m[:, 1:2], accum_out=m[:, 2:3])
            yield
            r = recip(m[:, 2:3], m[:, 2:3], te)
            yield from room(side)
            yield from room(PT)
            bank, bt = side.take()
            for k in range(qt + 1):
                t = tr(bank[:, 128 * k:128 * k + 128], s[:, 128 * k:128 * k + 128], 128, te, bt, sig=k == qt)
            SCO.give(s, t)
            pt, pt_t = PT.take()
            t = (copy_act if h % 2 else copy_dve)(pt[:, 0:n], bank[:, 0:n], t, pt_t)
            side.give(bank, t)
            yield
            yield from room(side)
            bank, bt = side.take()
            for k in range(qt + 1):
                t2 = mm(bank[:, 0:64], pt[:, 128 * k:128 * k + 128], V[:, k, 64 * h:64 * h + 64], k == 0, k == qt, t, v_tok[k], bt, sig=k == qt)
            PT.give(pt, t2)
            t = ts(dve, MIX[:, qt, 64 * h:64 * h + 64], bank[:, 0:64], m[:, 2:3], None, ALU.mult, None, t2, r, wt_tok)
            side.give(bank, t)
            head_tok[qt, h] = t
            yield

        def attend_norm(qt):
            while (qt, 7) not in head_tok:
                yield
            yield due(*[head_tok[qt, h] for h in range(8)])
            o = MIX[:, qt, 0:512]
            ss = small(1)
            t = square_sum(ss, o, [head_tok[qt, h] for h in range(8)])
            t = rstd(ss, ss, 512, RMS_EPS, t)
            yield
            att_tok[qt] = stt(o, o, ss, g_mix[0][:, 0:512], ALU.mult, ALU.mult, t, tg_mix)
            yield

        head_tok = {}
        wt_tok = []

        def spatial_weights():
            w = MIX[:, 0, :].rearrange("p (g j) -> p g j", g=8)
            t = tt(pool, w, w, mid(CST[:, C_TB:C_TB + 128], 8), ALU.mult, t_p1, t_cst)
            for b in range(2):
                bank, bt = side.take()
                for g in range(4):
                    t2 = tr(bank[:, 128 * g:128 * g + 128], w[:, 4 * b + g, :], 128, t, bt, sig=g == 3)
                t2 = copy_act(WT[:, 4 * b:4 * b + 4, :].rearrange("p g i -> p (g i)"), bank[:, :], t2)
                side.give(bank, t2)
                wt_tok.append(t2)
            yield

        task(spatial_weights())
        drain()
        for qt in range(4):
            task(*[attend(qt, h) for h in range(8)], attend_norm(qt))

        vs_tok, u_tok = {}, {}

        def ln_tile(t_, t0):
            v = VS[:, t_, :]
            st6, mv = small(6), small(2)
            t = dve.do(lambda e: e.bn_stats(st6, v), t0)
            t = dve.do(lambda e: e.bn_aggr(mv, st6), t)
            t = rstd(mv[:, 1:2], mv[:, 1:2], 1.0, LN_EPS, t)
            t = ts(dve, v, v, mv[:, 0:1], mv[:, 1:2], ALU.subtract, ALU.mult, t)
            t = tt(pool, v, v, g_ln[0][:, 0:512], ALU.mult, t, tg_ln)
            t = tt(pool, v, v, g_ln[0][:, 512:1024], ALU.add, t)
            vs_tok[t_] = t

        def evac_vs(t_, bank, t):
            t = act.do(lambda e: e.activation(VS[:, t_, :], bank[:, :], ACT.Gelu), t)
            ln_tile(t_, t)
            return t

        def evac_u(t_, bank, t):
            u_tok[t_] = act.do(lambda e: e.activation(MIX[:, t_, 512:1024], bank[:, :], ACT.Gelu), t, wt_tok)
            return u_tok[t_]

        tm_block("in_vs", 4, hH, hL, htok, evac_vs, rate=RA[5])
        in_done = tm_block("in_u", 4, hH, hL, htok, evac_u, rate=RA[5])

        sgu_tok = {}

        sp_tok = {}

        def spatial(g):
            yield from room(side)
            bank, bt = side.take()
            t = mm(bank[:, 0:256].rearrange("p (n c) -> p n c", n=4), WT[:, g, :], VS[:, :, 64 * g:64 * g + 64], True, True,
                   [vs_tok[i] for i in range(4)], wt_tok, bt, sig=True)
            u = MIX[:, :, 512 + 64 * g:576 + 64 * g]
            t = stt(u, bank[:, 0:256].rearrange("p (n c) -> p n c", n=4), SB_[:, g:g + 1], u, ALU.add, ALU.mult, t, [u_tok[i] for i in range(4)], t_p1)
            side.give(bank, t)
            sp_tok[g] = t
            yield

        def spatial_norm(t_):
            while len(sp_tok) < 8:
                yield
            yield due(*sp_tok.values())
            ss = small(1)
            o = MIX[:, t_, 512:1024]
            t2 = square_sum(ss, o, [sp_tok[g] for g in range(8)])
            t2 = rstd(ss, ss, 512, RMS_EPS, t2)
            yield
            sgu_tok[t_] = stt(o, o, ss, g_mix[0][:, 512:1024], ALU.mult, ALU.mult, t2, tg_mix)
            yield

        def turn_mix(t_):
            while t_ not in sgu_tok or t_ not in att_tok:
                yield
            yield due(sgu_tok[t_], att_tok[t_])
            for b in range(2):
                yield from room(side)
                d, turned[t_] = turn(MIX[:, t_, 512 * b:512 * b + 512], 4, hH[:, 4 * b:4 * b + 4, :], hL[:, 4 * b:4 * b + 4, :], 128 * t_, in_done, sgu_tok[t_], att_tok[t_])
                mtk[t_].extend(d)
                yield

        mtk = Tiles()
        turned = {}
        for g in range(8):
            soon(spatial(g), vs_tok[3], u_tok[3])
        for t_ in range(4):
            soon(spatial_norm(t_))
        task(*[turn_mix(t_) for t_ in range(4)])

        wout_banks = [main.take() for _ in range(4)]
        us = []
        for u in range(4):
            look_ahead()
            us.append(take_unit("wout"))
        wout_t = []
        for t_ in range(4):
            drain(lambda: len(mtk[t_]) == 4)
            for u in range(4):
                i, wh, wl, wt = us[u]
                for kk in range(2):
                    t = tm_mms(wout_banks[t_][0][:, :], 4, 4, u, kk, (0, 512), wh, wl, hH, hL, t_, wt, mtk[t_], wout_banks[t_][1], sig=(t_ == 3 and kk == 1))
                if t_ == 3:
                    release(i, t)
                    look_ahead()
                pump(RA[5])
            wout_t.append(t)
        drain()
        turned = list(turned.values())
        gains.give(g_mix, [list(sgu_tok.values()), list(att_tok.values())])
        gains.give(g_ln, [vs_tok[i] for i in range(4)])

        P1.close()

        def project(P, tag, nu, a_h, a_l, a_tok, Y, yfree, tail_fn, add=False, tail=True, rate=0, first=True):
            ytok = {}

            def evac(h):
                def f(t_, bank, t):
                    y = Y[:, t_, 512 * h:512 * h + 512]
                    if add:
                        r = tt(dve, y, bank[:, :], y, ALU.add, t, yfree)
                    else:
                        r = copy_act(y, bank[:, :], t, yfree)
                    ytok.setdefault(t_, []).append(r)
                    if h == 1 and tail_fn:
                        tails.append([t_, tail_fn(t_, list(ytok[t_])), due(r)])
                    return r
                return f

            if first:
                tm_block(tag, nu, a_h, a_l, a_tok, evac(0), rate=rate)
            else:
                for t_ in range(4):
                    main.give(wout_banks[t_][0], evac(0)(t_, wout_banks[t_][0], wout_t[t_]))
            last = tm_block(tag, nu, a_h, a_l, a_tok, evac(1), rate=rate, tail=tail)
            return last, ytok

        def post_add(t_, tok, y, gain, g_tok):
            ss = small(1)
            ts_ = square_sum(ss, y, tok)
            t = rstd(ss, ss, D, RMS_EPS, ts_)
            yield
            ty = tt(dve, y, y, gain[:, :], ALU.mult, ts_, g_tok)
            xtok[t_] = stt(X[:, t_, :], y, ss, X[:, t_, :], ALU.mult, ALU.add, t, ty)

        P2 = ExitStack()
        Y = sb("Y", [128, 4, D], c=P2)
        aH = sb("aH", [128, 8, S], F32R, c=P2)
        aL = sb("aL", [128, 8, S], F32R, c=P2)
        SG = Ring([sb(f"sg{i}", [128, 512], c=P2) for i in range(2)])
        g_post, tg_post = load_gain(A["post_mix_norm"][0])
        g_ffn, tg_ffn = load_gain(A["pre_ffn_norm"][0])
        htok = Tiles()
        xtok = {}

        def tail1(t_, tok):
            yield from post_add(t_, tok, Y[:, t_, :], g_post[0], tg_post)
            yield from norm_steps(X[:, t_, :], g_ffn[0], tg_ffn, 128 * t_, hH, hL, tok, htok[t_], xtok[t_])

        project(P2, "wout", 4, hH, hL, mtk, Y, turned, tail1, first=False)

        NCS = CST[:, C_BT:C_BT + 128].rearrange("p (c h) -> p c h", c=4)
        PAR = CST[:, C_BT + 128:C_BT + 288]
        CW = CST[:, C_BT + 288:C_BT + 480]
        DTB, ALOG, DSK = PAR[:, 0:64], PAR[:, 64:128], PAR[:, 128:160]
        CR1, CR2 = CST[:, C_PERM:C_PERM + 128], CST[0:64, C_BT:C_BT + 128]
        l_par = line("l_par")

        def ldp(o, i, *tok):
            return l_par.go(pool, lambda e: e.dma_start(o, i), *tok)

        wrows = A["conv_w_2"][0].rearrange("k (t p) -> (k t) p", p=128)
        ldp(CR1, wrows[0:128, :], turned, list(mtk))
        ldp(CR2[0:32, :], wrows[128:160, :])
        ldp(CR2[32:64, :], A["conv_b_2"][0].rearrange("(t p) -> t p", p=128))
        ldp(DTB, A["dt_bias_2"][0].rearrange("a h -> (a h)").partition_broadcast(128))
        ldp(ALOG, A["a_log_2"][0].rearrange("a h -> (a h)").partition_broadcast(128))
        SINK = CST[:, C_BT + 480:C_BT + 496]
        ldp(SINK, A["attn_sink_2"][0].partition_broadcast(128))
        t_par = ldp(DSK, A["d_skip_2"][0].partition_broadcast(128))

        def conv_weights():
            yield from room(side)
            bank, bt = side.take()
            tr(bank[:, 0:128], CR1, 128, t_par, bt)
            t = tr(bank[:, 128:192], CR2, 64, sig=True)
            cw_tok.append(copy_act(CW[:, :], bank[:, 0:192], t, scale=0.5))
            side.give(bank, cw_tok)
            cw_tok.append(t)
            yield

        cw_tok = []

        gf = {}

        def gains_ffn():
            gains.give(g_post, xtok[3])
            gains.give(g_ffn, list(htok))
            gf["post"] = load_gain(A["post_ffn_norm"][0])
            gf["mix"] = load_gain(A["norm_mix_2"][0])

        a_free = [turned]
        task(conv_weights())

        def split_evac(dst_f, src, t):
            th, tl = split_from(src, aH[:, dst_f, :], aL[:, dst_f, :], t)
            return th, tl

        for c, (b0, nb) in enumerate(FF1):
            atok = Parts()
            for b in range(nb):
                gate = {}

                def evac_gu(f, bank, t, b=b):
                    if f < 2:
                        s, st = SG.take()
                        r = fn_act(s[:, :], bank[:, :], ACT.Sigmoid, t, st, turned)
                        r = tt(dve, s[:, :], s[:, :], bank[:, :], ALU.mult, r)
                        gate[f] = (s, r)
                        return r
                    s, r = gate[f - 2]
                    r1 = tt(dve, s[:, :], s[:, :], bank[:, :], ALU.mult, r, t)
                    th, tl = split_from(s[:, :], aH[:, 2 * b + f - 2, :], aL[:, 2 * b + f - 2, :], r1, a_free)
                    SG.give(s, [th, tl])
                    atok[2 * b + f - 2] = [th, tl]
                    return r1

                if c == 0 and b == 0:
                    fm_halves("gu", 4, 4, hH, hL, htok, evac_gu, then=gains_ffn)
                else:
                    hdone = fm_block("gu", 4, 4, hH, hL, htok, evac_gu)
                    drain()
            if c < len(FF1) - 1:
                last, yt = project(P2, "down", nb, aH, aL, atok, Y, [xtok[i] for i in range(4)], None, add=c > 0, tail=False)
                a_free = [last]
                yfree = [yt[i] for i in range(4)]
            else:
                g_pf, tg_pf = gf["post"]
                g_nm, tg_nm = gf["mix"]
                htok = Tiles()

                def tail2(t_, tok):
                    yield from post_add(t_, tok, Y[:, t_, :], g_pf[0], tg_pf)
                    yield from norm_steps(X[:, t_, :], g_nm[0], tg_nm, 128 * t_, hH, hL, hdone, htok[t_], xtok[t_])
                last, yt = project(P2, "down", nb, aH, aL, atok, Y, yfree, tail2, add=True)
        p2_done = [last, htok]
        P2.close()

        PL = ExitStack()
        LOW = sb("LOW", [128, 8, 512], c=PL)
        PA = ExitStack()
        XS0 = sb("XS0", [128, 4, 512], c=PA)
        BCF = sb("BCF", [128, 4, 512], c=PA)
        BF0, CF0 = BCF[:, 0:2, :], BCF[:, 2:4, :]
        BTK = sb("BTK", [128, 4, 512], c=PA)
        BT0 = BTK[:, 0:2, :].rearrange("p a (c n) -> p a c n", c=4)
        KF = BTK[:, 2:4, :]
        P3 = ExitStack()
        xs_buf = [XS0, X[:, 0:2, :].rearrange("p a (b c) -> p (a b) c", b=2)]
        bf_buf = [BF0, X[:, 2, :].rearrange("p (b c) -> p b c", b=2)]
        cf_buf = [CF0, X[:, 3, :].rearrange("p (b c) -> p b c", b=2)]
        bt_buf = [BT0]
        buf_free = [[p2_done], [p2_done]]
        ZS, YS = LOW[:, 0:4, :], LOW[:, 4:8, :]
        tmp = Ring([sb(f"tb{i}", [128, 512], c=P3) for i in range(NTB)])
        for i in range(NTB):
            tmp.free[i] = (tmp.free[i][0], p2_done)
        cb_sets = Ring([(sb(f"CBU{i}", [128, 4, 128], c=P3), sb(f"CBL{i}", [128, 4, 128], c=P3)) for i in range(2)])
        for i in range(2):
            cb_sets.free[i] = (cb_sets.free[i][0], p2_done)
        PREV = sb("PREV", [128, 2, 3, 256], c=P3)
        DT = sb("DT", [128, 4, 64], c=P3)
        CS = sb("CS", [128, 4, 64], c=P3)
        ECS = sb("ECS", [128, 4, 64], c=P3)
        WST = sb("WST", [128, 4, 64], c=P3)
        CDEC = sb("CDEC", [128, 4, 64], c=P3)

        l_xs = line("l_xs")

        def x_out():
            x_saved.append(l_xs.go(act, lambda e: e.dma_start(scr["x"], X[:, :, :].rearrange("p t d -> p (t d)")), [xtok[i] for i in range(4)]))
            buf_free[1] += x_saved
            gains.give(g_pf, xtok[3])
            gains.give(g_nm, list(htok))
            g, free = gains.take()
            bt1_gain.append(g)
            bt1_free.append(free)
            bt_buf.append(g[0][:, :].rearrange("p (a c n) -> p a c n", a=2, c=4))
            buf_free[1].append(bt1_free)

        x_saved, bt1_gain, bt1_free = [], [], []
        def dt_block():
            bank, bt = side.take()
            us = []
            for u in range(4):
                look_ahead()
                us.append(take_unit("dt"))
            for t_ in range(4):
                for u in range(4):
                    i, wh, wl, wt = us[u]
                    for kk in range(2):
                        tk = tm_mms(bank[:, 64 * t_:64 * t_ + 64], 4, 4, u, kk, (0, 64), wh, wl, hH, hL, t_, wt, of(htok, t_), bt, sig=(t_ == 3 and kk == 1))
                    if t_ == 3:
                        release(i, tk)
            return bank, tk

        dts = {}

        def steps_dt(dt_bank, dt_t):
            c4 = lambda ap: ap[:, 0:256].rearrange("p (c h) -> p c h", c=4)
            yield from room(tmp, 4)
            xe, a0 = tmp.take()
            ud, a2 = tmp.take()
            f1, b1 = tmp.take()
            f2, b2 = tmp.take()
            x_, e_, u_, d_ = c4(xe), c4(xe[:, 256:512]), c4(ud), c4(ud[:, 256:512])
            t = tt(dve, x_, c4(dt_bank), mid(DTB, 4), ALU.add, dt_t, a0, t_par)
            side.give(dt_bank, t)
            t2 = fn_act(e_, x_, ACT.Abs, t)
            t2 = fn_act(e_, e_, ACT.Exp, t2, scale=-1.0)
            t3 = ts(dve, u_, e_, 1.0, None, ALU.add, None, t2, a2)
            t4 = fn_act(DT[:, :, :], u_, ACT.Ln, t3, p2_done)
            tx = ts(dve, x_, x_, 0.0, None, ALU.max, None, t2)
            yield
            t5 = ts(dve, d_, u_, 1.0, None, ALU.subtract, None, t3)
            t5 = tt(dve, d_, e_, d_, ALU.subtract, t5)
            t6 = recip(u_, u_, t4, t5)
            t6 = tt(dve, d_, d_, u_, ALU.mult, t6)
            t6 = tt(dve, d_, d_, x_, ALU.add, t6, tx)
            tdt = tt(dve, DT[:, :, :], DT[:, :, :], d_, ALU.add, t6, t4)
            yield
            ta = fn_act(ALOG, ALOG, ACT.Exp, t_par)
            ta = ts(dve, ALOG, ALOG, -1.0, None, ALU.mult, None, ta)
            ta = tt(dve, x_, DT[:, :, :], mid(ALOG, 4), ALU.mult, ta, tdt)
            yield
            ft = []
            for d, (dst, dstt) in enumerate(((f1, b1), (f2, b2))):
                bank, bt = side.take()
                tri = CST[:, (C_TF, C_TB)[d]:(C_TF, C_TB)[d] + 128]
                for c in range(4):
                    t = mm(bank[0:32, 128 * c:128 * c + 128], x_[:, c, 32 * d:32 * d + 32], tri, True, True, ta, bt, sig=c == 3)
                t = copy_act(dst[0:32, :], bank[0:32, :], t, dstt)
                side.give(bank, t)
                ft.append(t)
                l_cs.go(act, lambda e, dst=dst, d=d: e.dma_start(scr["cs"][:, 512 * d:512 * d + 512], dst[0:32, :]), t)
            dts["cs"] = (l_cs.sem, l_cs.n)
            yield
            bank, bt = side.take()
            for d, dst in enumerate((f1, f2)):
                for c in range(4):
                    t = tr(bank[:, 64 * c + 32 * d:64 * c + 32 * d + 32], dst[0:32, 128 * c:128 * c + 128], 32, ft[d], bt, sig=c == 3)
            tcs = copy_act(CS[:, :, :], c4(bank), t)
            side.give(bank, tcs)
            yield
            bank, bt = side.take()
            for d in range(2):
                t = mm(bank[:, 128 * d:128 * d + 128].rearrange("p (c h) -> p c h", c=4), CST[:, (C_LL, C_FF)[d]:(C_LL, C_FF)[d] + 128],
                       CS[:, :, 32 * d:32 * d + 32], True, True, tcs, bt, sig=True)
            tot = bank[:, 0:256].rearrange("p (d c h) -> p d c h", d=2, c=4)
            td = []
            for d in range(2):
                v = lambda ap: ap[:, :, 32 * d:32 * d + 32]
                t1 = copy_act(v(CDEC), tot[:, d], t)
                td.append(tt(dve, v(WST), v(CDEC), v(CS), ALU.subtract, t1, tcs))
            side.give(bank, t1)
            td.append(fn_act(CDEC[:, :, :], CDEC[:, :, :], ACT.Exp, td))
            t1 = fn_act(WST[:, :, :], WST[:, :, :], ACT.Exp, td)
            t1 = tt(dve, WST[:, :, :], WST[:, :, :], DT[:, :, :], ALU.mult, t1, tdt)
            t2 = fn_act(ECS[:, :, :], CS[:, :, :], ACT.Exp, tcs)
            tn = fn_act(NCS[:, :, :], CS[:, :, 0:32], ACT.Copy, tcs, scale=-1.0)
            for b in (xe, ud):
                tmp.give(b, [ta, t6, tdt, t])
            tmp.give(f1, [t, dts["cs"]])
            tmp.give(f2, [t, dts["cs"]])
            dts["small"] = [t1, t2, tcs, td, tdt, tn]
            yield

        l_cs = line("l_cs")

        def conv(bank, t, ct):
            drain(lambda: len(tmp.free) >= CONV_ROOM)
            w = lambda k: CW[:, 32 * k + ct:32 * k + ct + 1]
            u, ut = tmp.take()
            t = fn_act(u[:, :], bank[:, :], ACT.Identity, t, ut, cw_tok, scale=w(2), bias=CW[:, 160 + ct:161 + ct])
            t = stt(u[:, 2:512], bank[:, 0:510], w(0), u[:, 2:512], ALU.mult, ALU.add, t)
            t = stt(u[:, 1:512], bank[:, 0:511], w(1), u[:, 1:512], ALU.mult, ALU.add, t)
            t = stt(u[:, 0:511], bank[:, 1:512], w(3), u[:, 0:511], ALU.mult, ALU.add, t)
            return u, stt(u[:, 0:510], bank[:, 2:512], w(4), u[:, 0:510], ALU.mult, ALU.add, t)

        def silu(u, t, dst, dst_free, toks, key, after=None):
            yield from room(tmp)
            h, ht = tmp.take()
            t = fn_act(h[:, :], u[:, :], ACT.Tanh, t, ht)
            yield
            o = h[:, :] if dst is None else dst
            t = stt(o, h[:, :], 1.0, u[:, :], ALU.add, ALU.mult, t, dst_free)
            tmp.give(u, t)
            if dst is not None:
                tmp.give(h, t)
                toks[key] = t
            yield
            if after:
                yield from after(h, t)

        bf_tok, cf_tok, bt_tok, xs_tok, zs_tok = {}, {}, {}, {}, {}
        zs_free = [p2_done]
        ys_free = [p2_done]

        def turn_b(j, f):
            yield from room(side)
            bank, bt = side.take()
            for c in range(4):
                t = tr(bank[:, 128 * c:128 * c + 128], bf_buf[j % 2][:, f, 128 * c:128 * c + 128], 128, bf_tok[j, f], bt, sig=c == 3)
            t = copy_act(bt_buf[j % 2][:, f, :, :].rearrange("p c n -> p (c n)"), bank[:, :], t, buf_free[j % 2])
            side.give(bank, t)
            bt_tok[j, f] = t
            yield

        def turn_xs(j, f, src, t0):
            yield from room(side)
            bank, bt = side.take()
            for c in range(4):
                t = tr(bank[:, 128 * c:128 * c + 128], src[:, 128 * c:128 * c + 128], 128, t0, bt, sig=c == 3)
            tmp.give(src, t)
            t = copy_act(xs_buf[j % 2][:, :, 128 * f:128 * f + 128], bank[:, :].rearrange("p (c n) -> p c n", c=4), t, buf_free[j % 2])
            side.give(bank, t)
            xs_tok[j, f] = t
            yield

        def evac_bc(j):
            def evac(f, bank, t):
                u, t = conv(bank, t, 16 + 2 * j + f if f < 2 else 24 + 2 * j + f - 2)
                if f < 2:
                    soon(silu(u, t, bf_buf[j % 2][:, f, :], buf_free[j % 2], bf_tok, (j, f), lambda h, t0: turn_b(j, f)), t)
                else:
                    soon(silu(u, t, cf_buf[j % 2][:, f - 2, :], buf_free[j % 2], cf_tok, (j, f - 2)), t)
                return t
            return evac

        def evac_xs(j):
            def evac(f, bank, t):
                u, t = conv(bank, t, 4 * j + f)
                soon(silu(u, t, None, None, None, None, lambda h, t0: turn_xs(j, f, h, t0)), t)
                return t
            return evac

        def evac_z(j):
            def evac(t_, bank, t):
                z = ZS[:, t_, :]
                if j:
                    drain(lambda: (j - 1, 1, 3) in yt)
                t = copy_act(z, bank[:, :], t, zs_free, scale=0.5)
                soon(silu_z(j, t_, z, t), t)
                return t
            return evac

        def silu_z(j, t_, z, t):
            yield from room(tmp)
            h, ht = tmp.take()
            t = fn_act(h[:, :], z, ACT.Tanh, t, ht)
            yield
            t = stt(z, h[:, :], 1.0, z, ALU.add, ALU.mult, t)
            tmp.give(h, t)
            zs_tok[j, t_] = t
            yield

        r64 = lambda ap: ap.rearrange("p (r d) -> p r d", d=64)
        l_cb = [line(f"l_cb{i}") for i in range(2)]
        cb_n = [0]
        prev_free = [p2_done]
        cb_free = [p2_done]
        l_ys = [line(f"l_ys{f}") for f in range(4)]
        gn = {}

        def cb_steps(j, gg, S_):
            while "small" not in dts or any((j, f) not in xs_tok for f in range(4)) or (j, gg) not in bt_tok or (j, gg) not in cf_tok:
                yield
            yield due(bf_tok[j, gg], cf_tok[j, gg])
            yield from room(side)
            yield from room(cb_sets)
            bank, bt = side.take()
            for c in range(4):
                t = mm(bank[:, 128 * c:128 * c + 128], bf_buf[j % 2][:, gg, 128 * c:128 * c + 128], cf_buf[j % 2][:, gg, 128 * c:128 * c + 128], True, True,
                       bf_tok[j, gg], cf_tok[j, gg], bt, sig=c == 3)
            b4 = bank[:, :].rearrange("p (c l) -> p c l", c=4)
            S_["cb"], free = cb_sets.take()
            S_["tu"] = tt(dve, S_["cb"][0][:, :, :], b4, mid(CST[:, C_TF:C_TF + 128], 4), ALU.mult, t, free)
            S_["tl"] = tt(dve, S_["cb"][1][:, :, :], b4, mid(CST[:, C_TB:C_TB + 128], 4), ALU.mult, t, free)
            side.give(bank, [S_["tu"], S_["tl"]])
            yield

        def state_steps(j, gg, d, S_, before):
            g = 2 * j + gg
            co = slice(256 * gg, 256 * gg + 256)
            while "small" not in dts or any((j, f) not in xs_tok for f in range(4)) or (j, gg) not in bt_tok or (before is not None and "off" not in before):
                yield
            xt = [xs_tok[j, f] for f in range(4)]
            for n in range(3):
                c = n if d == 0 else 3 - n
                hs = slice(32 * d + 4 * g, 32 * d + 4 * g + 4)
                yield from room(tmp, 5)
                xw, xwt = tmp.take()
                t = tt(pool, r64(xw[:, 0:256]), r64(xs_buf[j % 2][:, c, co]), bc(WST[:, c, hs], 64), ALU.mult, xwt, xt, dts["small"])
                if n:
                    pd, pdt = tmp.take()
                    t2 = tt(pool, r64(pd[:, 0:256]), r64(PREV[:, d, n - 1, :]), bc(CDEC[:, c, hs], 64), ALU.mult, S_["pv", d, n - 1], pdt)
                yield
                yield from room(side)
                bank, bt = side.take()
                t = mm(bank[:, 0:256], bt_buf[j % 2][:, gg, c, :], xw[:, 0:256], True, True, t, bt, bt_tok[j, gg], sig=True)
                tmp.give(xw, t)
                if n == 0:
                    t = copy_act(PREV[:, d, 0, :], bank[:, 0:256], t, prev_free)
                else:
                    t = tt(dve, PREV[:, d, n, :], bank[:, 0:256], pd[:, 0:256], ALU.add, t, t2, prev_free)
                    tmp.give(pd, t)
                side.give(bank, t)
                S_["pv", d, n] = t
                yield

        def head_steps(j, gg, r, S_):
            g = 2 * j + gg
            h = 4 * g + r
            yield from room(hn_ring)
            cb, cbt = hn_ring.take()
            ln = l_cb[h % 2]
            while "cs" not in dts:
                yield
            tc = ln.go(CSQ, lambda e: e.dma_start(cb[:, :], scr["cs"][h].partition_broadcast(128)), cbt, dts["cs"])
            yield
            while "tl" not in S_:
                yield
            yield due(tc, S_["tl"], S_["tu"])
            small_t = dts["small"]
            yield from room(tmp, 5)
            a, at = tmp.take()
            b, bt_ = tmp.take()
            for c in range(4):
                k = slice(128 * c, 128 * c + 128)
                t1 = fn_act(a[:, k], cb[:, k], ACT.Identity, tc, at, small_t, bias=NCS[:, c, h:h + 1])
            yield
            for c in range(4):
                k = slice(128 * c, 128 * c + 128)
                t = stt(b[:, k], cb[:, 512 + 128 * c:640 + 128 * c], CS[:, c, 32 + h:33 + h], a[:, k], ALU.subtract, ALU.min, tc, t1, bt_)
            hn_ring.give(cb, [t1, t])
            yield
            te = fn_act(b[:, :], b[:, :], ACT.Exp, t)
            cbu, cbl = S_["cb"]
            for c in range(4):
                k = slice(128 * c, 128 * c + 128)
                t3 = fn_act(a[:, k], cbl[:, c, :], ACT.Copy, S_["tl"], t, scale=DT[:, c, 32 + h:33 + h])
            yield
            for c in range(4):
                k = slice(128 * c, 128 * c + 128)
                t4 = stt(a[:, k], cbu[:, c, :], DT[:, c, h:h + 1], a[:, k], ALU.mult, ALU.add, S_["tu"], t3)
            t4 = tt(dve, b[:, :], a[:, :], b[:, :], ALU.mult, t4, te)
            tmp.give(a, t4)
            yield
            yield from room(side)
            bank, bt = side.take()
            x = xs_buf[j % 2][:, :, 256 * gg + 64 * r:256 * gg + 64 * r + 64]
            for c in range(4):
                t = mm(bank[:, 64 * c:64 * c + 64], b[:, 128 * c:128 * c + 128], x[:, c, :], True, True, t4, [xs_tok[j, f] for f in range(4)], bt, sig=c == 3)
            tmp.give(b, t)
            y = YS[:, :, 256 * gg + 64 * r:256 * gg + 64 * r + 64]
            t = stt(y, x, DSK[:, h:h + 1], r64(bank[:, 0:256]), ALU.mult, ALU.add, t, ys_free)
            side.give(bank, t)
            S_["y", r] = t
            if all(("y", i) in S_ for i in range(4)):
                cb_sets.give(S_["cb"], [t3, t4])
            yield

        def off_steps(j, gg, d, S_):
            g = 2 * j + gg
            co = slice(256 * gg, 256 * gg + 256)
            for n in range(3):
                c = n + 1 if d == 0 else 2 - n
                hs = slice(32 * d + 4 * g, 32 * d + 4 * g + 4)
                while ("pv", d, n) not in S_ or not all(("y", i) in S_ for i in range(4)):
                    yield
                yield due(S_["pv", d, n])
                yield from room(side)
                yield from room(tmp, 4)
                bank, bt = side.take()
                t = mm(bank[:, 0:256], cf_buf[j % 2][:, gg, 128 * c:128 * c + 128], PREV[:, d, n, :], True, True, S_["pv", d, n], bt, sig=True)
                S_["pe", d] = t
                o, ot = tmp.take()
                t2 = tt(dve, r64(o[:, 0:256]), r64(bank[:, 0:256]), bc(ECS[:, c, hs], 64), ALU.mult, t, ot)
                side.give(bank, t2)
                y = YS[:, c, co]
                t2 = tt(pool, y, y, o[:, 0:256], ALU.add, t2, S_.get(("off", c)), [S_["y", i] for i in range(4)])
                S_["off", c] = t2
                tmp.give(o, t2)
                yield
            S_["done", d] = True
            if ("done", 0) in S_ and ("done", 1) in S_:
                S_["off"] = True
                prev_free[:] = [S_["pe", 0], S_["pe", 1]]

        def fin_steps(j, gg, S_):
            g = 2 * j + gg
            co = slice(256 * gg, 256 * gg + 256)
            while any((j, f) not in zs_tok for f in range(4)) or "off" not in S_:
                yield
            yield due(*[S_["off", c] for c in range(4)], *[zs_tok[j, c] for c in range(4)])
            if gg == 0:
                gn[j] = load_gain(A["ssd_norm_2"][0][512 * j:512 * j + 512])
            rs = small(4)
            yield from room(tmp, 4)
            o, ot = tmp.take()
            for c in range(4):
                y = YS[:, c, co]
                t = tt(dve, y, y, ZS[:, c, co], ALU.mult, S_["off", c], zs_tok[j, c])
                t = fn_act(o[:, 0:256], y, ACT.Square, t, ot, accum_out=rs[:, c:c + 1])
                ot = t
            tmp.give(o, t)
            t = rstd(rs, rs, 256, RMS_EPS, t)
            yield
            yield
            for c in range(4):
                y = YS[:, c, co]
                yt[j, gg, c] = stt(y, y, rs[:, c:c + 1], gn[j][0][0][:, co], ALU.mult, ALU.mult, t, gn[j][1])
            yield
            if gg == 1:
                zs_free[:] = [yt[j, 1, 3]]
                gains.give(gn[j][0], [yt[j, 1, 3]])
                buf_free[j % 2][:] = [yt[j, 0, 3], yt[j, 1, 3], prev_free, S_["y", 3]]
                if j % 2:
                    buf_free[1].append(bt1_free)

        def out_steps(j, f):
            while (j, 1, 3) not in yt:
                yield
            yield due(yt[j, f // 2, 3])
            yield from room(side)
            yield from room(tmp, 4)
            bank, bt = side.take()
            for c in range(4):
                t = tr(bank[:, 128 * c:128 * c + 128], YS[:, c, 128 * f:128 * f + 128], 128, yt[j, f // 2, c], bt, sig=c == 3)
            o, ot = tmp.take()
            t2 = copy_act(o[:, :], bank[:, :], t, ot)
            side.give(bank, t2)
            td = l_ys[f].go(CSQ, lambda e: e.dma_start(scr["ys"][128 * (4 * j + f):128 * (4 * j + f) + 128, :], o[:, :]), t2)
            tmp.give(o, td)
            yr.setdefault(j, []).append(t)
            if len(yr[j]) == 4:
                ys_free[:] = [yr[j]]
                if j == 3:
                    ys_done.extend([(ln.sem, ln.n) for ln in l_ys])
            yield

        yt, yr = {}, {}

        def ssd_tasks(j):
            if j:
                task(wait_for(lambda: len(yr.get(j - 1, [])) == 4))
            before = groups[-1] if groups else None
            for gg in range(2):
                S_ = {}
                groups.append(S_)
                task(cb_steps(j, gg, S_), state_steps(j, gg, 0, S_, before), state_steps(j, gg, 1, S_, before))
                task(*[head_steps(j, gg, r, S_) for r in range(4)])
                task(off_steps(j, gg, 0, S_), off_steps(j, gg, 1, S_), fin_steps(j, gg, S_))
                before = S_
            task(*[out_steps(j, f) for f in range(4)])

        def wait_for(cond):
            while not cond():
                yield

        groups = []
        kf_tok, v2_tok, q2_tok, sg_tok = {}, {}, {}, {}
        V2 = BTK[:, 0:2, :].rearrange("p a (b d) -> p (a b) d", b=2)
        Q2 = [XS0[:, i, :] for i in range(4)] + [BF0[:, i, :] for i in range(2)] + [CF0[:, i, :] for i in range(2)]
        saved = {"q": [], "g": []}

        def save(what, k, o, t):
            ln = line(f"l_{what}{k}")
            td = ln.go(pool, lambda e: e.dma_start(scr[what][:, 512 * k:512 * k + 512], o[:, :]), t)
            tmp.give(o, td)
            saved[what].append(td)

        def q_block(j):
            def evac(f, bank, t):
                drain(lambda: len(tmp.free) >= 2)
                o, ot = tmp.take()
                t = copy_act(o[:, :], bank[:, :], t, ot, scale=0.125)
                save("q", 4 * j + f, o, t)
                return t
            fm_block("q2", 4, 4, hH, hL, htok, evac, rate=RA[3])

        def g_block(j):
            def evac(f, bank, t):
                drain(lambda: len(tmp.free) >= 2)
                o, ot = tmp.take()
                t = fn_act(o[:, :], bank[:, :], ACT.Tanh, t, ot, scale=0.5)
                save("g", 4 * j + f, o, ts(pool, o[:, :], o[:, :], 0.5, 0.5, ALU.mult, ALU.add, t))
                return t
            fm_block("gate", 4, 4, hH, hL, htok, evac, rate=RA[3])

        def kv_block(_):
            free0 = list(buf_free[0])
            banks = [main.take() for _ in range(4)]
            us = []
            for u in range(4):
                look_ahead()
                i, wh, wl, wt = take_unit("kv2")
                for f in range(2):
                    for kk in range(2):
                        k = 2 * u + kk
                        w_h, w_l = wh[:, kk, 128 * f:128 * f + 128], wl[:, kk, 128 * f:128 * f + 128]
                        mm(banks[f][0][:, :], w_h, hH[:, k, :], k == 0, False, wt, htok, banks[f][1])
                        mm(banks[f][0][:, :], w_h, hL[:, k, :], False, False)
                        t = mm(banks[f][0][:, :], w_l, hH[:, k, :], False, k == 7, sig=k == 7)
                    if u == 3:
                        kf_tok[f] = copy_act(KF[:, f, :], banks[f][0][:, :], t, p2_done)
                        main.give(banks[f][0], kf_tok[f])
                    pump(RA[3])
                us.append((i, wh, wl, wt))
            for t_ in range(4):
                b = banks[2 + t_ // 2]
                for u in range(4):
                    i, wh, wl, wt = us[u]
                    for kk in range(2):
                        t = tm_mms(b[0][:, 256 * (t_ % 2):256 * (t_ % 2) + 256], 4, 4, u, kk, (256, 512), wh, wl, hH, hL, t_, wt, b[1], sig=(t_ == 3 and kk == 1))
                    if t_ == 3:
                        release(i, t)
                        look_ahead()
                    if u % 2:
                        pump(RA[3])
                if t_ % 2:
                    r = copy_act(V2[:, t_ - 1:t_ + 1, :].rearrange("p t d -> p (t d)"), b[0][:, :], t, free0)
                    v2_tok[t_ - 1] = v2_tok[t_] = r
                    main.give(b[0], r)

        extra = {"q": q_block, "g": g_block, "k": kv_block}
        for j in range(4):
            if j == 0:
                fm_halves("bc", 4, 4, hH, hL, htok, evac_bc(j), then=x_out)
                task(steps_dt(*dt_block()))
            else:
                fm_tiles("bc", 4, 4, hH, hL, htok, evac_bc(j), rate=RA[0])
            fm_tiles("xs", 4, 4, hH, hL, htok, evac_xs(j), rate=RA[1])
            ssd_tasks(j)
            for kind, n in EXTRA[j]:
                extra[kind](n)
            tm_block("z", 4, hH, hL, htok, evac_z(j), rate=RA[2])
        l_back = line("l_back")
        l_back.go(pool, lambda e: e.dma_start(XS0[:, :, :].rearrange("p a n -> p (a n)"), scr["q"][:, 0:2048]), list(buf_free[0]), saved["q"])
        tq = l_back.go(pool, lambda e: e.dma_start(BCF[:, :, :].rearrange("p a n -> p (a n)"), scr["q"][:, 2048:4096]))
        for k in range(8):
            q2_tok[k] = tq
        for kind, n in EXTRA[4]:
            extra[kind](n)
        drain()
        P3.close()
        gains.give(bt1_gain[0], buf_free[1])

        ssd_done = [ys_free[0], buf_free[1], ys_done, zs_free[0]]
        SIGA = X[:, :, :].rearrange("p a (b c) -> p (a b) c", b=2)
        SIGB = LOW
        P5 = ExitStack()
        ATT = sb("ATT", [128, 4, D], c=P5)
        sc_ring = Ring([sb(f"SC2{i}", [128, 384], c=P5) for i in range(4)])
        bias_ring = Ring([sb(f"BI2{i}", [128, 384], c=P5) for i in range(2)])
        pt_ring = Ring([sb(f"PTb{i}", [128, 384], c=P5) for i in range(3)])
        ssd_done.append(saved["q"] + saved["g"])
        for rg in (sc_ring, bias_ring, pt_ring):
            for i in range(len(rg.free)):
                rg.free[i] = (rg.free[i][0], ssd_done)
        l_ga = line("l_ga")
        tg = l_ga.go(pool, lambda e: e.dma_start(SIGA.rearrange("p k n -> p (k n)"), scr["g"]), ssd_done)
        for k in range(8):
            sg_tok[k] = tg

        def evac_gate(j):
            def evac(f, bank, t):
                dst = SIGB[:, 4 * (j % 2) + f, :]
                t = fn_act(dst, bank[:, :], ACT.Tanh, t, ssd_done, scale=0.5)
                sg_tok[4 * j + f] = ts(pool, dst, dst, 0.5, 0.5, ALU.mult, ALU.add, t)
                return t
            return evac

        at_tok = []
        o2_tok = {}
        bias = {}

        def make_bias(h):
            yield from room(bias_ring)
            b, bt = bias_ring.take()
            t = ts(pool, b[:, :], CST[:, C_NB:C_NB + 384], float(2.0 ** (-8.0 * (h + 1) / 16)), None, ALU.mult, None, bt)
            bias[h] = [b, t, 0]
            yield

        def attend2(h, qt):
            kv = h // 4
            f, p0 = 4 * (kv // 2) + h % 4, 64 * (kv % 2)
            lo_k, hi_k = max(0, qt - 1), min(3, qt + 1)
            nk = hi_k - lo_k + 1
            n = 128 * nk
            bo = 128 * (lo_k - (qt - 1))
            while h not in bias:
                yield
            yield from room(side)
            yield from room(sc_ring)
            s, st = sc_ring.take()
            m = small(4)
            mx, nm, den, sk = m[:, 0:1], m[:, 1:2], m[:, 2:3], m[:, 3:4]
            bank, bt = side.take()
            t = mm(bank[:, 0:n], Q2[f][p0:p0 + 64, 128 * qt:128 * qt + 128], KF[p0:p0 + 64, kv // 2, 128 * lo_k:128 * lo_k + n], True, True,
                   q2_tok[f], kf_tok[kv // 2], bt, sig=True)
            t = ttr(s[:, 0:n], bank[:, 0:n], bias[h][0][:, bo:bo + n], SINK[:, h:h + 1], ALU.add, ALU.max, mx, t, st, bias[h][1], t_par)
            side.give(bank, t)
            bias[h][2] += 1
            if bias[h][2] == 4:
                bias_ring.give(bias[h][0], t)
            t = ts(dve, nm, mx, -1.0, None, ALU.mult, None, t)
            yield
            te = fn_act(s[:, 0:n], s[:, 0:n], ACT.Exp, t, bias=nm, accum_out=den)
            t5 = fn_act(sk, SINK[:, h:h + 1], ACT.Exp, t, bias=nm)
            yield
            t5 = tt(dve, den, den, sk, ALU.add, t5, te)
            t5 = recip(den, den, t5)
            yield from room(side)
            yield from room(pt_ring)
            bank, bt = side.take()
            for k in range(nk):
                t = tr(bank[:, 128 * k:128 * k + 128], s[:, 128 * k:128 * k + 128], 128, te, bt, sig=k == nk - 1)
            sc_ring.give(s, t)
            pt, ptt = pt_ring.take()
            t2 = (copy_act if qt % 2 else copy_dve)(pt[:, 0:n], bank[:, 0:n], t, ptt)
            side.give(bank, t2)
            yield
            yield from room(side)
            bank, bt = side.take()
            for k in range(nk):
                t3 = mm(bank[:, 0:64], pt[:, 128 * k:128 * k + 128], V2[:, lo_k + k, 64 * kv:64 * kv + 64], k == 0, k == nk - 1,
                        t2, v2_tok[lo_k + k], bt, sig=k == nk - 1)
            pt_ring.give(pt, t3)
            t = ts(dve, ATT[:, qt, 64 * h:64 * h + 64], bank[:, 0:64], den, None, ALU.mult, None, t3, t5, ssd_done)
            side.give(bank, t)
            o2_tok[h, qt] = t
            yield

        for h in range(16):
            task(make_bias(h), *[attend2(h, qt) for qt in range(4)])
        for j in range(2, 4):
            gates_mm = fm_block("gate", 4, 4, hH, hL, htok, evac_gate(j), rate=RA[4])

        mg_tok = {}
        for j in range(2):
            banks = [main.take() for _ in range(4)]
            for u in range(8):
                look_ahead()
                i, wh, wl, wt = take_unit("wssd")
                look_ahead()
                i2, yh, yl, ytk = take_unit("ys")
                for f in range(4):
                    for kk in range(2):
                        first, last = u == 0 and kk == 0, u == 7 and kk == 1
                        w_h, w_l = wh[:, kk, 128 * f:128 * f + 128], wl[:, kk, 128 * f:128 * f + 128]
                        mm(banks[f][0][:, :], w_h, yh[:, kk, :], first, False, wt, ytk, banks[f][1])
                        mm(banks[f][0][:, :], w_h, yl[:, kk, :], False, False)
                        t = mm(banks[f][0][:, :], w_l, yh[:, kk, :], False, last, sig=last or (f == 3 and kk == 1))
                    if last:
                        dst = SIGB[:, 4 * j + f, :]
                        mg_tok[4 * j + f] = tt(dve, dst, dst, banks[f][0][:, :], ALU.mult, t, sg_tok[8 + 4 * j + f])
                        main.give(banks[f][0], mg_tok[4 * j + f])
                    if f == 3:
                        release(i, t)
                        release(i2, t)
                    pump(RA[4])
        drain()
        for qt in range(4):
            d, _ = turn(ATT[:, qt, :], 8, hH, hL, 128 * qt, gates_mm, [o2_tok[h, qt] for h in range(16)])
            at_tok += d
        P5.close()
        PA.close()
        PM = ExitStack()
        MEMX = sb("MEMX", [128, 2, D], c=PM)
        mH = sb("mH", [128, 8, 256], F32R, c=PM)
        mL = sb("mL", [128, 8, 256], F32R, c=PM)
        P6 = ExitStack()
        l_mem = [line(f"l_mem{t}") for t in range(2)]
        att_done = list(o2_tok.values())
        g_mem, tg_mem = load_gain(A["norm_mem_2"][0])
        mtok = [[], []]

        def mem_norm(t):
            x = MEMX[:, t, :]
            tx = l_mem[t].go(pool, lambda e: e.dma_start(x, A["mem_2"][0, 128 * t:128 * t + 128, :]), att_done)
            yield
            yield from norm_steps(x, g_mem[0], tg_mem, 128 * t, mH, mL, att_done, mtok[t], tx)

        task(mem_norm(0), mem_norm(1))
        gH = sb("gH", [128, 8, S], F32R, c=P6)
        gL = sb("gL", [128, 8, S], F32R, c=P6)
        merged = Parts()

        def evac_attn(j):
            def evac(f, bank, t):
                k = 4 * j + f
                a = SIGA[:, k, :]
                t1 = tt(dve, a, a, bank[:, :], ALU.mult, t, sg_tok[k])
                t2 = tt(pool, a, a, SIGB[:, k, :], ALU.add, t1, mg_tok[k])
                th, tl = split_from(a, gH[:, k, :], gL[:, k, :], t2, at_tok)
                merged[k] = [th, tl]
                return t1
            return evac

        for j in range(2):
            at_mm = fm_block("wattn", 4, 4, hH, hL, at_tok, evac_attn(j), rate=1)
        drain()
        l_xr = line("l_xr")
        x_back = l_xr.go(act, lambda e: e.dma_start(X[:, :, :].rearrange("p t d -> p (t d)"), scr["x"]), list(merged), x_saved)
        g_nc, tg_nc = load_gain(A["norm_cross_2"][0])
        htok = Tiles()

        def tail3(t_, tok):
            xtok[t_] = tok
            yield from norm_steps(X[:, t_, :], g_nc[0], tg_nc, 128 * t_, hH, hL, at_mm, htok[t_], tok)

        wout_mm, _ = project(P6, "wout2", 4, gH, gL, merged, X, x_back, tail3, add=True)
        p6_done = [wout_mm, list(merged)]
        P6.close()
        gains.give(g_mem, mtok)

        P7 = ExitStack()
        QX, VM = LOW[:, 0:4, :], LOW[:, 6:8, :]
        KM = LOW[:, 4:6, :].rearrange("p a (b k) -> p (a b) k", b=2)
        oH = sb("oH", [128, 4, S], F32R, c=P7)
        oL = sb("oL", [128, 4, S], F32R, c=P7)
        OX = [sb(f"OX{i}", [128, 512], c=P7) for i in range(2)]
        ox_ring = Ring(OX)
        px_ring = Ring([sb(f"PX{i}", [128, 4, 256], c=P7) for i in range(2)])
        pxt_ring = Ring([sb(f"PXT{i}", [128, 512], c=P7) for i in range(2)])
        for rg in (ox_ring, px_ring, pxt_ring):
            for i in range(len(rg.free)):
                rg.free[i] = (rg.free[i][0], p6_done)
        km_tok, vm_tok = [], []

        def evac_km(f, bank, t):
            km_tok.append(copy_act(KM[:, f, :], bank[:, 0:256], t, p6_done))
            return km_tok[-1]

        def evac_vm(t_, bank, t):
            vm_tok.append(copy_act(VM[:, t_, :], bank[:, :], t, p6_done))
            return vm_tok[-1]

        fm_block("xk", 4, 4, mH, mL, mtok, evac_km, N=256, with_tails=True)
        end_tails()
        gains.give(g_nc, list(htok))
        qx_tok = {}

        def evac_qx(f, bank, t):
            qx_tok[f] = copy_act(QX[:, f, :], bank[:, :], t, p6_done, scale=float(128 ** -0.5))
            return qx_tok[f]

        qx_mm = fm_block("xq", 4, 4, hH, hL, htok, evac_qx)
        tm_block("xv", 4, mH, mL, mtok, evac_vm, ntok=2)
        g_nf, tg_nf = load_gain(A["norm_ffn_2"][0])
        us = []
        for u in range(4):
            look_ahead()
            us.append(take_unit("xo"))
        ftok = Tiles()
        crossed = []
        p7_x = []

        def cross(qt):
            yield from room(side, 3)
            yield from room(px_ring)
            pair = []
            m = small(12)
            mx, nm, den = m[:, 0:4], m[:, 4:8], m[:, 8:12]
            for b in range(2):
                bank, bt = side.take()
                for r in range(2):
                    h = 2 * b + r
                    t = mm(bank[:, 256 * r:256 * r + 256], QX[:, h, 128 * qt:128 * qt + 128], KM[:, h, :], True, True, qx_tok[h], km_tok, bt, sig=r == 1)
                t1 = dve.do(lambda e, bank=bank, b=b: e.tensor_reduce(mx[:, 2 * b:2 * b + 2], bank[:, :].rearrange("p (h k) -> p h k", h=2), AX.X, ALU.max), t)
                pair.append((bank, t1))
            t = ts(dve, nm, mx, -1.0, None, ALU.mult, None, t1)
            p, pt_ = px_ring.take()
            te = []
            for h in range(4):
                te.append(fn_act(p[:, h, :], pair[h // 2][0][:, 256 * (h % 2):256 * (h % 2) + 256], ACT.Exp, t, pt_, bias=nm[:, h:h + 1], accum_out=den[:, h:h + 1]))
            side.give(pair[0][0], te[1])
            side.give(pair[1][0], te[3])
            rt = recip(den, den, te)
            yield
            yield from room(side, 2)
            yield from room(ox_ring)
            ob, obt = side.take()
            for b in range(2):
                bank, bt = side.take()
                for r in range(2):
                    for k in range(2):
                        h = 2 * b + r
                        c = 256 * r + 128 * k
                        t = tr(bank[:, c:c + 128], p[:, h, 128 * k:128 * k + 128], 128, te[h], bt, sig=r == 1 and k == 1)
                q, qt_ = pxt_ring.take()
                t2 = (copy_act, copy_dve)[b](q[:, :], bank[:, :], t, qt_)
                side.give(bank, t2)
                for r in range(2):
                    h = 2 * b + r
                    for k in range(2):
                        c = 256 * r + 128 * k
                        t3 = mm(ob[:, 128 * h:128 * h + 128], q[:, c:c + 128], VM[:, k, 128 * h:128 * h + 128], k == 0, k == 1, t2, obt, vm_tok, sig=r == 1 and k == 1)
                pxt_ring.give(q, t3)
            px_ring.give(p, t)
            o, ot = ox_ring.take()
            t = tt(dve, o[:, :].rearrange("p (h d) -> p h d", h=4), ob[:, :].rearrange("p (h d) -> p h d", h=4), bc(den, 128), ALU.mult, t3, rt, ot)
            side.give(ob, t)
            yield
            yield from room(side)
            d, last = turn(o, 4, oH, oL, 128 * qt, p6_done, t)
            ox_ring.give(o, last)
            yield
            yield from room(side)
            ad = []
            for h in range(2):
                bank, bt = side.take()
                for u in range(2):
                    i, wh, wl, wt = us[2 * h + u]
                    for kk in range(2):
                        t = tm_mms(bank[:, :], 4, 2, u, kk, (0, 512), wh, wl, oH, oL, qt, wt, d, bt, sig=qt == 3)
                    if qt == 3:
                        release(i, t)
                x = X[:, qt, 512 * h:512 * h + 512]
                ad.append(tt(dve, x, bank[:, :], x, ALU.add, t, xtok[qt]))
                side.give(bank, ad[-1])
            xtok[qt] = ad
            crossed.append(qt)
            yield
            yield from norm_steps(X[:, qt, :], g_nf[0], tg_nf, 128 * qt, hH, hL, qx_mm, ftok[qt], ad)

        for qt in range(4):
            tails.append([qt, cross(qt), 0.0])
        while len(crossed) < 4:
            step_tails(force=True)
        p7_done = [ftok, p7_x]
        P7.close()
        PM.close()
        PL.close()

        P8 = ExitStack()
        fH = sb("fH", [128, 8, S], F32R, c=P8)
        fL = sb("fL", [128, 8, S], F32R, c=P8)
        rl = Ring([sb(f"rl{i}", [128, 512], c=P8) for i in range(3)])
        for i in range(3):
            rl.free[i] = (rl.free[i][0], p7_done)
        gfi = []

        def crossed_all():
            gains.give(g_nf, list(ftok))
            gfi.append(load_gain(A["norm_final_2"]))
            p7_x.extend(xtok[i] for i in range(4))

        f_free = [p7_done]
        xfree = [xtok[i] for i in range(4)]
        l_out = line("l_out")

        def tail4(t_, tok):
            g_fi, tg_fi = gfi[0]
            ss = small(1)
            x = X[:, t_, :]
            t = square_sum(ss, x, tok)
            t = rstd(ss, ss, D, RMS_EPS, t)
            yield
            t = stt(x, x, ss, g_fi[0][:, :], ALU.mult, ALU.mult, t, tg_fi)
            l_out.go(sp, lambda e, t_=t_: e.dma_start(out[0, 128 * t_:128 * t_ + 128, :], X[:, t_, :]), t)

        for fc in range(NFF2):
            atok = Parts()
            for b in range(2):
                def evac_up(f, bank, t, b=b):
                    s, st = rl.take()
                    tr1 = fn_act(s[:, :], bank[:, :], ACT.Relu, t, st)
                    r = tt(dve, s[:, :], s[:, :], bank[:, :], ALU.mult, tr1)
                    th, tl = split_from(s[:, :], fH[:, 4 * b + f, :], fL[:, 4 * b + f, :], r, f_free)
                    rl.give(s, [th, tl])
                    atok[4 * b + f] = [th, tl]
                    return r
                if fc == 0 and b == 0:
                    fm_halves("up2", 4, 4, hH, hL, ftok, evac_up, then=crossed_all)
                else:
                    fm_block("up2", 4, 4, hH, hL, ftok, evac_up)
            if fc < NFF2 - 1:
                last, yt = project(P8, "down2", 4, fH, fL, atok, X, xfree, None, add=True, tail=False)
                f_free = [last]
                xfree = [yt[i] for i in range(4)]
            else:
                last, yt = project(P8, "down2", 4, fH, fL, atok, X, xfree, tail4, add=True)
        end_tails()
        P8.close()
        sp.wait((l_out.sem, l_out.n), *ys_done, (l_cs.sem, l_cs.n), (l_xs.sem, l_xs.n))
        assert st_["use"] == len(units), (st_, len(units))

        block = ctx.enter_context(nc.Block())

        @block.sync
        def _(e):
            sp.emit(e)

        @block.gpsimd
        def _(e):
            pool.emit(e)

        @block.scalar
        def _(e):
            act.emit(e)

        @block.vector
        def _(e):
            dve.emit(e)

        @block.tensor
        def _(e):
            pe.emit(e)


_INS = ['x', 'positions', 'pre_mix_norm', 'w_in', 'sgu_ln_gain', 'sgu_ln_bias', 'sgu_w_spatial', 'sgu_b_spatial', 'attn_out_norm', 'sgu_out_norm', 'w_out', 'post_mix_norm', 'pre_ffn_norm', 'w_gate', 'w_up', 'w_down', 'post_ffn_norm', 'mem_2', 'norm_mix_2', 'w_in_2', 'attn_sink_2', 'conv_w_2', 'conv_b_2', 'dt_bias_2', 'a_log_2', 'd_skip_2', 'ssd_norm_2', 'w_attn_branch_2', 'w_ssd_branch_2', 'w_out_2', 'norm_cross_2', 'norm_mem_2', 'w_xq_2', 'w_xkv_2', 'w_xo_2', 'norm_ffn_2', 'w_up_2', 'w_down_2', 'norm_final_2']


def kernel(**inputs):
    import numpy as _np
    import concourse.bacc as _bacc
    from concourse import mybir as _mybir
    from concourse.bass_utils import run_bass_kernel_spmd as _run

    nc = _bacc.Bacc("TRN2", target_bir_lowering=False, num_devices=1)
    arrays, args = {}, {}
    for name in _INS + ["consts"]:
        a = constants() if name == "consts" else _np.ascontiguousarray(inputs[name])
        arrays[f"in_{name}_dram"] = a
        args[name] = nc.dram_tensor(f"in_{name}_dram", a.shape, _mybir.dt.from_np(a.dtype), kind="ExternalInput").ap()
    out = nc.dram_tensor("out_0_dram", (1, S, D), F32, kind="ExternalOutput").ap()
    scr = {n: nc.dram_tensor(f"scr_{n}_dram", shape, F32, kind="Internal").ap() for n, shape in SCRATCH.items()}
    build(nc, args, out, scr)
    r = _run(nc, [arrays], core_ids=[0])
    return r.results[0]["out_0_dram"]
```
